# Optimizing a Trainium2 kernel written in Bass

```python
import math
import jax, jax.numpy as jnp
from jax import lax
import numpy as np

D_MODEL = 2048
BATCH = 1
SEQ = 512
DEPTH = 2
DEC_BATCH = 8
DEC_SEQ = 4
PAST_LEN = 2048
PAGE_SIZE = 128

N_A_LAYERS = DEPTH // 2
N_B_LAYERS = DEPTH - N_A_LAYERS
CONV_WIDTH = 3
CONV_DIM = D_MODEL
N_HEADS = 8
HEAD_DIM = D_MODEL // (2 * N_HEADS)
V_DIM = 2 * HEAD_DIM
QK_DIM = N_HEADS * 2 * HEAD_DIM
ATTN_DIM = N_HEADS * V_DIM
ROT_DIM = HEAD_DIM // 4
ROPE_THETA = 500000.0
Q_BLOCK = 128
EPS = 1e-6
LAMBDA_INITS = tuple(0.8 - 0.6 * math.exp(-0.3 * (N_A_LAYERS + j)) for j in range(N_B_LAYERS))

kernel_name = 'yoco_shortconv_diffattn_step'

def rms_norm(x, g):
    xf = x.astype(jnp.float32)
    y = xf * lax.rsqrt(jnp.mean(xf * xf, axis=-1, keepdims=True) + EPS)
    return (y * g.astype(jnp.float32)).astype(x.dtype)

def rope(x, pos):
    inv = ROPE_THETA ** (-jnp.arange(0, ROT_DIM, 2, dtype=jnp.float32) / ROT_DIM)
    ang = pos.astype(jnp.float32)[:, None] * inv[None, :]
    cos = jnp.cos(ang)[:, None, None, :]
    sin = jnp.sin(ang)[:, None, None, :]
    xr = x[..., :ROT_DIM].astype(jnp.float32)
    x1, x2 = xr[..., :ROT_DIM // 2], xr[..., ROT_DIM // 2:]
    rot = jnp.concatenate([x1 * cos - x2 * sin, x2 * cos + x1 * sin], axis=-1).astype(x.dtype)
    return jnp.concatenate([rot, x[..., ROT_DIM:]], axis=-1)

def short_conv_layer(x, prev_u, norm_g, w_in, conv_w, w_out):
    h = rms_norm(x, norm_g) @ w_in
    b_gate, c_gate, hx, z = jnp.split(h, 4, axis=-1)
    u = c_gate * hx
    upad = jnp.concatenate([prev_u.astype(u.dtype), u], axis=1)
    conv = lax.conv_general_dilated(upad, conv_w[:, None, :].astype(u.dtype), window_strides=(1,),
                                    padding='VALID', dimension_numbers=('NWC', 'WIO', 'NWC'),
                                    feature_group_count=CONV_DIM)
    y = (b_gate * conv * jax.nn.silu(z)) @ w_out
    return x + y, upad[:, -(CONV_WIDTH - 1):]

def shared_kv(x, pos, norm_kv, w_kv, k_norm):
    B, T, _ = x.shape
    kv = rms_norm(x, norm_kv) @ w_kv
    k, v = jnp.split(kv, [QK_DIM], axis=-1)
    k = rope(rms_norm(k.reshape(B, T, N_HEADS, 2, HEAD_DIM), k_norm), pos)
    return k, v.reshape(B, T, N_HEADS, V_DIM)

def diff_query(x, pos, norm_g, w_in, q_norm):
    B, T, _ = x.shape
    h = rms_norm(x, norm_g) @ w_in
    q, z = jnp.split(h, [QK_DIM], axis=-1)
    q = rope(rms_norm(q.reshape(B, T, N_HEADS, 2, HEAD_DIM), q_norm), pos)
    return q, z

def diff_lambda(lam, lam_init):
    lf = lam.astype(jnp.float32)
    return jnp.exp(jnp.sum(lf[0] * lf[1])) - jnp.exp(jnp.sum(lf[2] * lf[3])) + lam_init

def diff_weights(s, mask, lam_full):
    p = jax.nn.softmax(jnp.where(mask, s, -jnp.inf), axis=-1)
    return p[:, :, 0] - lam_full * p[:, :, 1]

def diff_attn_prompt(q, k, v, lam_full):
    B, S = q.shape[:2]
    nb = S // Q_BLOCK
    qb = q.reshape(B, nb, Q_BLOCK, N_HEADS, 2, HEAD_DIM).swapaxes(0, 1)
    kpos = jnp.arange(S)
    scale = HEAD_DIM ** -0.5

    def block(args):
        q_blk, i = args
        qpos = i * Q_BLOCK + jnp.arange(Q_BLOCK)
        s = jnp.einsum('bqhcd,bkhcd->bhcqk', q_blk, k, preferred_element_type=jnp.float32) * scale
        w = diff_weights(s, kpos[None, :] <= qpos[:, None], lam_full)
        return jnp.einsum('bhqk,bkhe->bqhe', w.astype(v.dtype), v)

    o = lax.map(block, (qb, jnp.arange(nb)))
    return o.swapaxes(0, 1).reshape(B, S, N_HEADS, V_DIM)

def diff_attn_sample(q, k_new, v_new, k_past, v_past, lam_full):
    T = q.shape[1]
    P = k_past.shape[1]
    scale = HEAD_DIM ** -0.5
    s_past = jnp.einsum('bqhcd,bkhcd->bhcqk', q, k_past, preferred_element_type=jnp.float32)
    s_new = jnp.einsum('bqhcd,bkhcd->bhcqk', q, k_new, preferred_element_type=jnp.float32)
    s = jnp.concatenate([s_past, s_new], axis=-1) * scale
    kpos = jnp.arange(P + T)
    qpos = P + jnp.arange(T)
    w = diff_weights(s, kpos[None, :] <= qpos[:, None], lam_full).astype(v_new.dtype)
    return (jnp.einsum('bhqk,bkhe->bqhe', w[..., :P], v_past)
            + jnp.einsum('bhqk,bkhe->bqhe', w[..., P:], v_new))

def diff_output(o, z, subln_g, lam_init, w_out):
    B, T = o.shape[:2]
    o = rms_norm(o, subln_g) * (1.0 - lam_init)
    return (o.reshape(B, T, ATTN_DIM) * jax.nn.silu(z)) @ w_out

def setup_inputs(seed: int = 0) -> dict:
    key = jax.random.key(seed)
    ks = jax.random.split(key, 20)
    f32 = jnp.float32
    n_pages = PAST_LEN // PAGE_SIZE
    n_used = DEC_BATCH * n_pages
    n_phys = n_used + max(1, n_used // 4)

    def nrm(k, shape, scale):
        return jax.random.normal(k, shape, f32) * scale

    def gain(k, shape):
        return 1.0 + 0.02 * jax.random.normal(k, shape, f32)

    page_table = jax.random.permutation(ks[0], n_phys)[:n_used].reshape(DEC_BATCH, n_pages).astype(jnp.int32)
    return {
        'x_prompt': nrm(ks[1], (BATCH, SEQ, D_MODEL), 1.0),
        'x_sample': nrm(ks[2], (DEC_BATCH, DEC_SEQ, D_MODEL), 1.0),
        'state_conv': nrm(ks[3], (N_A_LAYERS, DEC_BATCH, CONV_WIDTH - 1, CONV_DIM), 1.0),
        'cache_k': nrm(ks[4], (n_phys, PAGE_SIZE, N_HEADS, 2, HEAD_DIM), 1.0),
        'cache_v': nrm(ks[5], (n_phys, PAGE_SIZE, N_HEADS, V_DIM), 1.0),
        'page_table': page_table,
        'norm_a': gain(ks[6], (N_A_LAYERS, D_MODEL)),
        'w_in_a': nrm(ks[7], (N_A_LAYERS, D_MODEL, 4 * CONV_DIM), D_MODEL ** -0.5),
        'conv_w': nrm(ks[8], (N_A_LAYERS, CONV_WIDTH, CONV_DIM), CONV_WIDTH ** -0.5),
        'w_out_a': nrm(ks[9], (N_A_LAYERS, CONV_DIM, D_MODEL), CONV_DIM ** -0.5),
        'norm_kv': gain(ks[10], (D_MODEL,)),
        'w_kv': nrm(ks[11], (D_MODEL, QK_DIM + ATTN_DIM), D_MODEL ** -0.5),
        'k_norm': gain(ks[12], (HEAD_DIM,)),
        'norm_b': gain(ks[13], (N_B_LAYERS, D_MODEL)),
        'w_in_b': nrm(ks[14], (N_B_LAYERS, D_MODEL, QK_DIM + ATTN_DIM), D_MODEL ** -0.5),
        'q_norm': gain(ks[15], (N_B_LAYERS, HEAD_DIM)),
        'lam': nrm(ks[16], (N_B_LAYERS, 4, HEAD_DIM), 0.1),
        'subln_w': gain(ks[17], (N_B_LAYERS, V_DIM)),
        'w_out_b': nrm(ks[18], (N_B_LAYERS, ATTN_DIM, D_MODEL), ATTN_DIM ** -0.5),
    }

def reference(x_prompt, x_sample, state_conv, cache_k, cache_v, page_table,
              norm_a, w_in_a, conv_w, w_out_a, norm_kv, w_kv, k_norm,
              norm_b, w_in_b, q_norm, lam, subln_w, w_out_b):
    n_seq, n_pages = page_table.shape
    past = n_pages * PAGE_SIZE
    pos_p = jnp.arange(x_prompt.shape[1])
    pos_s = past + jnp.arange(x_sample.shape[1])
    k_past = cache_k[page_table].reshape(n_seq, past, N_HEADS, 2, HEAD_DIM)
    v_past = cache_v[page_table].reshape(n_seq, past, N_HEADS, V_DIM)

    xp, xs = x_prompt, x_sample
    conv_p, conv_s = [], []
    k_p = v_p = k_s = v_s = None
    for layer in range(DEPTH):
        if layer < N_A_LAYERS:
            zero_u = jnp.zeros((xp.shape[0], CONV_WIDTH - 1, CONV_DIM), xp.dtype)
            xp, cp = short_conv_layer(xp, zero_u, norm_a[layer], w_in_a[layer], conv_w[layer], w_out_a[layer])
            xs, cs = short_conv_layer(xs, state_conv[layer], norm_a[layer], w_in_a[layer], conv_w[layer], w_out_a[layer])
            conv_p.append(cp)
            conv_s.append(cs)
            if layer == N_A_LAYERS - 1:
                k_p, v_p = shared_kv(xp, pos_p, norm_kv, w_kv, k_norm)
                k_s, v_s = shared_kv(xs, pos_s, norm_kv, w_kv, k_norm)
        else:
            j = layer - N_A_LAYERS
            lam_init = LAMBDA_INITS[j]
            lam_full = diff_lambda(lam[j], lam_init)
            q, z = diff_query(xp, pos_p, norm_b[j], w_in_b[j], q_norm[j])
            xp = xp + diff_output(diff_attn_prompt(q, k_p, v_p, lam_full), z, subln_w[j], lam_init, w_out_b[j])
            q, z = diff_query(xs, pos_s, norm_b[j], w_in_b[j], q_norm[j])
            xs = xs + diff_output(diff_attn_sample(q, k_s, v_s, k_past, v_past, lam_full), z, subln_w[j], lam_init, w_out_b[j])

    new_conv_p = jnp.stack(conv_p)
    new_conv_s = jnp.stack(conv_s)
    return (xp, xs, k_p, v_p, new_conv_p, k_s, v_s, new_conv_s)


_drawn_inputs = setup_inputs


def setup_inputs(seed=0):
    import zlib

    import numpy as np

    out = dict(_drawn_inputs(seed))
    spreads = {}
    factors = {'norm_kv': 2.833, 'k_norm': 3.044, 'norm_b': 5.992, 'q_norm': 8.0, 'subln_w': 8.0}
    for name, (base, spread) in spreads.items():
        noise = np.random.default_rng([zlib.crc32(name.encode()), seed]).standard_normal(out[name].shape)
        drawn = base * np.exp(spread * noise) if base else spread * noise
        out[name] = __import__('jax').numpy.asarray(drawn.astype(out[name].dtype))
    for name, factor in factors.items():
        out[name] = (out[name] * factor).astype(out[name].dtype)
    return out
```

```python
import math
from contextlib import ExitStack

import concourse.bass as bass
from concourse import mybir

F32 = mybir.dt.float32
F32R = mybir.dt.float32r
I32 = mybir.dt.int32
ALU = mybir.AluOpType
ACT = mybir.ActivationFunctionType
AX = mybir.AxisListType
ds = bass.ds

P = 128
D = 2048
KT = D // P
SEQ = 512
NSEQ, NEW = 8, 4
CONV = 3
H = 8
HC = 2 * H
HD = 128
VD = 256
PAGE = 128
NPG = 16
PAST = NPG * PAGE
G = 2
GP = SEQ // G
GS = NSEQ * NEW // G
GT = GP + GS
T = G * GT
TT = SEQ // P
ROT = HD // 4
THETA = 500000.0
EPS = 1e-6
LAM_INIT = 0.8 - 0.6 * math.exp(-0.3 * 1)
SCALE = HD ** -0.5
BIG = -3.0e38

GA, GKV, GB, CW, KN_, QN_, SUB, LAM = 0, 16, 32, 48, 96, 97, 98, 100
NPAR = 104

SLOTS = 2


class Bag:
    pass


class Chain:

    def __init__(self, eng, sem, base=0):
        self.eng, self.sem, self.base, self.n = eng, sem, base, 0

    def link(self, ins):
        ins.then_inc(self.sem, 1)
        self.n += 1
        self.eng.wait_ge(self.sem, self.base + self.n)


def new_sem(nc, m, name):
    m.sems.append(m.keep.enter_context(nc.semaphore(name)))
    return m.sems[-1]


def grouped(ap):
    return ap.rearrange("p (g t) -> p g t", g=G)


def w_block(w, col):
    return w.rearrange("(k p) n -> p k n", p=P)[:, :, ds(col, P)]


def tiles(ap):
    return ap.rearrange("p (k n) -> p k n", k=KT)


def project_hi(pe, m, s, out, xh, xl):
    for k in range(KT):
        for x in (xh, xl):
            for g in range(G):
                pe.matmul(out[:, g, 0:GT], m.WH[s][:, k * P:(k + 1) * P], x[:, k * T + g * GT:k * T + (g + 1) * GT],
                          start=(k == 0 and x is xh), stop=False, skip_group_check=True)


def project_lo(pe, m, s, out, xh):
    for k in range(KT):
        for g in range(G):
            last = pe.matmul(out[:, g, 0:GT], m.WL[s][:, k * P:(k + 1) * P], xh[:, k * T + g * GT:k * T + (g + 1) * GT],
                             start=False, stop=(k == KT - 1), skip_group_check=True)
    return last


def rsqrt(act, step, at, total, n, m, out, out_squared=None):
    act.activation(out, total, ACT.Ln, bias=m.EPSC[0:total.shape[0], 0:1], scale=1.0 / n).then_inc(step, 1)
    act.wait_ge(step, at + 1)
    if out_squared is not None:
        act.activation(out_squared, out, ACT.Exp, scale=-1.0).then_inc(step, 1)
    return act.activation(out, out, ACT.Exp, scale=-0.5).then_inc(step, 1)


def memory(nc, ctx):
    def sb(name, shape, dt=F32):
        return ctx.enter_context(nc.sbuf_tensor(name, shape, dt))
    m = Bag()
    m.XH = sb("x_hi", [P, KT * T], F32R)
    m.XL = sb("x_lo", [P, KT * T], F32R)
    m.WH = [sb(f"w_hi{s}", [P, D], F32R) for s in range(SLOTS)]
    m.WL = [sb(f"w_lo{s}", [P, D], F32R) for s in range(SLOTS)]
    m.PAR = sb("params", [P, NPAR])
    m.IDENT = sb("ident", [P, P])
    m.ONES = sb("ones", [P, P])
    m.EPSC = sb("eps", [P, 1])
    m.RS = sb("rs", [P, T])
    m.NLAM = sb("neg_lambda", [P, 1])
    m.GSUB = sb("subln_gain", [P, 2])
    m.PS = ctx.enter_context(nc.psum_tensor("psum", [P, 8, 512], F32))
    return m


def read_inputs(nc, m, d, st):
    with ExitStack() as ctx:
        def sb(name, shape, dt=F32):
            return ctx.enter_context(nc.sbuf_tensor(name, shape, dt))

        def sem(name):
            return new_sem(nc, m, name)
        xp = sb("xp_rows", [P, TT, D])
        xs = sb("xs_rows", [GS, G, D])
        srow = sb("state_rows", [GS, D])
        prow = sb("param_rows", [NPAR, P])
        sq = [sb(f"x_sq{s}", [P, T]) for s in range(2)]
        acc = sb("x_sq_sum", [P, T])
        lprod = sb("lam_prod", [P, 2])
        lexp = sb("lam_exp", [P, 2])
        par_in, small_in = sem("par_in"), sem("small_in")
        x_in = [sem(f"x_in{c}") for c in range(4)]
        const_ready, par_t, par_ready = sem("const_ready"), sem("par_transposed"), sem("par_ready")
        xt_ready, xh_ready, xl_ready = sem("xt_ready"), sem("xh_ready"), sem("xl_ready")
        sq_ready, sq_used, sum_ready = sem("sq_ready"), sem("sq_used"), sem("sum_ready")
        state_t, lam_ready, lam_sum, lam_exp = sem("state_transposed"), sem("lam_ready"), sem("lam_sum"), sem("lam_exp")
        act_step, pool_step, dve_step = sem("act_step"), sem("pool_step"), sem("dve_step")
        block = ctx.enter_context(nc.Block())

        @block.sync
        def _(sp):
            rows = [(GA, d["norm_a"].rearrange("l (k p) -> (l k) p", p=P), 16),
                    (GKV, d["norm_kv"].rearrange("(k p) -> k p", p=P), 16),
                    (GB, d["norm_b"].rearrange("l (k p) -> (l k) p", p=P), 16),
                    (CW, d["conv_w"].rearrange("l i (k p) -> (l i k) p", p=P), 48),
                    (KN_, d["k_norm"].rearrange("(k p) -> k p", p=P), 1),
                    (QN_, d["q_norm"], 1),
                    (SUB, d["subln_w"].rearrange("l (k p) -> (l k) p", p=P), 2),
                    (LAM, d["lam"].rearrange("l r p -> (l r) p"), 4)]
            sp.dma_start(xs[:, :, :], d["x_sample"].rearrange("(g b) t c -> (b t) g c", g=G)).then_inc(small_in, 16)
            sp.dma_start(srow[:, :], d["state_conv"].rearrange("l b i c -> (l b i) c")).then_inc(small_in, 16)
            x_rows = d["x_prompt"].rearrange("o (t p) c -> p (o t) c", p=P)
            for c in range(4):
                sp.dma_start(xp[:, :, c * 512:(c + 1) * 512], x_rows[:, :, c * 512:(c + 1) * 512]).then_inc(x_in[c], 16)
            for at, src, n in rows:
                sp.dma_start(prow[at:at + n, :], src).then_inc(par_in, 16)

        @block.gpsimd
        def _(pool):
            pool.memset(m.ONES[:, :], 1.0).then_inc(pool_step, 1)
            pool.memset(m.EPSC[:, :], EPS).then_inc(pool_step, 1)
            pool.memset(acc[:, :], 0.0).then_inc(pool_step, 1)
            pool.memset(m.IDENT[:, :], 0.0).then_inc(pool_step, 1)
            pool.wait_ge(pool_step, 4)
            pool.affine_select(out=m.IDENT[:, :], in_=m.IDENT[:, :], compare_op=ALU.not_equal, fill=1.0, base=0,
                               pattern=[[-1, P]], channel_multiplier=1).then_inc(const_ready, 1)
            for k in range(KT):
                pool.wait_ge(sq_ready, k + 1)
                pool.wait_ge(sq_used, k) if k else None
                pool.tensor_tensor(acc[:, :], acc[:, :], sq[k % 2][:, :], ALU.add).then_inc(sq_used, 1)

        @block.scalar
        def _(act):
            for k in range(KT):
                b = 2 * (k % 2)
                xt = m.PS[:, b:b + 2, 0:GT]
                act.wait_ge(xt_ready, k + 1)
                act.activation(grouped(m.XH[:, k * T:(k + 1) * T]), xt, ACT.Copy).then_inc(xh_ready, 1)
                if k >= 2:
                    act.wait_ge(sq_used, k - 1)
                act.activation(grouped(sq[k % 2][:, :]), xt, ACT.Square).then_inc(sq_ready, 1)
            act.wait_ge(lam_sum, 1)
            act.activation(lexp[:, :], m.PS[:, 4, 256:258], ACT.Exp).then_inc(lam_exp, 1)
            act.wait_ge(sum_ready, 1)
            rsqrt(act, act_step, 0, m.PS[:, 6:8, 0:GT], D, m, grouped(m.RS[:, :]), grouped(st.RS2[:, :]))

        @block.vector
        def _(dve):
            for k in range(KT):
                b = 2 * (k % 2)
                xk = slice(k * T, (k + 1) * T)
                dve.wait_ge(sq_ready, k + 1)
                dve.tensor_tensor(grouped(m.XL[:, xk]), m.PS[:, b:b + 2, 0:GT], grouped(m.XH[:, xk].bitcast(F32)),
                                  ALU.subtract).then_inc(xl_ready, 1)
            dve.wait_ge(par_t, 1)
            dve.tensor_copy(m.PAR[:, :], m.PS[:, 4, 0:NPAR]).then_inc(par_ready, 1)
            dve.wait_ge(par_ready, 1)
            dve.tensor_tensor(lprod[:, :], m.PAR[:, LAM:LAM + 4:2], m.PAR[:, LAM + 1:LAM + 4:2],
                              ALU.mult).then_inc(lam_ready, 1)
            dve.tensor_scalar(m.GSUB[:, :], m.PAR[:, SUB:SUB + 2], 1.0 - LAM_INIT, None, ALU.mult).then_inc(dve_step, 1)
            dve.wait_ge(state_t, 1)
            dve.tensor_copy(st.STATE[:, :], m.PS[:, 5, 0:KT * GS]).then_inc(dve_step, 1)
            dve.wait_ge(lam_exp, 1)
            dve.scalar_tensor_tensor(out=m.NLAM[:, :], in0=lexp[:, 1:2], scalar=-LAM_INIT, in1=lexp[:, 0:1],
                                     op0=ALU.add, op1=ALU.subtract).then_inc(dve_step, 1)

        @block.tensor
        def _(pe):
            pe.wait_ge(const_ready, 1)
            pe.wait_ge(small_in, 32)
            for k in range(KT):
                b = 2 * (k % 2)
                if k % 4 == 0:
                    pe.wait_ge(x_in[k // 4], 16)
                if k >= 2:
                    pe.wait_ge(xl_ready, k - 1)
                for t in range(TT):
                    pe.transpose(m.PS[:, b + t // 2, (t % 2) * P:(t % 2 + 1) * P], xp[:, t, k * P:(k + 1) * P], m.IDENT[:, :])
                for g in range(G):
                    last = pe.transpose(m.PS[:, b + g, GP:GT], xs[:, g, k * P:(k + 1) * P], m.IDENT[0:GS, 0:GS])
                last.then_inc(xt_ready, 1)
            pe.wait_ge(par_in, 8 * 16)
            pe.transpose(m.PS[:, 4, 0:NPAR], prow[:, :], m.IDENT[0:NPAR, 0:NPAR]).then_inc(par_t, 1)
            for k in range(KT):
                last = pe.transpose(m.PS[:, 5, k * GS:(k + 1) * GS], srow[:, k * P:(k + 1) * P], m.IDENT[0:GS, 0:GS])
            last.then_inc(state_t, 1)
            pe.wait_ge(lam_ready, 1)
            pe.matmul(m.PS[:, 4, 256:258], m.ONES[:, :], lprod[:, :], start=True, stop=True).then_inc(lam_sum, 1)
            pe.wait_ge(sq_used, KT)
            for g in range(G):
                last = pe.matmul(m.PS[:, 6 + g, 0:GT], m.ONES[:, :], acc[:, g * GT:(g + 1) * GT], start=True, stop=True)
            last.then_inc(sum_ready, 1)


def conv_in(nc, m, d, st):
    cols = [D, 2 * D, 3 * D, 0]
    NB = 4 * KT
    with ExitStack() as ctx:
        def sb(name, shape, dt=F32):
            return ctx.enter_context(nc.sbuf_tensor(name, shape, dt))

        def sem(name):
            return new_sem(nc, m, name)
        raw = [sb(f"a_raw{s}", [P, D]) for s in range(SLOTS)]
        cg = sb("c_gate", [P, T])
        zs = sb("z", [P, T])
        ex = sb("z_exp", [P, T])
        up = sb("u_prompt", [P, CONV - 1 + SEQ])
        us = sb("u_sample", [P, NSEQ, CONV - 1 + NEW])
        lastu = sb("u_last", [P, 2 + NSEQ * 2])
        lastr = sb("u_last_rows", [2 + NSEQ * 2, P])
        raw_in = [sem(f"a_raw_in{s}") for s in range(SLOTS)]
        scaled, hi_ready, lo_ready = sem("a_scaled"), sem("a_hi_ready"), sem("a_lo_ready")
        block_done, evacuated = sem("a_block_done"), sem("a_evacuated")
        e_ready, yh_ready, yl_ready = sem("a_e_ready"), sem("a_yh_ready"), sem("a_yl_ready")
        lu_ready, lu_turned, lr_ready, lr_out = sem("a_lu_ready"), sem("a_lu_turned"), sem("a_lr_ready"), sem("a_lr_out")
        dve_step, granted = sem("a_dve_step"), sem("a_slot_granted")
        block = ctx.enter_context(nc.Block())
        psum = [m.PS[:, 2 * s:2 * s + 2, :] for s in range(SLOTS)]

        @block.sync
        def _(sp):
            with sp.Fori(0, KT) as j:
                for p in range(4):
                    sp.wait_ge(lo_ready, j * 4 + (p + 1))
                    sp.sem_inc(granted, 1)
                    sp.dma_start(tiles(raw[p % 2][:, :]), w_block(d["w_in_a"][0], j * P + cols[p])).then_inc(raw_in[p % 2], 16)

        @block.gpsimd
        def _(pool):
            with pool.Fori(0, KT) as j:
                for p in range(4):
                    pool.wait_ge(raw_in[p % 2], j * 32 + 16 * (p // 2 + 1))
                    pool.tensor_tensor(tiles(raw[p % 2][:, :]), tiles(raw[p % 2][:, :]),
                                       m.PAR[:, GA:GA + KT].unsqueeze(2).to_broadcast([P, KT, P]),
                                       ALU.mult).then_inc(scaled, 1)

        @block.scalar
        def _(act):
            def split_hi(j, p):
                act.wait_ge(scaled, j * 4 + (p + 1))
                act.wait_ge(block_done, j * 4 + (p + 1))
                act.activation(m.WH[p % 2][:, :], raw[p % 2][:, :], ACT.Copy).then_inc(hi_ready, 1)

            def body(j, last=False):
                split_hi(j, 1)
                split_hi(j, 2)
                split_hi(j, 3)
                act.wait_ge(evacuated, j * 4 + (3 + SLOTS))
                act.activation(ex[:, :], zs[:, :], ACT.Exp, scale=-1.0).then_inc(e_ready, 1)
                act.wait_ge(lu_turned, j + 2)
                act.activation(lastr[:, :], m.PS[0:18, 6, 0:P], ACT.Copy).then_inc(lr_ready, 1)
                act.wait_ge(lr_ready, j + 2)
                act.dma_start(d["new_conv_prompt"].rearrange("l o i c -> (l o i) c")[:, ds(j * P, P)],
                              lastr[0:2, :]).then_inc(lr_out, 16)
                act.dma_start(d["new_conv_sample"].rearrange("l b i c -> (l b i) c")[:, ds(j * P, P)],
                              lastr[2:18, :]).then_inc(lr_out, 16)
                if not last:
                    split_hi(j, 4)
                act.wait_ge(evacuated, j * 4 + (4 + SLOTS))
                act.activation(st.YH[:, ds(j * T, T)], zs[:, :], ACT.Copy).then_inc(yh_ready, 1)
                act.wait_ge(lr_out, j * 32 + 32)
            act.sem_inc(lr_ready, 1)
            split_hi(0, 0)
            with act.Fori(0, KT - 1) as j:
                body(j)
            body(KT - 1, last=True)

        @block.vector
        def _(dve):
            dve.sem_inc(lo_ready, SLOTS)
            dve.sem_inc(evacuated, SLOTS)
            dve.sem_inc(yl_ready, 1)
            dve.memset(up[:, 0:2], 0.0).then_inc(dve_step, 1)
            dve.wait_ge(dve_step, 1)
            per = 18

            def split_lo(j, p):
                dve.wait_ge(hi_ready, j * 4 + (p + 1))
                dve.wait_ge(block_done, j * 4 + (p + 1))
                dve.tensor_tensor(m.WL[p % 2][:, :], raw[p % 2][:, :], m.WH[p % 2][:, :].bitcast(F32),
                                  ALU.subtract).then_inc(lo_ready, 1)

            def body(j, last=False):
                chain = Chain(dve, dve_step, j * per + 1)
                split_lo(j, 1)
                dve.wait_ge(block_done, j * 4 + (1 + SLOTS))
                dve.tensor_tensor(grouped(cg[:, :]), psum[0][:, :, 0:GT], grouped(st.RS2[:, :]), ALU.mult).then_inc(evacuated, 1)
                split_lo(j, 2)
                chain.link(dve.tensor_copy(us[:, :, 0:2], st.STATE[:, ds(j * GS, GS)].rearrange("p (b i) -> p b i", i=2)))
                dve.wait_ge(block_done, j * 4 + (2 + SLOTS))
                dve.wait_ge(evacuated, j * 4 + (1 + SLOTS))
                chain.link(dve.tensor_tensor(up[:, 2:2 + SEQ].rearrange("p (g t) -> p g t", g=G), psum[1][:, :, 0:GP],
                                             grouped(cg[:, :])[:, :, 0:GP], ALU.mult))
                for g in range(G):
                    ins = dve.tensor_tensor(us[:, 4 * g:4 * g + 4, 2:6],
                                            psum[1][:, g, GP:GT].rearrange("p (b t) -> p b t", t=NEW),
                                            cg[:, g * GT + GP:(g + 1) * GT].rearrange("p (b t) -> p b t", t=NEW), ALU.mult)
                    if g == 0:
                        chain.link(ins)
                    else:
                        ins.then_inc(evacuated, 1)
                dve.wait_ge(evacuated, j * 4 + (2 + SLOTS))
                split_lo(j, 3)
                dve.wait_ge(lu_turned, j + 1)
                chain.link(dve.tensor_copy(lastu[:, 0:2], up[:, SEQ:SEQ + 2]))
                dve.tensor_copy(lastu[:, 2:18].rearrange("p (b i) -> p b i", i=2), us[:, :, 4:6]).then_inc(lu_ready, 1)
                tap = [m.PAR[:, ds(j + (CW + KT * i), 1)] for i in range(CONV)]
                cvp = grouped(cg[:, :])[:, :, 0:GP]
                chain.link(dve.tensor_scalar(cvp, up[:, 2:2 + SEQ].rearrange("p (g t) -> p g t", g=G), tap[2], None, ALU.mult))
                for i in (1, 0):
                    chain.link(dve.scalar_tensor_tensor(out=cvp, in0=up[:, i:i + SEQ].rearrange("p (g t) -> p g t", g=G),
                                                        scalar=tap[i], in1=cvp, op0=ALU.mult, op1=ALU.add))
                for g in range(G):
                    cvs = cg[:, g * GT + GP:(g + 1) * GT].rearrange("p (b t) -> p b t", t=NEW)
                    ub = us[:, 4 * g:4 * g + 4, :]
                    chain.link(dve.tensor_scalar(cvs, ub[:, :, 2:6], tap[2], None, ALU.mult))
                    for i in (1, 0):
                        chain.link(dve.scalar_tensor_tensor(out=cvs, in0=ub[:, :, i:i + 4], scalar=tap[i], in1=cvs,
                                                            op0=ALU.mult, op1=ALU.add))
                dve.wait_ge(block_done, j * 4 + (3 + SLOTS))
                dve.wait_ge(yl_ready, j + 1)
                dve.tensor_tensor(grouped(zs[:, :]), psum[0][:, :, 0:GT], grouped(m.RS[:, :]), ALU.mult).then_inc(evacuated, 1)
                if not last:
                    split_lo(j, 4)
                dve.wait_ge(e_ready, j + 1)
                chain.link(dve.tensor_scalar(ex[:, :], ex[:, :], 1.0, None, ALU.add))
                chain.link(dve.reciprocal(ex[:, :], ex[:, :]))
                chain.link(dve.tensor_tensor(ex[:, :], ex[:, :], zs[:, :], ALU.mult))
                chain.link(dve.tensor_tensor(cg[:, :], cg[:, :], ex[:, :], ALU.mult))
                chain.link(dve.tensor_tensor(cg[:, :], cg[:, :], m.RS[:, :], ALU.mult))
                assert chain.n == per
                dve.wait_ge(block_done, j * 4 + (4 + SLOTS))
                dve.tensor_tensor(grouped(zs[:, :]), psum[1][:, :, 0:GT], grouped(cg[:, :]), ALU.mult).then_inc(evacuated, 1)
                dve.wait_ge(yh_ready, j + 1)
                dve.tensor_tensor(st.YL[:, ds(j * T, T)], zs[:, :], st.YH[:, ds(j * T, T)].bitcast(F32),
                                  ALU.subtract).then_inc(yl_ready, 1)
            split_lo(0, 0)
            with dve.Fori(0, KT - 1) as j:
                body(j)
            body(KT - 1, last=True)

        @block.tensor
        def _(pe):
            pe.sem_inc(block_done, SLOTS)
            pe.sem_inc(lu_turned, 1)
            with pe.Fori(0, KT) as j:
                for p in range(4):
                    pe.wait_ge(hi_ready, j * 4 + (p + 1))
                    pe.wait_ge(evacuated, j * 4 + (p + 1))
                    project_hi(pe, m, p % 2, psum[p % 2], m.XH, m.XL)
                    pe.wait_ge(lo_ready, j * 4 + (p + 1 + SLOTS))
                    project_lo(pe, m, p % 2, psum[p % 2], m.XH).then_inc(block_done, 1)
                    if p == 2:
                        pe.wait_ge(lu_ready, j + 1)
                        pe.wait_ge(lr_ready, j + 1)
                        pe.transpose(m.PS[0:18, 6, 0:P], lastu[:, :], m.IDENT[:, :]).then_inc(lu_turned, 1)


def conv_out(nc, m, d, st):
    with ExitStack() as ctx:
        def sb(name, shape, dt=F32):
            return ctx.enter_context(nc.sbuf_tensor(name, shape, dt))

        def sem(name):
            return new_sem(nc, m, name)
        raw = [sb(f"o_raw{s}", [P, D]) for s in range(SLOTS)]
        x1 = sb("x1", [P, T])
        sq = sb("x1_sq", [P, T])
        acc = sb("x1_sq_sum", [P, T])
        raw_in = [sem(f"o_raw_in{s}") for s in range(SLOTS)]
        hi_ready, lo_ready, block_done, evacuated = sem("o_hi_ready"), sem("o_lo_ready"), sem("o_block_done"), sem("o_evacuated")
        x1_ready, x1_split, xh_ready, sq_ready, sq_used = (sem("o_x1_ready"), sem("o_x1_split"), sem("o_xh_ready"),
                                                           sem("o_sq_ready"), sem("o_sq_used"))
        sum_ready, act_step = sem("o_sum_ready"), sem("o_act_step")
        granted = sem("o_slot_granted")
        block = ctx.enter_context(nc.Block())
        psum = [m.PS[:, 2 * s:2 * s + 2, :] for s in range(SLOTS)]

        @block.sync
        def _(sp):
            with sp.Fori(0, KT // 2) as pair:
                j = pair * 2
                for s in range(2):
                    sp.wait_ge(lo_ready, j + (s + 1))
                    sp.sem_inc(granted, 1)
                    sp.dma_start(tiles(raw[s][:, :]), w_block(d["w_out_a"][0], j * P + s * P)).then_inc(raw_in[s], 16)

        @block.gpsimd
        def _(pool):
            pool.memset(acc[:, :], 0.0).then_inc(sq_used, 1)
            with pool.Fori(0, KT) as j:
                pool.wait_ge(sq_ready, j + 2)
                pool.wait_ge(sq_used, j + 1)
                pool.tensor_tensor(acc[:, :], acc[:, :], sq[:, :], ALU.add).then_inc(sq_used, 1)

        @block.scalar
        def _(act):
            def split_hi(j, s):
                act.wait_ge(raw_in[s % 2], j * 8 + 16 * (s // 2 + 1))
                act.wait_ge(block_done, j + (s + 1))
                act.activation(m.WH[s % 2][:, :], raw[s % 2][:, :], ACT.Copy).then_inc(hi_ready, 1)

            def body(j, last=False):
                for s in range(2):
                    if not (last and s == 1):
                        split_hi(j, s + 1)
                    act.wait_ge(x1_ready, j + (s + 1))
                    act.activation(m.XH[:, ds((j + s) * T, T)], x1[:, :], ACT.Copy).then_inc(xh_ready, 1)
                    act.wait_ge(sq_used, j + (s + 1))
                    act.activation(sq[:, :], x1[:, :], ACT.Square).then_inc(sq_ready, 1)
            act.sem_inc(sq_ready, 1)
            split_hi(0, 0)
            with act.Fori(0, KT // 2 - 1) as pair:
                body(pair * 2)
            body(KT - 2, last=True)
            act.wait_ge(sum_ready, 1)
            rsqrt(act, act_step, 0, m.PS[:, 6:8, 0:GT], D, m, grouped(m.RS[:, :]))

        @block.vector
        def _(dve):
            dve.sem_inc(lo_ready, SLOTS)
            dve.sem_inc(x1_split, 1)

            def split_lo(j, s):
                dve.wait_ge(hi_ready, j + (s + 1))
                dve.wait_ge(block_done, j + (s + 1))
                dve.tensor_tensor(m.WL[s % 2][:, :], raw[s % 2][:, :], m.WH[s % 2][:, :].bitcast(F32),
                                  ALU.subtract).then_inc(lo_ready, 1)

            def body(j, last=False):
                for s in range(2):
                    if not (last and s == 1):
                        split_lo(j, s + 1)
                    xj = ds((j + s) * T, T)
                    dve.wait_ge(block_done, j + (s + 1 + SLOTS))
                    dve.wait_ge(x1_split, j + (s + 1))
                    dve.wait_ge(sq_ready, j + (s + 1))
                    dve.tensor_tensor(grouped(x1[:, :]), psum[s][:, :, 0:GT], grouped(m.XH[:, xj].bitcast(F32)),
                                      ALU.add).then_inc(evacuated, 1)
                    dve.wait_ge(evacuated, j + (s + 1))
                    dve.tensor_tensor(x1[:, :], x1[:, :], m.XL[:, xj].bitcast(F32), ALU.add).then_inc(x1_ready, 1)
                    dve.wait_ge(xh_ready, j + (s + 1))
                    dve.tensor_tensor(m.XL[:, xj], x1[:, :], m.XH[:, xj].bitcast(F32), ALU.subtract).then_inc(x1_split, 1)
            split_lo(0, 0)
            with dve.Fori(0, KT // 2 - 1) as pair:
                body(pair * 2)
            body(KT - 2, last=True)

        @block.tensor
        def _(pe):
            pe.sem_inc(block_done, SLOTS)
            def one(j, s, wait):
                pe.wait_ge(hi_ready, j + (s + 1))
                if wait:
                    pe.wait_ge(evacuated, j + (s - 1))
                project_hi(pe, m, s, psum[s], st.YH, st.YL)
                pe.wait_ge(lo_ready, j + (s + 1 + SLOTS))
                project_lo(pe, m, s, psum[s], st.YH).then_inc(block_done, 1)
            for s in range(2):
                one(0, s, False)
            with pe.Fori(1, KT // 2) as pair:
                for s in range(2):
                    one(pair * 2, s, True)
            pe.wait_ge(sq_used, KT + 1)
            for g in range(G):
                last = pe.matmul(m.PS[:, 6 + g, 0:GT], m.ONES[:, :], acc[:, g * GT:(g + 1) * GT], start=True, stop=True)
            last.then_inc(sum_ready, 1)


def project_heads(nc, m, d, st, kind):
    w, col0, gain = {"q": (d["w_in_b"][0], 0, GB), "k": (d["w_kv"], 0, GKV), "v": (d["w_kv"], D, GKV)}[kind]
    norm, turn = kind != "v", kind != "q"
    ngain = {"q": QN_, "k": KN_, "v": None}[kind]
    scratch = {"q": d["q_scratch"], "k": d["k_scratch"], "v": None}[kind]
    keep = {"q": st.QS, "k": st.KS, "v": None}[kind]
    with ExitStack() as ctx:
        def sb(name, shape, dt=F32):
            return ctx.enter_context(nc.sbuf_tensor(f"{kind}_{name}", shape, dt))

        def sem(name):
            return new_sem(nc, m, f"{kind}_{name}")
        raw = [sb(f"raw{s}", [P, D]) for s in range(2)]
        plain = [sb(f"plain{s}", [P, T]) for s in range(2)]
        sq = sb("sq", [P, T])
        r = [sb(f"r{s}", [P, T]) for s in range(2)]
        tile = [sb(f"tile{s}", [P, T]) for s in range(2)]
        swap = sb("swap", [ROT, T])
        cos, sin = sb("cos", [ROT, T]), sb("sin", [ROT, T])
        rows = [sb(f"rows{s}", [P, TT * P]) for s in range(2)]
        srows = [sb(f"srows{s}", [GS, G * P]) for s in range(2)]
        raw_in = [sem(f"raw_in{s}") for s in range(2)]
        tables_in = sem("tables_in")
        scaled, hi_ready, lo_ready = sem("scaled"), sem("hi_ready"), sem("lo_ready")
        block_done, evacuated = sem("block_done"), sem("evacuated")
        sq_ready, summed, ln_step, tile_ready = sem("sq_ready"), sem("summed"), sem("ln_step"), sem("tile_ready")
        turned, rows_ready, granted, dve_step = sem("turned"), sem("rows_ready"), sem("granted"), sem("dve_step")
        scratch_out = [sem(f"scratch_out{s}") for s in range(2)]
        rows_out = [sem(f"rows_out{s}") for s in range(2)]
        block = ctx.enter_context(nc.Block())
        psum = [m.PS[:, 2 * s:2 * s + 2, :] for s in range(2)]
        N = KT

        @block.sync
        def _(sp):
            if norm:
                sp.dma_start(cos[:, :], d["rope_cos"]).then_inc(tables_in, 16)
                sp.dma_start(sin[:, :], d["rope_sin"]).then_inc(tables_in, 16)
            with sp.Fori(0, N // 2) as pair:
                for s in range(2):
                    sp.wait_ge(lo_ready, pair * 2 + (s + 1))
                    sp.sem_inc(granted, 1)
                    sp.dma_start(tiles(raw[s][:, :]), w_block(w, pair * 2 * P + (s * P + col0))).then_inc(raw_in[s], 16)

        @block.gpsimd
        def _(pool):
            with pool.Fori(0, N // 2) as pair:
                for s in range(2):
                    pool.wait_ge(raw_in[s], pair * 16 + 16)
                    pool.tensor_tensor(tiles(raw[s][:, :]), tiles(raw[s][:, :]),
                                       m.PAR[:, gain:gain + KT].unsqueeze(2).to_broadcast([P, KT, P]),
                                       ALU.mult).then_inc(scaled, 1)

        @block.scalar
        def _(act):
            out_p = {"k": d["new_k_prompt"].rearrange("o (t p) h c d -> p (o t) (h c d)", p=P),
                     "v": d["new_v_prompt"].rearrange("o (t p) h e -> p (o t) (h e)", p=P)}.get(kind)
            out_s = {"k": d["new_k_sample"].rearrange("(g b) t h c d -> (b t) g (h c d)", g=G),
                     "v": d["new_v_sample"].rearrange("(g b) t h e -> (b t) g (h e)", g=G)}.get(kind)

            def split_hi(n, s):
                act.wait_ge(scaled, n + 1)
                act.wait_ge(block_done, n + 1)
                act.activation(m.WH[s][:, :], raw[s][:, :], ACT.Copy).then_inc(hi_ready, 1)

            def store_tile(n, s):
                if scratch is not None:
                    act.wait_ge(tile_ready, n + 3)
                    act.dma_start(scratch.rearrange("m p t -> p m t")[:, ds(n, 1), :].rearrange("p m (g t) -> p (m g) t", g=G),
                                  grouped(tile[s][:, :])[:, :, 0:GP]).then_inc(scratch_out[s], 16)

            def store_rows(n, s, slot_uses):
                if turn:
                    act.wait_ge(turned, n + 3)
                    act.wait_ge(rows_out[s], slot_uses * 32 + 32)
                    act.activation(rows[s][:, :], m.PS[:, 6, :], ACT.Copy).then_inc(rows_ready, 1)
                    act.activation(srows[s][:, :], m.PS[0:GS, 7, 0:G * P], ACT.Copy).then_inc(rows_ready, 1)
                    act.wait_ge(rows_ready, n * 2 + 3)
                    act.dma_start(out_p[:, :, ds(n * P, P)], rows[s][:, :].rearrange("p (t c) -> p t c", t=TT)).then_inc(rows_out[s], 16)
                    act.dma_start(out_s[:, :, ds(n * P, P)], srows[s][:, :].rearrange("p (g c) -> p g c", g=G)).then_inc(rows_out[s], 16)

            def norm_scale(n, s):
                if norm:
                    act.wait_ge(summed, n + 1)
                    act.wait_ge(tile_ready, n + 1)
                    rsqrt(act, ln_step, n * 2, m.PS[:, 4:6, 0:GT], HD, m, grouped(r[s][:, :]))

            def square(n, s):
                if norm:
                    act.wait_ge(evacuated, n + 3)
                    act.activation(sq[:, :], plain[s][:, :], ACT.Square).then_inc(sq_ready, 1)

            def body(n, s):
                if isinstance(n, int) and n == N - 1:
                    pass
                else:
                    split_hi(n + 1, 1 - s)
                if not isinstance(n, int) or n >= 2:
                    store_tile(n - 2, s)
                    half = (pair_of(n, s) - 1)
                    store_rows(n - 2, s, half)
                if not isinstance(n, int) or n >= 1:
                    norm_scale(n - 1, 1 - s)
                square(n, s)

            act.sem_inc(rows_ready, 1)
            for s in range(2):
                act.sem_inc(scratch_out[s], 16)
                act.sem_inc(rows_out[s], 32)
            split_hi(0, 0)
            pairs = {}

            def pair_of(n, s):
                return n // 2 if isinstance(n, int) else pairs["at"]
            for n in range(2):
                body(n, n)
            with act.Fori(1, N // 2 - 1) as pair:
                pairs["at"] = pair
                for s in range(2):
                    body(pair * 2 + s, s)
            for n in range(N - 2, N):
                body(n, n % 2)
            norm_scale(N - 1, 1)
            for n in range(N - 2, N):
                store_tile(n, n % 2)
                store_rows(n, n % 2, n // 2)
            for s in range(2):
                act.wait_ge(scratch_out[s], 16 * (N // 2 + 1) if scratch is not None else 16)
                act.wait_ge(rows_out[s], 32 * (N // 2 + 1) if turn else 32)

        @block.vector
        def _(dve):
            per = 5

            def split_lo(n, s):
                dve.wait_ge(hi_ready, n + 1)
                dve.wait_ge(block_done, n + 1)
                dve.tensor_tensor(m.WL[s][:, :], raw[s][:, :], m.WH[s][:, :].bitcast(F32), ALU.subtract).then_inc(lo_ready, 1)

            def finish(n, s, uses):
                chain = Chain(dve, dve_step, n * per)
                t, t32 = tile[s], tile[s][0:ROT, :]
                dve.wait_ge(ln_step, n * 2 + 2)
                dve.wait_ge(scratch_out[s], uses * 16 + 16)
                if turn:
                    dve.wait_ge(turned, n + 1)
                chain.link(dve.scalar_tensor_tensor(out=t[:, :], in0=plain[s][:, :], scalar=m.PAR[:, ngain:ngain + 1],
                                                    in1=r[s][:, :], op0=ALU.mult, op1=ALU.mult))
                half = ROT // 2
                dve.sem_inc(granted, 1)
                chain.link(dve.stream_shuffle(swap[:, :], t32, [(i + half) % ROT for i in range(ROT)]))
                chain.link(dve.tensor_tensor(swap[:, :], swap[:, :], sin[:, :], ALU.mult))
                chain.link(dve.tensor_tensor(t32, t32, cos[:, :], ALU.mult))
                chain.link(dve.tensor_tensor(t32, t32, swap[:, :], ALU.add))
                dve.tensor_copy(keep[:, ds(n * G * GS, G * GS)].rearrange("p (g t) -> p g t", g=G),
                                grouped(t[:, :])[:, :, GP:GT]).then_inc(tile_ready, 1)
                assert chain.n == per

            def body(n, s, uses):
                if not (isinstance(n, int) and n == N - 1):
                    split_lo(n + 1, 1 - s)
                dve.wait_ge(block_done, n + 3)
                if norm:
                    dve.tensor_tensor(grouped(plain[s][:, :]), psum[s][:, :, 0:GT], grouped(m.RS[:, :]), ALU.mult).then_inc(evacuated, 1)
                    if not isinstance(n, int) or n >= 1:
                        finish(n - 1, 1 - s, uses if s else uses - 1)
                else:
                    dve.wait_ge(turned, n + 1)
                    dve.tensor_tensor(grouped(tile[s][:, :]), psum[s][:, :, 0:GT], grouped(m.RS[:, :]), ALU.mult).then_inc(evacuated, 1)

            dve.sem_inc(lo_ready, 2)
            dve.sem_inc(evacuated, 2)
            dve.sem_inc(tile_ready, 2)
            if norm:
                dve.wait_ge(tables_in, 32)
            split_lo(0, 0)
            for n in range(2):
                body(n, n, 0)
            with dve.Fori(1, N // 2 - 1) as pair:
                for s in range(2):
                    body(pair * 2 + s, s, pair)
            for n in range(N - 2, N):
                body(n, n % 2, N // 2 - 1)
            if norm:
                finish(N - 1, 1, N // 2 - 1)

        @block.tensor
        def _(pe):
            def turn_tile(n, s):
                if turn:
                    pe.wait_ge(tile_ready if norm else evacuated, n + 3)
                    pe.wait_ge(rows_ready, n * 2 + 1)
                    for t in range(TT):
                        pe.transpose(m.PS[:, 6, t * P:(t + 1) * P],
                                     tile[s][:, (t // 2) * GT + (t % 2) * P:(t // 2) * GT + (t % 2 + 1) * P], m.IDENT[:, :])
                    for g in range(G):
                        last = pe.transpose(m.PS[0:GS, 7, g * P:(g + 1) * P], tile[s][:, g * GT + GP:(g + 1) * GT], m.IDENT[:, :])
                    last.then_inc(turned, 1)

            def sum_squares(n):
                if norm:
                    pe.wait_ge(sq_ready, n + 1)
                    if not isinstance(n, int) or n >= 1:
                        pe.wait_ge(ln_step, n * 2)
                    for g in range(G):
                        last = pe.matmul(m.PS[:, 4 + g, 0:GT], m.ONES[:, :], sq[:, g * GT:(g + 1) * GT], start=True, stop=True)
                    last.then_inc(summed, 1)

            def body(n, s):
                pe.wait_ge(hi_ready, n + 1)
                pe.wait_ge(evacuated, n + 1)
                project_hi(pe, m, s, psum[s], m.XH, m.XL)
                if not isinstance(n, int) or n >= 2:
                    turn_tile(n - 2, s)
                if not isinstance(n, int) or n >= 1:
                    sum_squares(n - 1)
                pe.wait_ge(lo_ready, n + 3)
                project_lo(pe, m, s, psum[s], m.XH).then_inc(block_done, 1)

            pe.sem_inc(block_done, 2)
            pe.sem_inc(turned, 2)
            for n in range(2):
                body(n, n)
            with pe.Fori(1, N // 2) as pair:
                for s in range(2):
                    body(pair * 2 + s, s)
            turn_tile(N - 2, 0)
            sum_squares(N - 1)
            turn_tile(N - 1, 1)


def attention(nc, m, d, st):
    items = ([("z", 0)] + [("k", p) for p in range(12)] + [("z", 1)] + [("k", p) for p in range(12, NPG)]
             + [("vn", 0)] + [("v", p) for p in range(NPG)])
    NR = st.NR
    place = {it: t for t, it in enumerate(items)}
    uses = [len(range(s, len(items), NR)) for s in range(NR)]
    HQ = HC * NEW
    WQ = H * NEW
    with ExitStack() as ctx:
        def sb(name, shape, dt=F32):
            return ctx.enter_context(nc.sbuf_tensor(name, shape, dt))

        def sem(name):
            return new_sem(nc, m, name)
        ring = [sb(f"ring{s}", [P, D]) for s in range(NR)]
        kt = [sb(f"key_t{q}", [P, 4 * PAGE]) for q in range(4)]
        pr = sb("probs", [P, NPG * HQ])
        wt = sb("weights", [P, NPG * WQ])
        qcur, kcur = sb("q_cur", [P, HQ]), sb("k_cur", [P, HQ])
        prn = sb("probs_new", [NEW, HQ])
        wtn = sb("weights_new", [NEW, WQ])
        mx, mc, mdiag, mb = sb("max_part", [P, HQ]), sb("max_col", [HQ, 1]), sb("max_diag", [HQ, HQ]), sb("max_row", [P, HQ])
        den, inv = sb("denom", [P, HQ]), sb("inv_denom", [P, HQ])
        mask_new, mask_diag = sb("mask_new", [NEW, NEW]), sb("mask_diag", [P, P])
        pages = sb("page_ids", [1, NSEQ * NPG], I32)
        qh, kh, vh = sb("q_head", [P, 2 * SEQ]), sb("k_head", [P, 2 * SEQ]), sb("v_head", [P, TT * VD])
        pp = sb("prompt_probs", [P, 2 * SEQ])
        pmx, pden, pinv = sb("prompt_max", [P, 2]), sb("prompt_denom", [P, 2]), sb("prompt_inv", [P, 2])
        pwt = sb("prompt_weights_t", [P, TT * SEQ])
        o = sb("o_head", [P, 2 * SEQ])
        ro = sb("o_rms", [P, SEQ])
        z = [sb(f"z_head{e}", [P, T]) for e in range(2)]
        ez = sb("z_head_exp", [P, T])
        ost, zst = sb("o_sample", [P, HC * G * GS]), sb("z_sample", [P, HC * G * GS])

        page_in = [sem(f"page_in{s}") for s in range(NR)]
        page_free = [sem(f"page_free{s}") for s in range(NR)]
        ids_in, page_id_step = sem("ids_in"), sem("page_id_step")
        const_ready, const_step = sem("const2_ready"), sem("const2_step")
        cur_ready = sem("cur_ready")
        scaled, hi_ready, lo_ready = sem("z_scaled"), sem("z_hi_ready"), sem("z_lo_ready")
        z_done, z_evac, z_exp, z_silu = sem("z_done"), sem("z_evac"), sem("z_exp"), sem("z_silu")
        kt_turned, kt_act, kt_dve, scored = sem("kt_turned"), sem("kt_act"), sem("kt_dve"), sem("scored")
        new_scored, max_ready, max_turned, diag_ready, max_spread = (sem("new_scored"), sem("max_ready"), sem("max_turned"),
                                                                     sem("diag_ready"), sem("max_spread"))
        shifted, exp_ready, den_ready, den_sum, weights_ready = (sem("shifted"), sem("exp_ready"), sem("den_ready"),
                                                                 sem("den_sum"), sem("weights_ready"))
        out_done, out_taken = sem("out_done"), sem("out_taken")
        head_in = [sem(f"head_in{n}") for n in range(3)]
        prompt_scored, prompt_maxed, prompt_exp, prompt_w = (sem("prompt_scored"), sem("prompt_maxed"), sem("prompt_exp"),
                                                             sem("prompt_w"))
        prompt_turned, prompt_wt, o_done, o_taken = sem("prompt_turned"), sem("prompt_wt"), sem("o_done"), sem("o_taken")
        osq_ready, osq_sum, o_ln, y_ready, y_out = sem("osq_ready"), sem("osq_sum"), sem("o_ln"), sem("y_ready"), sem("y_out")
        dve_step, dve_tail, act_tail = sem("b_dve_step"), sem("b_dve_tail"), sem("b_act_tail")
        wait_taken, y_stored = sem("wait_taken"), sem("y_stored")
        fin_sq, fin_sum, fin_r = sem("fin_sq"), sem("fin_sum"), sem("fin_r")
        block = ctx.enter_context(nc.Block())

        S = m.PS[:, 6:8, :]
        SMALL = 4
        OUT = m.PS[:, 6, 0:HC * NEW]
        zps = [m.PS[:, 0:2, 0:GT], m.PS[:, 2:4, 0:GT]]

        def slot(it):
            return ring[place[it] % NR]

        def arrived(eng, i, it):
            t = place[it]
            eng.wait_ge(page_in[t % NR], i * (16 * uses[t % NR]) + 16 * (t // NR + 1))

        @block.sync
        def _(sp):
            sp.dma_start(pages[:, :], d["page_table"].rearrange("(o b) p -> o (b p)", o=1)).then_inc(ids_in, 16)
            sp.wait_ge(ids_in, 16)
            new_v = d["new_v_sample"].rearrange("b t h e -> b t (h e)")
            n_phys = d["cache_k"].shape[0]
            cache_k = d["cache_k"].rearrange("n p h c d -> n p (h c d)")
            cache_v = d["cache_v"].rearrange("n p h e -> n p (h e)")
            with sp.Fori(0, NSEQ) as i:
                for t, (what, p) in enumerate(items):
                    s = t % NR
                    if what in "kv":
                        page = sp.value_load(pages[0:1, ds(i * NPG + p, 1)], min_val=0, max_val=n_phys - 1)
                        src = (cache_k if what == "k" else cache_v)[ds(page, 1), :, :].rearrange("o p n -> (o p) n")
                        dst = ring[s][:, :]
                    elif what == "vn":
                        src = new_v[ds(i, 1), :, :].rearrange("o t n -> (o t) n")
                        dst = ring[s][0:NEW, :]
                    else:
                        src = w_block(d["w_in_b"][0], i * 2 * P + (D + p * P))
                        dst = tiles(ring[s][:, :])
                    sp.wait_ge(page_free[s], i * uses[s] + (t // NR + 1))
                    sp.sem_inc(page_id_step, 1)
                    sp.dma_start(dst, src).then_inc(page_in[s], 16)

        @block.gpsimd
        def _(pool):
            pool.memset(mask_new[:, :], 0.0).then_inc(const_step, 1)
            pool.memset(mask_diag[:, :], 0.0).then_inc(const_step, 1)
            pool.wait_ge(const_step, 2)
            pool.affine_select(out=mask_new[:, :], in_=mask_new[:, :], compare_op=ALU.is_ge, fill=BIG, base=0,
                               pattern=[[1, NEW]], channel_multiplier=-1).then_inc(const_ready, 1)
            pool.affine_select(out=mask_diag[:, :], in_=mask_diag[:, :], compare_op=ALU.is_ge, fill=BIG, base=0,
                               pattern=[[-1, P]], channel_multiplier=1).then_inc(const_ready, 1)
            pool.sem_inc(y_stored, 1)
            with pool.Fori(0, NSEQ) as i:
                pool.wait_ge(new_scored, i + 1)
                for dst, src in ((qcur, st.QS), (kcur, st.KS)):
                    pool.tensor_copy(dst[:, :].rearrange("p (m t) -> p m t", t=NEW),
                                     src[:, :].rearrange("p (m t) -> p m t", t=G * GS)[:, :, ds(i * NEW, NEW)]).then_inc(cur_ready, 1)
                for e in range(2):
                    arrived(pool, i, ("z", e))
                    zw = tiles(slot(("z", e))[:, :])
                    pool.tensor_tensor(zw, zw, m.PAR[:, GB:GB + KT].unsqueeze(2).to_broadcast([P, KT, P]),
                                       ALU.mult).then_inc(scaled, 1)
                pool.wait_ge(y_ready, i + 1)
                pool.sem_inc(page_id_step, 1)
                pool.dma_start(d["y_scratch"].rearrange("m p t -> p m t")[:, ds(i * 2, 2), :],
                               o[:, :].rearrange("p (e t) -> p e t", e=2)).then_inc(y_out, 16)
                pool.wait_ge(y_out, i * 16 + 16)
                pool.sem_inc(y_stored, 1)

        @block.scalar
        def _(act):
            act.sem_inc(o_ln, 2)

            def split_hi(i, e):
                act.wait_ge(scaled, i * 2 + (e + 1))
                act.wait_ge(z_done, i * 2 + (e + 1))
                act.activation(m.WH[e][:, :], slot(("z", e))[:, :], ACT.Copy).then_inc(hi_ready, 1)

            def o_scale(i):
                act.wait_ge(osq_sum, i + 1)
                rsqrt(act, o_ln, i * 2 + 2, m.PS[:, 2, 0:SEQ], VD, m, ro[:, :])

            with act.Fori(0, NSEQ) as i:
                act.wait_ge(o_done, i + 1)
                for n, (dst, src) in enumerate(((qh, d["q_scratch"]), (kh, d["k_scratch"]))):
                    act.dma_start(dst[:, :].rearrange("p (c t) -> p c t", c=2),
                                  src.rearrange("m p t -> p m t")[:, ds(i * 2, 2), :]).then_inc(head_in[n], 16)
                act.dma_start(vh[:, :].rearrange("p (t e) -> p t e", t=TT),
                              d["new_v_prompt"].rearrange("o (t p) h e -> p (o t) (h e)", p=P)[:, :, ds(i * VD, VD)]
                              ).then_inc(head_in[2], 16)
                for p in range(NPG):
                    if p == 1:
                        split_hi(i, 0)
                    if p == 14:
                        split_hi(i, 1)
                    for q4 in (0, 2):
                        act.wait_ge(kt_turned, i * 64 + (4 * p + q4 + 1))
                        act.wait_ge(scored, i * 64 + (4 * p + q4 + 1))
                        act.activation(kt[q4][:, :], m.PS[:, 4, :], ACT.Copy).then_inc(kt_act, 1)
                act.wait_ge(shifted, i * 2 + 2)
                act.activation(pr[:, :], pr[:, :], ACT.Exp, scale=SCALE).then_inc(exp_ready, 1)
                act.activation(prn[:, :], prn[:, :], ACT.Exp, scale=SCALE).then_inc(exp_ready, 1)
                act.wait_ge(z_evac, i * 2 + 1)
                act.activation(ez[:, :], z[0][:, :], ACT.Exp, scale=-1.0).then_inc(z_exp, 1)
                for qb in range(TT):
                    n = (qb + 1) * P
                    act.wait_ge(prompt_maxed, i * 4 + (qb + 1))
                    for c in range(2):
                        act.activation(pp[:, c * SEQ:c * SEQ + n], m.PS[:, 4 + c, 0:n], ACT.Exp, scale=SCALE,
                                       bias=pmx[:, c:c + 1], accum_out=pden[:, c:c + 1]).then_inc(prompt_exp, 1)
                    if qb == 0:
                        act.wait_ge(z_evac, i * 2 + 2)
                        act.wait_ge(z_silu, i * 2 + 1)
                        act.activation(ez[:, :], z[1][:, :], ACT.Exp, scale=-1.0).then_inc(z_exp, 1)
                    act.wait_ge(prompt_turned, i * 4 + (qb + 1))
                    act.activation(pwt[:, :].rearrange("p (b t) -> p b t", b=TT)[:, 0:qb + 1, qb * P:(qb + 1) * P],
                                   m.PS[:, 7, 0:n].rearrange("p (b t) -> p b t", t=P), ACT.Copy).then_inc(prompt_wt, 1)
                act.wait_ge(o_taken, i + 2)
                act.activation(pp[:, :], o[:, :], ACT.Square).then_inc(osq_ready, 1)
                o_scale(i)
            act.wait_ge(out_taken, NSEQ + 1)
            act.activation(pr[:, 0:HC * G * GS], ost[:, :], ACT.Square).then_inc(fin_sq, 1)
            act.wait_ge(fin_sum, 1)
            rsqrt(act, fin_r, 0, m.PS[:, 2, 0:H * G * GS], VD, m, ro[:, 0:H * G * GS])

        @block.vector
        def _(dve):
            per = 30

            def split_lo(i, e):
                dve.wait_ge(hi_ready, i * 2 + (e + 1))
                t = place[("z", e)]
                dve.wait_ge(z_done, i * 2 + (e + 1))
                dve.tensor_tensor(m.WL[e][:, :], slot(("z", e))[:, :], m.WH[e][:, :].bitcast(F32), ALU.subtract).then_inc(lo_ready, 1)
                dve.wait_ge(lo_ready, i * 2 + (e + 1))
                dve.sem_inc(page_free[t % NR], 1)

            def take_z(i, e):
                dve.wait_ge(z_done, i * 2 + (e + 3))
                dve.tensor_tensor(grouped(z[e][:, :]), zps[e], grouped(m.RS[:, :]), ALU.mult).then_inc(z_evac, 1)

            def silu(i, e, chain):
                dve.wait_ge(z_exp, i * 2 + (e + 1))
                chain.link(dve.tensor_scalar(ez[:, :], ez[:, :], 1.0, None, ALU.add))
                chain.link(dve.reciprocal(ez[:, :], ez[:, :]))
                chain.link(dve.tensor_tensor(z[e][:, :], z[e][:, :], ez[:, :], ALU.mult))
                dve.tensor_copy(zst[:, ds(i * (2 * G * GS) + e * G * GS, G * GS)].rearrange("p (g t) -> p g t", g=G),
                                grouped(z[e][:, :])[:, :, GP:GT]).then_inc(z_silu, 1)

            for s in range(NR):
                dve.sem_inc(page_free[s], 1)
            dve.sem_inc(o_taken, 1)
            dve.sem_inc(out_taken, 1)
            dve.wait_ge(const_ready, 2)
            with dve.Fori(0, NSEQ) as i:
                chain = Chain(dve, dve_step, i * per)
                for p in range(NPG):
                    if p == 1:
                        split_lo(i, 0)
                    if p == 15:
                        split_lo(i, 1)
                    for q4 in (1, 3):
                        dve.wait_ge(kt_turned, i * 64 + (4 * p + q4 + 1))
                        dve.wait_ge(scored, i * 64 + (4 * p + q4 + 1))
                        dve.tensor_copy(kt[q4][:, :], m.PS[:, 5, :]).then_inc(kt_dve, 1)
                dve.wait_ge(new_scored, i + 2)
                dve.tensor_reduce(mx[:, :], S.rearrange("p b (g c) -> p c b g", c=HQ), AX.XY, ALU.max).then_inc(max_ready, 1)
                dve.tensor_tensor(prn[:, :].rearrange("p (m q) -> p m q", q=NEW),
                                  m.PS[0:NEW, SMALL, 0:HQ].rearrange("p (m q) -> p m q", q=NEW),
                                  mask_new[:, :].unsqueeze(1).to_broadcast([NEW, HC, NEW]), ALU.add).then_inc(max_ready, 1)
                dve.wait_ge(max_turned, i + 1)
                chain.link(dve.tensor_reduce(mc[:, :], m.PS[0:HQ, SMALL, P:2 * P + NEW], AX.X, ALU.max))
                dve.tensor_scalar(mdiag[:, :], m.IDENT[0:HQ, 0:HQ], mc[:, 0:1], None, ALU.mult).then_inc(diag_ready, 1)
                dve.wait_ge(max_spread, i + 1)
                chain.link(dve.tensor_copy(mb[:, :], m.PS[:, SMALL, 320:320 + HQ]))
                dve.tensor_tensor(pr[:, :].rearrange("p (g c) -> p g c", c=HQ), S.rearrange("p b (g c) -> p (b g) c", c=HQ),
                                  mb[:, :].unsqueeze(1).to_broadcast([P, NPG, HQ]), ALU.subtract).then_inc(shifted, 1)
                dve.tensor_tensor(prn[:, :], prn[:, :], mb[0:NEW, :], ALU.subtract).then_inc(shifted, 1)
                take_z(i, 0)
                dve.wait_ge(exp_ready, i * 2 + 2)
                dve.tensor_reduce(den[:, :], pr[:, :].rearrange("p (g c) -> p c g", c=HQ), AX.X, ALU.add).then_inc(den_ready, 1)
                dve.wait_ge(den_sum, i + 1)
                chain.link(dve.reciprocal(inv[:, :], m.PS[:, SMALL, 384:384 + HQ]))
                inv4 = inv[:, :].rearrange("p (h c q) -> p h c q", h=H, c=2)
                chain.link(dve.tensor_scalar(inv4[:, :, 1, :], inv4[:, :, 1, :], m.NLAM[:, 0:1], None, ALU.mult))
                pr4 = pr[:, :].rearrange("p (g h c q) -> p g h c q", g=NPG, h=H, c=2)
                prn4 = prn[:, :].rearrange("p (h c q) -> p h c q", h=H, c=2)
                w4 = wt[:, :].rearrange("p (g h q) -> p g h q", g=NPG, h=H)
                wn4 = wtn[:, :].rearrange("p (h q) -> p h q", h=H)
                dve.tensor_tensor(w4, pr4[:, :, :, 0, :], inv4[:, :, 0, :].unsqueeze(1).to_broadcast([P, NPG, H, NEW]), ALU.mult)
                dve.tensor_tensor(wn4, prn4[:, :, 0, :], inv4[0:NEW, :, 0, :], ALU.mult)
                dve.tensor_tensor(prn4[:, :, 1, :], prn4[:, :, 1, :], inv4[0:NEW, :, 1, :], ALU.mult)
                chain.link(dve.tensor_tensor(pr4[:, :, :, 1, :], pr4[:, :, :, 1, :],
                                             inv4[:, :, 1, :].unsqueeze(1).to_broadcast([P, NPG, H, NEW]), ALU.mult))
                dve.tensor_tensor(wn4, wn4, prn4[:, :, 1, :], ALU.add)
                dve.tensor_tensor(w4, w4, pr4[:, :, :, 1, :], ALU.add).then_inc(weights_ready, 1)
                silu(i, 0, chain)
                take_z(i, 1)
                for qb in range(TT):
                    n = (qb + 1) * P
                    dve.wait_ge(prompt_scored, i * 4 + (qb + 1))
                    for c in range(2):
                        dg = m.PS[:, 4 + c, qb * P:n]
                        ins = dve.tensor_tensor(dg, dg, mask_diag[:, :], ALU.add)
                    chain.link(ins)
                    chain.link(dve.tensor_reduce(pmx[:, :], m.PS[:, 4:6, 0:n], AX.X, ALU.max))
                    dve.tensor_scalar(pmx[:, :], pmx[:, :], -SCALE, None, ALU.mult).then_inc(prompt_maxed, 1)
                    dve.wait_ge(prompt_exp, i * 8 + (2 * qb + 2))
                    chain.link(dve.reciprocal(pinv[:, :], pden[:, :]))
                    chain.link(dve.tensor_scalar(pp[:, SEQ:SEQ + n], pp[:, SEQ:SEQ + n], pinv[:, 1:2], m.NLAM[:, 0:1],
                                                 ALU.mult, ALU.mult))
                    dve.scalar_tensor_tensor(out=pp[:, 0:n], in0=pp[:, 0:n], scalar=pinv[:, 0:1], in1=pp[:, SEQ:SEQ + n],
                                             op0=ALU.mult, op1=ALU.add).then_inc(prompt_w, 1)
                    if qb == 0:
                        silu(i, 1, chain)
                dve.wait_ge(o_done, i + 2)
                dve.wait_ge(y_stored, i + 1)
                dve.tensor_copy(o[:, :].rearrange("p (e t) -> p e t", e=2), m.PS[:, 0:2, :]).then_inc(o_taken, 1)
                dve.wait_ge(o_ln, i * 2 + 4)
                for e in range(2):
                    oe = o[:, e * SEQ:(e + 1) * SEQ]
                    chain.link(dve.scalar_tensor_tensor(out=oe, in0=oe, scalar=m.GSUB[:, e:e + 1], in1=ro[:, :],
                                                        op0=ALU.mult, op1=ALU.mult))
                    ins = dve.tensor_tensor(oe.rearrange("p (g t) -> p g t", g=G), oe.rearrange("p (g t) -> p g t", g=G),
                                            grouped(z[e][:, :])[:, :, 0:GP], ALU.mult)
                    if e == 0:
                        chain.link(ins)
                    else:
                        ins.then_inc(y_ready, 1)
                dve.wait_ge(out_done, i + 1)
                dve.tensor_copy(ost[:, :].rearrange("p (m t) -> p m t", t=G * GS)[:, :, ds(i * NEW, NEW)],
                                OUT.rearrange("p (m t) -> p m t", t=NEW)).then_inc(out_taken, 1)
                dve.sem_inc(page_free[place[("v", NPG - 1)] % NR], 1)
                assert chain.n == per, chain.n
            tail = Chain(dve, dve_tail)
            dve.wait_ge(fin_r, 2)
            dve.wait_ge(z_silu, 2 * NSEQ)
            o4 = ost[:, :].rearrange("p (h e t) -> p h e t", h=H, e=2)
            z4 = zst[:, :].rearrange("p (h e t) -> p h e t", h=H, e=2)
            y4 = st.YS[:, :].rearrange("p (h e t) -> p h e t", h=H, e=2)
            r3 = ro[:, 0:H * G * GS].rearrange("p (h t) -> p h t", h=H)
            for e in range(2):
                tail.link(dve.scalar_tensor_tensor(out=y4[:, :, e, :], in0=o4[:, :, e, :], scalar=m.GSUB[:, e:e + 1],
                                                   in1=r3, op0=ALU.mult, op1=ALU.mult))
                tail.link(dve.tensor_tensor(y4[:, :, e, :], y4[:, :, e, :], z4[:, :, e, :], ALU.mult))

        @block.tensor
        def _(pe):
            def turn_keys(i, p, q4):
                pe.wait_ge(kt_dve if q4 % 2 else kt_act, i * 32 + (2 * p + q4 // 2 + 1))
                for n in range(4):
                    hc = 4 * q4 + n
                    last = pe.transpose(m.PS[:, 4 + q4 % 2, n * PAGE:(n + 1) * PAGE], slot(("k", p))[:, hc * P:(hc + 1) * P], m.IDENT[:, :])
                last.then_inc(kt_turned, 1)

            def score(i, p, q4):
                pe.wait_ge(kt_dve if q4 % 2 else kt_act, i * 32 + (2 * p + q4 // 2 + 2))
                for n in range(4):
                    hc = 4 * q4 + n
                    last = pe.matmul(m.PS[:, 6 + p // 8, (p % 8) * HQ + hc * NEW:(p % 8) * HQ + (hc + 1) * NEW],
                                     kt[q4][:, n * PAGE:(n + 1) * PAGE], qcur[:, hc * NEW:(hc + 1) * NEW],
                                     start=True, stop=True)
                last.then_inc(scored, 1)

            def z_hi(e, k):
                for x in (m.XH, m.XL):
                    for g in range(G):
                        pe.matmul(zps[e][:, g, :], m.WH[e][:, k * P:(k + 1) * P], x[:, k * T + g * GT:k * T + (g + 1) * GT],
                                  start=(k == 0 and x is m.XH), stop=False, skip_group_check=True)

            def z_lo(e, k):
                for g in range(G):
                    last = pe.matmul(zps[e][:, g, :], m.WL[e][:, k * P:(k + 1) * P], m.XH[:, k * T + g * GT:k * T + (g + 1) * GT],
                                     start=False, stop=(k == KT - 1), skip_group_check=True)
                return last

            def free(t):
                pe.sem_inc(page_free[t % NR], 1)

            pe.sem_inc(z_done, 2)
            pe.sem_inc(kt_act, 1)
            pe.sem_inc(kt_dve, 1)
            pe.sem_inc(scored, 4)
            pe.sem_inc(new_scored, 1)
            pe.sem_inc(o_done, 1)
            with pe.Fori(0, NSEQ) as i:
                pe.wait_ge(cur_ready, i * 2 + 2)
                for p in range(NPG):
                    arrived(pe, i, ("k", p))
                    turn_keys(i, p, 0)
                    turn_keys(i, p, 1)
                    if p == 0:
                        pe.wait_ge(out_taken, i + 1)
                    score(i, p, 0)
                    turn_keys(i, p, 2)
                    score(i, p, 1)
                    turn_keys(i, p, 3)
                    if p == 2:
                        pe.wait_ge(o_taken, i + 1)
                        pe.wait_ge(lo_ready, i * 2 + 1)
                    for k in [(), (), (0, 1), (2, 3)][p] if p < 4 else (p,):
                        z_hi(0, k)
                        last = z_lo(0, k)
                    if p == NPG - 1:
                        last.then_inc(z_done, 1)
                    score(i, p, 2)
                    pe.wait_ge(kt_dve, i * 32 + (2 * p + 3))
                    free(place[("k", p)])
                    score(i, p, 3)
                for hc in range(HC):
                    last = pe.matmul(m.PS[0:NEW, SMALL, hc * NEW:(hc + 1) * NEW], kcur[:, hc * NEW:(hc + 1) * NEW],
                                     qcur[:, hc * NEW:(hc + 1) * NEW], start=True, stop=True)
                last.then_inc(new_scored, 1)
                pe.wait_ge(lo_ready, i * 2 + 2)
                pe.wait_ge(o_ln, i * 2 + 1)
                for k in range(KT):
                    if k == 4:
                        pe.wait_ge(max_ready, i * 2 + 2)
                        pe.sem_inc(wait_taken, 1)
                        pe.transpose(m.PS[0:HQ, SMALL, P:2 * P], mx[:, :], m.IDENT[:, :])
                        pe.transpose(m.PS[0:HQ, SMALL, 2 * P:2 * P + NEW], prn[:, :], m.IDENT[0:NEW, 0:NEW]).then_inc(max_turned, 1)
                    if k == 6:
                        pe.wait_ge(diag_ready, i + 1)
                        pe.matmul(m.PS[:, SMALL, 320:320 + HQ], m.ONES[0:HQ, :], mdiag[:, :], start=True, stop=True).then_inc(max_spread, 1)
                    z_hi(1, k)
                    last = z_lo(1, k)
                last.then_inc(z_done, 1)
                pe.wait_ge(den_ready, i + 1)
                pe.matmul(m.PS[:, SMALL, 384:384 + HQ], m.ONES[:, :], den[:, :], start=True, stop=False)
                pe.matmul(m.PS[:, SMALL, 384:384 + HQ], m.ONES[0:NEW, :], prn[:, :], start=False, stop=True).then_inc(den_sum, 1)
                pe.wait_ge(weights_ready, i + 1)
                arrived(pe, i, ("vn", 0))
                vn = slot(("vn", 0))
                for t in range(HC):
                    last = pe.matmul(OUT[:, t * NEW:(t + 1) * NEW], vn[0:NEW, t * P:(t + 1) * P],
                                     wtn[:, (t // 2) * NEW:(t // 2 + 1) * NEW], start=(t == 0), stop=False, skip_group_check=True)
                last.then_inc(page_free[place[("vn", 0)] % NR], 1)
                for p in range(NPG):
                    arrived(pe, i, ("v", p))
                    vp = slot(("v", p))
                    for t in range(HC):
                        last = pe.matmul(OUT[:, t * NEW:(t + 1) * NEW], vp[:, t * P:(t + 1) * P],
                                         wt[:, p * WQ + (t // 2) * NEW:p * WQ + (t // 2 + 1) * NEW],
                                         start=False, stop=(p == NPG - 1), skip_group_check=True)
                    if p < NPG - 1:
                        last.then_inc(page_free[place[("v", p)] % NR], 1)
                    else:
                        last.then_inc(out_done, 1)
                    qb = p // 3
                    if p % 3 == 0 and qb < TT:
                        if qb == 0:
                            for n in range(3):
                                pe.wait_ge(head_in[n], i * 16 + 16)
                        else:
                            pe.wait_ge(prompt_exp, i * 8 + 2 * qb)
                        for c in range(2):
                            last = pe.matmul(m.PS[:, 4 + c, 0:(qb + 1) * P], qh[:, c * SEQ + qb * P:c * SEQ + (qb + 1) * P],
                                             kh[:, c * SEQ:c * SEQ + (qb + 1) * P], start=True, stop=True)
                        last.then_inc(prompt_scored, 1)
                    if p % 3 == 2 and qb < TT:
                        pe.wait_ge(prompt_w, i * 4 + (qb + 1))
                        if qb:
                            pe.wait_ge(prompt_wt, i * 4 + qb)
                        for kb in range(qb + 1):
                            last = pe.transpose(m.PS[:, 7, kb * P:(kb + 1) * P], pp[:, kb * P:(kb + 1) * P], m.IDENT[:, :])
                        last.then_inc(prompt_turned, 1)
                    if p == 14:
                        pe.wait_ge(osq_ready, i + 1)
                        for e in range(2):
                            last = pe.matmul(m.PS[:, 2, :], m.ONES[:, :], pp[:, e * SEQ:(e + 1) * SEQ],
                                             start=(e == 0), stop=(e == 1))
                        last.then_inc(osq_sum, 1)
                    if p == 12:
                        pe.wait_ge(prompt_wt, i * 4 + 4)
                        for e in range(2):
                            for kb in range(TT):
                                last = pe.matmul(m.PS[:, e, kb * P:SEQ], vh[:, kb * VD + e * P:kb * VD + (e + 1) * P],
                                                 pwt[:, kb * SEQ + kb * P:(kb + 1) * SEQ], start=(kb == 0), stop=(kb == TT - 1),
                                                 skip_group_check=True)
                        last.then_inc(o_done, 1)
            pe.wait_ge(fin_sq, 1)
            for e in range(2):
                last = pe.matmul(m.PS[:, 2, 0:H * G * GS], m.ONES[:, :],
                                 pr[:, 0:HC * G * GS].rearrange("p (h e t) -> p h e t", h=H, e=2)[:, :, e, :],
                                 start=(e == 0), stop=(e == 1))
            last.then_inc(fin_sum, 1)


def project_out(nc, m, d, st):
    with ExitStack() as ctx:
        def sb(name, shape, dt=F32):
            return ctx.enter_context(nc.sbuf_tensor(name, shape, dt))

        def sem(name):
            return new_sem(nc, m, name)
        yh, yl = sb("ay_hi", [P, KT * T], F32R), sb("ay_lo", [P, KT * T], F32R)
        raw = [sb(f"f_raw{s}", [P, D]) for s in range(2)]
        ys = [sb(f"y_in{s}", [P, SEQ]) for s in range(2)]
        x2 = [sb(f"x2_{s}", [P, T]) for s in range(2)]
        rows = sb("x2_rows", [P, TT * P])
        srows = sb("x2_srows", [GS, G * P])
        raw_in = [sem(f"f_raw_in{s}") for s in range(2)]
        y_in = [sem(f"y_in_done{s}") for s in range(2)]
        yh_ready, yl_ready, ys_ready = sem("f_yh_ready"), sem("f_yl_ready"), sem("f_ys_ready")
        hi_ready, lo_ready, block_done, evacuated = sem("f_hi_ready"), sem("f_lo_ready"), sem("f_block_done"), sem("f_evacuated")
        x2_ready, turned, rows_ready, rows_out, granted = (sem("f_x2_ready"), sem("f_turned"), sem("f_rows_ready"),
                                                           sem("f_rows_out"), sem("f_granted"))
        block = ctx.enter_context(nc.Block())
        psum = [m.PS[:, 2 * s:2 * s + 2, :] for s in range(2)]
        out_p = d["y_prompt"].rearrange("o (t p) c -> p (o t) c", p=P)
        out_s = d["y_sample"].rearrange("(g b) t c -> (b t) g c", g=G)

        @block.sync
        def _(sp):
            for s in range(2):
                sp.dma_start(ys[s][:, :], d["y_scratch"][s]).then_inc(y_in[s], 16)
                sp.wait_ge(lo_ready, s + 1)
                sp.dma_start(tiles(raw[s][:, :]), w_block(d["w_out_b"][0], s * P)).then_inc(raw_in[s], 16)
            for k in range(2, KT):
                sp.wait_ge(yl_ready, k - 1)
                sp.dma_start(ys[k % 2][:, :], d["y_scratch"][k]).then_inc(y_in[k % 2], 16)
            with sp.Fori(1, KT // 2) as pair:
                for s in range(2):
                    sp.wait_ge(lo_ready, pair * 2 + (s + 1))
                    sp.sem_inc(granted, 1)
                    sp.dma_start(tiles(raw[s][:, :]), w_block(d["w_out_b"][0], pair * 2 * P + s * P)).then_inc(raw_in[s], 16)

        @block.scalar
        def _(act):
            def split_hi(n, s, use):
                act.wait_ge(raw_in[s], use * 16 + 16)
                act.wait_ge(block_done, n + 1)
                act.activation(m.WH[s][:, :], raw[s][:, :], ACT.Copy).then_inc(hi_ready, 1)

            def store(n):
                act.wait_ge(turned, n + 3)
                act.wait_ge(rows_out, n * 32 + 32)
                act.activation(rows[:, :], m.PS[:, 6, :], ACT.Copy).then_inc(rows_ready, 1)
                act.activation(srows[:, :], m.PS[0:GS, 7, 0:G * P], ACT.Copy).then_inc(rows_ready, 1)
                act.wait_ge(rows_ready, n * 2 + 3)
                act.dma_start(out_p[:, :, ds(n * P, P)], rows[:, :].rearrange("p (t c) -> p t c", t=TT)).then_inc(rows_out, 16)
                act.dma_start(out_s[:, :, ds(n * P, P)], srows[:, :].rearrange("p (g c) -> p g c", g=G)).then_inc(rows_out, 16)

            act.sem_inc(rows_ready, 1)
            act.sem_inc(rows_out, 32)
            split_hi(0, 0, 0)
            for g in range(G):
                act.activation(yh[:, :].rearrange("p (k g t) -> p k g t", k=KT, g=G)[:, :, g, GP:GT],
                               st.YS[:, :].rearrange("p (k g t) -> p k g t", k=KT, g=G)[:, :, g, :], ACT.Copy).then_inc(ys_ready, 1)
            for k in range(KT):
                act.wait_ge(y_in[k % 2], 16 * (k // 2 + 1))
                act.activation(grouped(yh[:, k * T:(k + 1) * T])[:, :, 0:GP], ys[k % 2][:, :].rearrange("p (g t) -> p g t", g=G),
                               ACT.Copy).then_inc(yh_ready, 1)
            split_hi(1, 1, 0)
            with act.Fori(1, KT // 2) as pair:
                for s in range(2):
                    split_hi(pair * 2 + s, s, pair)
                    store(pair * 2 + (s - 2))
            store(KT - 2)
            store(KT - 1)
            act.wait_ge(rows_out, 32 * KT + 32)

        @block.vector
        def _(dve):
            def split_lo(n, s):
                dve.wait_ge(hi_ready, n + 1)
                dve.wait_ge(block_done, n + 1)
                dve.tensor_tensor(m.WL[s][:, :], raw[s][:, :], m.WH[s][:, :].bitcast(F32), ALU.subtract).then_inc(lo_ready, 1)

            def body(n, s):
                if not (isinstance(n, int) and n == KT - 1):
                    split_lo(n + 1, 1 - s)
                xn = ds(n * T, T)
                dve.wait_ge(block_done, n + 3)
                dve.wait_ge(turned, n + 1)
                dve.tensor_tensor(grouped(x2[s][:, :]), psum[s][:, :, 0:GT], grouped(m.XH[:, xn].bitcast(F32)),
                                  ALU.add).then_inc(evacuated, 1)
                dve.wait_ge(evacuated, n + 1)
                dve.tensor_tensor(x2[s][:, :], x2[s][:, :], m.XL[:, xn].bitcast(F32), ALU.add).then_inc(x2_ready, 1)

            dve.sem_inc(lo_ready, 2)
            split_lo(0, 0)
            dve.wait_ge(ys_ready, G)
            for g in range(G):
                v = [a.rearrange("p (k g t) -> p k g t", k=KT, g=G)[:, :, g, GP:GT] for a in (yl[:, :], yh[:, :])]
                dve.tensor_tensor(v[0], st.YS[:, :].rearrange("p (k g t) -> p k g t", k=KT, g=G)[:, :, g, :],
                                  v[1].bitcast(F32), ALU.subtract).then_inc(ys_ready, 1)
            for k in range(KT):
                dve.wait_ge(yh_ready, k + 1)
                yk = slice(k * T, (k + 1) * T)
                dve.tensor_tensor(grouped(yl[:, yk])[:, :, 0:GP], ys[k % 2][:, :].rearrange("p (g t) -> p g t", g=G),
                                  grouped(yh[:, yk].bitcast(F32))[:, :, 0:GP], ALU.subtract).then_inc(yl_ready, 1)
            for n in range(2):
                body(n, n)
            with dve.Fori(1, KT // 2 - 1) as pair:
                for s in range(2):
                    body(pair * 2 + s, s)
            for n in range(KT - 2, KT):
                body(n, n % 2)

        @block.tensor
        def _(pe):
            def turn_tile(n, s):
                pe.wait_ge(x2_ready, n + 1)
                pe.wait_ge(rows_ready, n * 2 + 1)
                for t in range(TT):
                    pe.transpose(m.PS[:, 6, t * P:(t + 1) * P],
                                 x2[s][:, (t // 2) * GT + (t % 2) * P:(t // 2) * GT + (t % 2 + 1) * P], m.IDENT[:, :])
                for g in range(G):
                    last = pe.transpose(m.PS[0:GS, 7, g * P:(g + 1) * P], x2[s][:, g * GT + GP:(g + 1) * GT], m.IDENT[:, :])
                last.then_inc(turned, 1)

            def body(n, s, first=False):
                pe.wait_ge(hi_ready, n + 1)
                if not first:
                    pe.wait_ge(evacuated, n - 1)
                elif n == 0:
                    pe.wait_ge(yl_ready, KT)
                    pe.wait_ge(ys_ready, 2 * G)
                project_hi(pe, m, s, psum[s], yh, yl)
                if not first:
                    turn_tile(n - 2, s)
                pe.wait_ge(lo_ready, n + 3)
                project_lo(pe, m, s, psum[s], yh).then_inc(block_done, 1)

            pe.sem_inc(block_done, 2)
            pe.sem_inc(turned, 2)
            for n in range(2):
                body(n, n, first=True)
            with pe.Fori(1, KT // 2) as pair:
                for s in range(2):
                    body(pair * 2 + s, s)
            turn_tile(KT - 2, 0)
            turn_tile(KT - 1, 1)


def build(nc, d):
    with ExitStack() as ctx:
        m = memory(nc, ctx)
        first = ctx.enter_context(ExitStack())
        m.keep, m.sems = first, []
        with ExitStack() as a:
            st = Bag()
            st.RS2 = a.enter_context(nc.sbuf_tensor("rs_squared", [P, T], F32))
            st.STATE = a.enter_context(nc.sbuf_tensor("state", [P, KT * GS], F32))
            read_inputs(nc, m, d, st)
            st.YH = a.enter_context(nc.sbuf_tensor("y_hi", [P, KT * T], F32R))
            st.YL = a.enter_context(nc.sbuf_tensor("y_lo", [P, KT * T], F32R))
            conv_in(nc, m, d, st)
            conv_out(nc, m, d, st)
        st = Bag()
        st.QS = ctx.enter_context(nc.sbuf_tensor("q_sample", [P, HC * G * GS], F32))
        st.KS = ctx.enter_context(nc.sbuf_tensor("k_sample", [P, HC * G * GS], F32))
        for kind in "qkv":
            project_heads(nc, m, d, st, kind)
        numbers = [s.num for s in m.sems]
        nc.all_engine_barrier(sems_to_clear=range(min(numbers), max(numbers) + 1))
        first.close()
        m.keep = ctx
        with ExitStack() as b:
            st.YS = b.enter_context(nc.sbuf_tensor("y_sample_rows", [P, HC * G * GS], F32))
            st.NR = 5
            attention(nc, m, d, st)
            project_out(nc, m, d, st)


_INS = ['x_prompt', 'x_sample', 'state_conv', 'cache_k', 'cache_v', 'page_table', 'norm_a', 'w_in_a', 'conv_w',
        'w_out_a', 'norm_kv', 'w_kv', 'k_norm', 'norm_b', 'w_in_b', 'q_norm', 'lam', 'subln_w', 'w_out_b']
_OUTS = [('y_prompt', (1, SEQ, D)), ('y_sample', (NSEQ, NEW, D)), ('new_k_prompt', (1, SEQ, H, 2, HD)),
         ('new_v_prompt', (1, SEQ, H, VD)), ('new_conv_prompt', (1, 1, CONV - 1, D)),
         ('new_k_sample', (NSEQ, NEW, H, 2, HD)), ('new_v_sample', (NSEQ, NEW, H, VD)),
         ('new_conv_sample', (1, NSEQ, CONV - 1, D))]


def _rope_tables():
    import numpy as np
    inv = np.float32(THETA) ** (-np.arange(0, ROT, 2, dtype=np.float32) / np.float32(ROT))
    sample = PAST + np.tile(np.arange(NEW), NSEQ // G)
    pos = np.concatenate([np.concatenate([np.arange(g * GP, (g + 1) * GP), sample]) for g in range(G)])
    ang = pos.astype(np.float32)[None, :] * inv[:, None].astype(np.float32)
    c, s = np.cos(ang), np.sin(ang)
    return np.concatenate([c, c]).astype(np.float32), np.concatenate([-s, s]).astype(np.float32)


def kernel(**inputs):
    import numpy as _np
    import concourse.bacc as _bacc
    from concourse import mybir as _mybir
    from concourse.bass_utils import run_bass_kernel_spmd as _run

    nc = _bacc.Bacc("TRN2", target_bir_lowering=False, num_devices=1)
    arrays, d = {}, {}

    def give(name, a):
        arrays[f"in_{name}_dram"] = a
        d[name] = nc.dram_tensor(f"in_{name}_dram", a.shape, _mybir.dt.from_np(a.dtype), kind="ExternalInput").ap()
    for name in _INS:
        give(name, _np.ascontiguousarray(inputs[name]))
    cos, sin = _rope_tables()
    give("rope_cos", cos)
    give("rope_sin", sin)
    for name, shape in _OUTS:
        d[name] = nc.dram_tensor(f"out_{name}_dram", shape, _mybir.dt.float32, kind="ExternalOutput").ap()
    for name in ("q_scratch", "k_scratch", "y_scratch"):
        d[name] = nc.dram_tensor(name, (HC, P, SEQ), _mybir.dt.float32, kind="Internal").ap()
    build(nc, d)
    r = _run(nc, [arrays], core_ids=[0])
    return tuple(r.results[0][f"out_{name}_dram"] for name, _ in _OUTS)
```

```python
import math
from contextlib import ExitStack

import concourse.bass as bass
from concourse import mybir

F32 = mybir.dt.float32
F32R = mybir.dt.float32r
I32 = mybir.dt.int32
ALU = mybir.AluOpType
ACT = mybir.ActivationFunctionType
AX = mybir.AxisListType
ds = bass.ds

P = 128
D = 2048
KT = D // P
SEQ = 512
NSEQ, NEW = 8, 4
CONV = 3
H = 8
HC = 2 * H
HD = 128
VD = 256
PAGE = 128
NPG = 16
PAST = NPG * PAGE
G = 2
GP = SEQ // G
GS = NSEQ * NEW // G
GT = GP + GS
T = G * GT
TT = SEQ // P
ROT = HD // 4
THETA = 500000.0
EPS = 1e-6
LAM_INIT = 0.8 - 0.6 * math.exp(-0.3 * 1)
SCALE = HD ** -0.5
BIG = -3.0e38

GA, GKV, GB, CW, KN_, QN_, SUB, LAM = 0, 16, 32, 48, 96, 97, 98, 100
NPAR = 104

SLOTS = 2


class Bag:
    pass


class Chain:

    def __init__(self, eng, sem, base=0):
        self.eng, self.sem, self.base, self.n = eng, sem, base, 0

    def link(self, ins):
        ins.then_inc(self.sem, 1)
        self.n += 1
        self.eng.wait_ge(self.sem, self.base + self.n)


def new_sem(nc, m, name):
    m.sems.append(m.keep.enter_context(nc.semaphore(name)))
    return m.sems[-1]


def grouped(ap):
    return ap.rearrange("p (g t) -> p g t", g=G)


def w_block(w, col):
    return w.rearrange("(k p) n -> p k n", p=P)[:, :, ds(col, P)]


def tiles(ap):
    return ap.rearrange("p (k n) -> p k n", k=KT)


def project_hi(pe, m, s, out, xh, xl):
    for k in range(KT):
        for x in (xh, xl):
            for g in range(G):
                pe.matmul(out[:, g, 0:GT], m.WH[s][:, k * P:(k + 1) * P], x[:, k * T + g * GT:k * T + (g + 1) * GT],
                          start=(k == 0 and x is xh), stop=False, skip_group_check=True)


def project_lo(pe, m, s, out, xh):
    for k in range(KT):
        for g in range(G):
            last = pe.matmul(out[:, g, 0:GT], m.WL[s][:, k * P:(k + 1) * P], xh[:, k * T + g * GT:k * T + (g + 1) * GT],
                             start=False, stop=(k == KT - 1), skip_group_check=True)
    return last


def rsqrt(act, step, at, total, n, m, out, out_squared=None):
    act.activation(out, total, ACT.Ln, bias=m.EPSC[0:total.shape[0], 0:1], scale=1.0 / n).then_inc(step, 1)
    act.wait_ge(step, at + 1)
    if out_squared is not None:
        act.activation(out_squared, out, ACT.Exp, scale=-1.0).then_inc(step, 1)
    return act.activation(out, out, ACT.Exp, scale=-0.5).then_inc(step, 1)


def weight_memory(nc, m, ctx, name):
    m.WH = [ctx.enter_context(nc.sbuf_tensor(f"{name}_hi{s}", [P, D], F32R)) for s in range(SLOTS)]
    m.WL = [ctx.enter_context(nc.sbuf_tensor(f"{name}_lo{s}", [P, D], F32R)) for s in range(SLOTS)]


def memory(nc, ctx):
    def sb(name, shape, dt=F32):
        return ctx.enter_context(nc.sbuf_tensor(name, shape, dt))
    m = Bag()
    m.PAR = sb("params", [P, NPAR])
    m.IDENT = sb("ident", [P, P])
    m.ONES = sb("ones", [P, P])
    m.EPSC = sb("eps", [P, 1])
    m.RS = sb("rs", [P, T])
    m.NLAM = sb("neg_lambda", [P, 1])
    m.GSUB = sb("subln_gain", [P, 2])
    m.PS = ctx.enter_context(nc.psum_tensor("psum", [P, 8, 512], F32))
    return m


def read_inputs(nc, m, d, st):
    with ExitStack() as ctx:
        def sb(name, shape, dt=F32):
            return ctx.enter_context(nc.sbuf_tensor(name, shape, dt))

        def sem(name):
            return new_sem(nc, m, name)
        xp = sb("xp_rows", [P, TT, D])
        xs = sb("xs_rows", [GS, G, D])
        srow = sb("state_rows", [GS, D])
        prow = sb("param_rows", [NPAR, P])
        sq = [sb(f"x_sq{s}", [P, T]) for s in range(2)]
        acc = sb("x_sq_sum", [P, T])
        lprod = sb("lam_prod", [P, 2])
        lexp = sb("lam_exp", [P, 2])
        par_in, small_in = sem("par_in"), sem("small_in")
        x_in = [sem(f"x_in{c}") for c in range(4)]
        const_ready, par_t, par_ready = sem("const_ready"), sem("par_transposed"), sem("par_ready")
        xt_ready, xh_ready, xl_ready = sem("xt_ready"), sem("xh_ready"), sem("xl_ready")
        sq_ready, sq_used, sum_ready = sem("sq_ready"), sem("sq_used"), sem("sum_ready")
        state_t, lam_ready, lam_sum, lam_exp = sem("state_transposed"), sem("lam_ready"), sem("lam_sum"), sem("lam_exp")
        act_step, pool_step, dve_step = sem("act_step"), sem("pool_step"), sem("dve_step")
        block = ctx.enter_context(nc.Block())

        @block.sync
        def _(sp):
            rows = [(GA, d["norm_a"].rearrange("l (k p) -> (l k) p", p=P), 16),
                    (GKV, d["norm_kv"].rearrange("(k p) -> k p", p=P), 16),
                    (GB, d["norm_b"].rearrange("l (k p) -> (l k) p", p=P), 16),
                    (CW, d["conv_w"].rearrange("l i (k p) -> (l i k) p", p=P), 48),
                    (KN_, d["k_norm"].rearrange("(k p) -> k p", p=P), 1),
                    (QN_, d["q_norm"], 1),
                    (SUB, d["subln_w"].rearrange("l (k p) -> (l k) p", p=P), 2),
                    (LAM, d["lam"].rearrange("l r p -> (l r) p"), 4)]
            sp.dma_start(xs[:, :, :], d["x_sample"].rearrange("(g b) t c -> (b t) g c", g=G)).then_inc(small_in, 16)
            sp.dma_start(srow[:, :], d["state_conv"].rearrange("l b i c -> (l b i) c")).then_inc(small_in, 16)
            x_rows = d["x_prompt"].rearrange("o (t p) c -> p (o t) c", p=P)
            for c in range(4):
                sp.dma_start(xp[:, :, c * 512:(c + 1) * 512], x_rows[:, :, c * 512:(c + 1) * 512]).then_inc(x_in[c], 16)
            for at, src, n in rows:
                sp.dma_start(prow[at:at + n, :], src).then_inc(par_in, 16)

        @block.gpsimd
        def _(pool):
            pool.memset(m.ONES[:, :], 1.0).then_inc(pool_step, 1)
            pool.memset(m.EPSC[:, :], EPS).then_inc(pool_step, 1)
            pool.memset(acc[:, :], 0.0).then_inc(pool_step, 1)
            pool.memset(m.IDENT[:, :], 0.0).then_inc(pool_step, 1)
            pool.wait_ge(pool_step, 4)
            pool.affine_select(out=m.IDENT[:, :], in_=m.IDENT[:, :], compare_op=ALU.not_equal, fill=1.0, base=0,
                               pattern=[[-1, P]], channel_multiplier=1).then_inc(const_ready, 1)
            for k in range(KT):
                pool.wait_ge(sq_ready, k + 1)
                pool.wait_ge(sq_used, k) if k else None
                pool.tensor_tensor(acc[:, :], acc[:, :], sq[k % 2][:, :], ALU.add).then_inc(sq_used, 1)

        @block.scalar
        def _(act):
            for k in range(KT):
                b = 2 * (k % 2)
                xt = m.PS[:, b:b + 2, 0:GT]
                act.wait_ge(xt_ready, k + 1)
                act.activation(grouped(m.XH[:, k * T:(k + 1) * T]), xt, ACT.Copy).then_inc(xh_ready, 1)
                if k >= 2:
                    act.wait_ge(sq_used, k - 1)
                act.activation(grouped(sq[k % 2][:, :]), xt, ACT.Square).then_inc(sq_ready, 1)
            act.wait_ge(lam_sum, 1)
            act.activation(lexp[:, :], m.PS[:, 4, 256:258], ACT.Exp).then_inc(lam_exp, 1)
            act.wait_ge(sum_ready, 1)
            rsqrt(act, act_step, 0, m.PS[:, 6:8, 0:GT], D, m, grouped(m.RS[:, :]), grouped(st.RS2[:, :]))

        @block.vector
        def _(dve):
            for k in range(KT):
                b = 2 * (k % 2)
                xk = slice(k * T, (k + 1) * T)
                dve.wait_ge(sq_ready, k + 1)
                dve.tensor_tensor(grouped(m.XL[:, xk]), m.PS[:, b:b + 2, 0:GT], grouped(m.XH[:, xk].bitcast(F32)),
                                  ALU.subtract).then_inc(xl_ready, 1)
            dve.wait_ge(par_t, 1)
            dve.tensor_copy(m.PAR[:, :], m.PS[:, 4, 0:NPAR]).then_inc(par_ready, 1)
            dve.wait_ge(par_ready, 1)
            dve.tensor_tensor(lprod[:, :], m.PAR[:, LAM:LAM + 4:2], m.PAR[:, LAM + 1:LAM + 4:2],
                              ALU.mult).then_inc(lam_ready, 1)
            dve.tensor_scalar(m.GSUB[:, :], m.PAR[:, SUB:SUB + 2], 1.0 - LAM_INIT, None, ALU.mult).then_inc(dve_step, 1)
            dve.wait_ge(state_t, 1)
            dve.tensor_copy(st.STATE[:, :], m.PS[:, 5, 0:KT * GS]).then_inc(dve_step, 1)
            dve.wait_ge(lam_exp, 1)
            dve.scalar_tensor_tensor(out=m.NLAM[:, :], in0=lexp[:, 1:2], scalar=-LAM_INIT, in1=lexp[:, 0:1],
                                     op0=ALU.add, op1=ALU.subtract).then_inc(dve_step, 1)

        @block.tensor
        def _(pe):
            pe.wait_ge(const_ready, 1)
            pe.wait_ge(small_in, 32)
            for k in range(KT):
                b = 2 * (k % 2)
                if k % 4 == 0:
                    pe.wait_ge(x_in[k // 4], 16)
                if k >= 2:
                    pe.wait_ge(xl_ready, k - 1)
                for t in range(TT):
                    pe.transpose(m.PS[:, b + t // 2, (t % 2) * P:(t % 2 + 1) * P], xp[:, t, k * P:(k + 1) * P], m.IDENT[:, :])
                for g in range(G):
                    last = pe.transpose(m.PS[:, b + g, GP:GT], xs[:, g, k * P:(k + 1) * P], m.IDENT[0:GS, 0:GS])
                last.then_inc(xt_ready, 1)
            pe.wait_ge(par_in, 8 * 16)
            pe.transpose(m.PS[:, 4, 0:NPAR], prow[:, :], m.IDENT[0:NPAR, 0:NPAR]).then_inc(par_t, 1)
            for k in range(KT):
                last = pe.transpose(m.PS[:, 5, k * GS:(k + 1) * GS], srow[:, k * P:(k + 1) * P], m.IDENT[0:GS, 0:GS])
            last.then_inc(state_t, 1)
            pe.wait_ge(lam_ready, 1)
            pe.matmul(m.PS[:, 4, 256:258], m.ONES[:, :], lprod[:, :], start=True, stop=True).then_inc(lam_sum, 1)
            pe.wait_ge(sq_used, KT)
            for g in range(G):
                last = pe.matmul(m.PS[:, 6 + g, 0:GT], m.ONES[:, :], acc[:, g * GT:(g + 1) * GT], start=True, stop=True)
            last.then_inc(sum_ready, 1)


def conv_in(nc, m, d, st):
    cols = [D, 2 * D, 3 * D, 0]
    NB = 4 * KT
    with ExitStack() as ctx:
        def sb(name, shape, dt=F32):
            return ctx.enter_context(nc.sbuf_tensor(name, shape, dt))

        def sem(name):
            return new_sem(nc, m, name)
        raw = [sb(f"a_raw{s}", [P, D]) for s in range(SLOTS)]
        cg = sb("c_gate", [P, T])
        zs = sb("z", [P, T])
        ex = sb("z_exp", [P, T])
        up = sb("u_prompt", [P, CONV - 1 + SEQ])
        us = sb("u_sample", [P, NSEQ, CONV - 1 + NEW])
        lastu = sb("u_last", [P, 2 + NSEQ * 2])
        lastr = sb("u_last_rows", [2 + NSEQ * 2, P])
        raw_in = [sem(f"a_raw_in{s}") for s in range(SLOTS)]
        scaled, hi_ready, lo_ready = sem("a_scaled"), sem("a_hi_ready"), sem("a_lo_ready")
        block_done, evacuated = sem("a_block_done"), sem("a_evacuated")
        e_ready, yh_ready, yl_ready = sem("a_e_ready"), sem("a_yh_ready"), sem("a_yl_ready")
        lu_ready, lu_turned, lr_ready, lr_out = sem("a_lu_ready"), sem("a_lu_turned"), sem("a_lr_ready"), sem("a_lr_out")
        dve_step, granted = sem("a_dve_step"), sem("a_slot_granted")
        block = ctx.enter_context(nc.Block())
        psum = [m.PS[:, 2 * s:2 * s + 2, :] for s in range(SLOTS)]

        @block.sync
        def _(sp):
            with sp.Fori(0, KT) as j:
                for p in range(4):
                    sp.wait_ge(lo_ready, j * 4 + (p + 1))
                    sp.sem_inc(granted, 1)
                    sp.dma_start(tiles(raw[p % 2][:, :]), w_block(d["w_in_a"][0], j * P + cols[p])).then_inc(raw_in[p % 2], 16)

        @block.gpsimd
        def _(pool):
            with pool.Fori(0, KT) as j:
                for p in range(4):
                    pool.wait_ge(raw_in[p % 2], j * 32 + 16 * (p // 2 + 1))
                    pool.tensor_tensor(tiles(raw[p % 2][:, :]), tiles(raw[p % 2][:, :]),
                                       m.PAR[:, GA:GA + KT].unsqueeze(2).to_broadcast([P, KT, P]),
                                       ALU.mult).then_inc(scaled, 1)

        @block.scalar
        def _(act):
            def split_hi(j, p):
                act.wait_ge(scaled, j * 4 + (p + 1))
                act.wait_ge(block_done, j * 4 + (p + 1))
                act.activation(m.WH[p % 2][:, :], raw[p % 2][:, :], ACT.Copy).then_inc(hi_ready, 1)

            def body(j, last=False):
                split_hi(j, 1)
                split_hi(j, 2)
                split_hi(j, 3)
                act.wait_ge(evacuated, j * 4 + (3 + SLOTS))
                act.activation(ex[:, :], zs[:, :], ACT.Exp, scale=-1.0).then_inc(e_ready, 1)
                act.wait_ge(lu_turned, j + 2)
                act.activation(lastr[:, :], m.PS[0:18, 6, 0:P], ACT.Copy).then_inc(lr_ready, 1)
                act.wait_ge(lr_ready, j + 2)
                act.dma_start(d["new_conv_prompt"].rearrange("l o i c -> (l o i) c")[:, ds(j * P, P)],
                              lastr[0:2, :]).then_inc(lr_out, 16)
                act.dma_start(d["new_conv_sample"].rearrange("l b i c -> (l b i) c")[:, ds(j * P, P)],
                              lastr[2:18, :]).then_inc(lr_out, 16)
                if not last:
                    split_hi(j, 4)
                act.wait_ge(evacuated, j * 4 + (4 + SLOTS))
                act.activation(st.YH[:, ds(j * T, T)], zs[:, :], ACT.Copy).then_inc(yh_ready, 1)
                act.wait_ge(lr_out, j * 32 + 32)
            act.sem_inc(lr_ready, 1)
            split_hi(0, 0)
            with act.Fori(0, KT - 1) as j:
                body(j)
            body(KT - 1, last=True)

        @block.vector
        def _(dve):
            dve.sem_inc(lo_ready, SLOTS)
            dve.sem_inc(evacuated, SLOTS)
            dve.sem_inc(yl_ready, 1)
            dve.memset(up[:, 0:2], 0.0).then_inc(dve_step, 1)
            dve.wait_ge(dve_step, 1)
            per = 18

            def split_lo(j, p):
                dve.wait_ge(hi_ready, j * 4 + (p + 1))
                dve.wait_ge(block_done, j * 4 + (p + 1))
                dve.tensor_tensor(m.WL[p % 2][:, :], raw[p % 2][:, :], m.WH[p % 2][:, :].bitcast(F32),
                                  ALU.subtract).then_inc(lo_ready, 1)

            def body(j, last=False):
                chain = Chain(dve, dve_step, j * per + 1)
                split_lo(j, 1)
                dve.wait_ge(block_done, j * 4 + (1 + SLOTS))
                dve.tensor_tensor(grouped(cg[:, :]), psum[0][:, :, 0:GT], grouped(st.RS2[:, :]), ALU.mult).then_inc(evacuated, 1)
                split_lo(j, 2)
                chain.link(dve.tensor_copy(us[:, :, 0:2], st.STATE[:, ds(j * GS, GS)].rearrange("p (b i) -> p b i", i=2)))
                dve.wait_ge(block_done, j * 4 + (2 + SLOTS))
                dve.wait_ge(evacuated, j * 4 + (1 + SLOTS))
                chain.link(dve.tensor_tensor(up[:, 2:2 + SEQ].rearrange("p (g t) -> p g t", g=G), psum[1][:, :, 0:GP],
                                             grouped(cg[:, :])[:, :, 0:GP], ALU.mult))
                for g in range(G):
                    ins = dve.tensor_tensor(us[:, 4 * g:4 * g + 4, 2:6],
                                            psum[1][:, g, GP:GT].rearrange("p (b t) -> p b t", t=NEW),
                                            cg[:, g * GT + GP:(g + 1) * GT].rearrange("p (b t) -> p b t", t=NEW), ALU.mult)
                    if g == 0:
                        chain.link(ins)
                    else:
                        ins.then_inc(evacuated, 1)
                dve.wait_ge(evacuated, j * 4 + (2 + SLOTS))
                split_lo(j, 3)
                dve.wait_ge(lu_turned, j + 1)
                chain.link(dve.tensor_copy(lastu[:, 0:2], up[:, SEQ:SEQ + 2]))
                dve.tensor_copy(lastu[:, 2:18].rearrange("p (b i) -> p b i", i=2), us[:, :, 4:6]).then_inc(lu_ready, 1)
                tap = [m.PAR[:, ds(j + (CW + KT * i), 1)] for i in range(CONV)]
                cvp = grouped(cg[:, :])[:, :, 0:GP]
                chain.link(dve.tensor_scalar(cvp, up[:, 2:2 + SEQ].rearrange("p (g t) -> p g t", g=G), tap[2], None, ALU.mult))
                for i in (1, 0):
                    chain.link(dve.scalar_tensor_tensor(out=cvp, in0=up[:, i:i + SEQ].rearrange("p (g t) -> p g t", g=G),
                                                        scalar=tap[i], in1=cvp, op0=ALU.mult, op1=ALU.add))
                for g in range(G):
                    cvs = cg[:, g * GT + GP:(g + 1) * GT].rearrange("p (b t) -> p b t", t=NEW)
                    ub = us[:, 4 * g:4 * g + 4, :]
                    chain.link(dve.tensor_scalar(cvs, ub[:, :, 2:6], tap[2], None, ALU.mult))
                    for i in (1, 0):
                        chain.link(dve.scalar_tensor_tensor(out=cvs, in0=ub[:, :, i:i + 4], scalar=tap[i], in1=cvs,
                                                            op0=ALU.mult, op1=ALU.add))
                dve.wait_ge(block_done, j * 4 + (3 + SLOTS))
                dve.wait_ge(yl_ready, j + 1)
                dve.tensor_tensor(grouped(zs[:, :]), psum[0][:, :, 0:GT], grouped(m.RS[:, :]), ALU.mult).then_inc(evacuated, 1)
                if not last:
                    split_lo(j, 4)
                dve.wait_ge(e_ready, j + 1)
                chain.link(dve.tensor_scalar(ex[:, :], ex[:, :], 1.0, None, ALU.add))
                chain.link(dve.reciprocal(ex[:, :], ex[:, :]))
                chain.link(dve.tensor_tensor(ex[:, :], ex[:, :], zs[:, :], ALU.mult))
                chain.link(dve.tensor_tensor(cg[:, :], cg[:, :], ex[:, :], ALU.mult))
                chain.link(dve.tensor_tensor(cg[:, :], cg[:, :], m.RS[:, :], ALU.mult))
                assert chain.n == per
                dve.wait_ge(block_done, j * 4 + (4 + SLOTS))
                dve.tensor_tensor(grouped(zs[:, :]), psum[1][:, :, 0:GT], grouped(cg[:, :]), ALU.mult).then_inc(evacuated, 1)
                dve.wait_ge(yh_ready, j + 1)
                dve.tensor_tensor(st.YL[:, ds(j * T, T)], zs[:, :], st.YH[:, ds(j * T, T)].bitcast(F32),
                                  ALU.subtract).then_inc(yl_ready, 1)
            split_lo(0, 0)
            with dve.Fori(0, KT - 1) as j:
                body(j)
            body(KT - 1, last=True)

        @block.tensor
        def _(pe):
            pe.sem_inc(block_done, SLOTS)
            pe.sem_inc(lu_turned, 1)
            with pe.Fori(0, KT) as j:
                for p in range(4):
                    pe.wait_ge(hi_ready, j * 4 + (p + 1))
                    pe.wait_ge(evacuated, j * 4 + (p + 1))
                    project_hi(pe, m, p % 2, psum[p % 2], m.XH, m.XL)
                    pe.wait_ge(lo_ready, j * 4 + (p + 1 + SLOTS))
                    project_lo(pe, m, p % 2, psum[p % 2], m.XH).then_inc(block_done, 1)
                    if p == 2:
                        pe.wait_ge(lu_ready, j + 1)
                        pe.wait_ge(lr_ready, j + 1)
                        pe.transpose(m.PS[0:18, 6, 0:P], lastu[:, :], m.IDENT[:, :]).then_inc(lu_turned, 1)


def conv_out(nc, m, d, st):
    with ExitStack() as ctx:
        def sb(name, shape, dt=F32):
            return ctx.enter_context(nc.sbuf_tensor(name, shape, dt))

        def sem(name):
            return new_sem(nc, m, name)
        raw = [sb(f"o_raw{s}", [P, D]) for s in range(SLOTS)]
        x1 = [sb(f"x1_{s}", [P, T]) for s in range(2)]
        x1_out = [sem(f"o_x1_out{s}") for s in range(2)]
        sq = sb("x1_sq", [P, T])
        acc = sb("x1_sq_sum", [P, T])
        raw_in = [sem(f"o_raw_in{s}") for s in range(SLOTS)]
        hi_ready, lo_ready, block_done, evacuated = sem("o_hi_ready"), sem("o_lo_ready"), sem("o_block_done"), sem("o_evacuated")
        x1_ready, x1_split, xh_ready, sq_ready, sq_used = (sem("o_x1_ready"), sem("o_x1_split"), sem("o_xh_ready"),
                                                           sem("o_sq_ready"), sem("o_sq_used"))
        sum_ready, act_step = sem("o_sum_ready"), sem("o_act_step")
        granted = sem("o_slot_granted")
        block = ctx.enter_context(nc.Block())
        psum = [m.PS[:, 2 * s:2 * s + 2, :] for s in range(SLOTS)]

        @block.sync
        def _(sp):
            with sp.Fori(0, KT // 2) as pair:
                j = pair * 2
                for s in range(2):
                    sp.wait_ge(lo_ready, j + (s + 1))
                    sp.sem_inc(granted, 1)
                    sp.dma_start(tiles(raw[s][:, :]), w_block(d["w_out_a"][0], j * P + s * P)).then_inc(raw_in[s], 16)

        @block.gpsimd
        def _(pool):
            pool.memset(acc[:, :], 0.0).then_inc(sq_used, 1)
            with pool.Fori(0, KT) as j:
                pool.wait_ge(sq_ready, j + 2)
                pool.wait_ge(sq_used, j + 1)
                pool.tensor_tensor(acc[:, :], acc[:, :], sq[:, :], ALU.add).then_inc(sq_used, 1)

        @block.scalar
        def _(act):
            def split_hi(j, s):
                act.wait_ge(raw_in[s % 2], j * 8 + 16 * (s // 2 + 1))
                act.wait_ge(block_done, j + (s + 1))
                act.activation(m.WH[s % 2][:, :], raw[s % 2][:, :], ACT.Copy).then_inc(hi_ready, 1)

            def body(j, last=False):
                for s in range(2):
                    if not (last and s == 1):
                        split_hi(j, s + 1)
                    act.wait_ge(x1_ready, j + (s + 1))
                    act.activation(m.XH[:, ds((j + s) * T, T)], x1[s][:, :], ACT.Copy).then_inc(xh_ready, 1)
                    act.dma_start(d["x_scratch"].rearrange("m p t -> p m t")[:, ds(j + s, 1), :].rearrange("p m t -> p (m t)"),
                                  x1[s][:, :]).then_inc(x1_out[s], 16)
                    act.wait_ge(sq_used, j + (s + 1))
                    act.activation(sq[:, :], x1[s][:, :], ACT.Square).then_inc(sq_ready, 1)
            act.sem_inc(sq_ready, 1)
            for s in range(2):
                act.sem_inc(x1_out[s], 16)
            split_hi(0, 0)
            with act.Fori(0, KT // 2 - 1) as pair:
                body(pair * 2)
            body(KT - 2, last=True)
            act.wait_ge(sum_ready, 1)
            rsqrt(act, act_step, 0, m.PS[:, 6:8, 0:GT], D, m, grouped(m.RS[:, :]))
            for s in range(2):
                act.wait_ge(x1_out[s], 16 * (KT // 2 + 1))

        @block.vector
        def _(dve):
            dve.sem_inc(lo_ready, SLOTS)
            dve.sem_inc(x1_split, 1)

            def split_lo(j, s):
                dve.wait_ge(hi_ready, j + (s + 1))
                dve.wait_ge(block_done, j + (s + 1))
                dve.tensor_tensor(m.WL[s % 2][:, :], raw[s % 2][:, :], m.WH[s % 2][:, :].bitcast(F32),
                                  ALU.subtract).then_inc(lo_ready, 1)

            def body(j, last=False):
                for s in range(2):
                    if not (last and s == 1):
                        split_lo(j, s + 1)
                    xj = ds((j + s) * T, T)
                    dve.wait_ge(block_done, j + (s + 1 + SLOTS))
                    dve.wait_ge(x1_split, j + (s + 1))
                    dve.wait_ge(sq_ready, j + (s + 1))
                    dve.wait_ge(x1_out[s], j * 8 + 16)
                    dve.tensor_tensor(grouped(x1[s][:, :]), psum[s][:, :, 0:GT], grouped(m.XH[:, xj].bitcast(F32)),
                                      ALU.add).then_inc(evacuated, 1)
                    dve.wait_ge(evacuated, j + (s + 1))
                    dve.tensor_tensor(x1[s][:, :], x1[s][:, :], m.XL[:, xj].bitcast(F32), ALU.add).then_inc(x1_ready, 1)
                    dve.wait_ge(xh_ready, j + (s + 1))
                    dve.tensor_tensor(m.XL[:, xj], x1[s][:, :], m.XH[:, xj].bitcast(F32), ALU.subtract).then_inc(x1_split, 1)
            split_lo(0, 0)
            with dve.Fori(0, KT // 2 - 1) as pair:
                body(pair * 2)
            body(KT - 2, last=True)

        @block.tensor
        def _(pe):
            pe.sem_inc(block_done, SLOTS)
            def one(j, s, wait):
                pe.wait_ge(hi_ready, j + (s + 1))
                if wait:
                    pe.wait_ge(evacuated, j + (s - 1))
                project_hi(pe, m, s, psum[s], st.YH, st.YL)
                pe.wait_ge(lo_ready, j + (s + 1 + SLOTS))
                project_lo(pe, m, s, psum[s], st.YH).then_inc(block_done, 1)
            for s in range(2):
                one(0, s, False)
            with pe.Fori(1, KT // 2) as pair:
                for s in range(2):
                    one(pair * 2, s, True)
            pe.wait_ge(sq_used, KT + 1)
            for g in range(G):
                last = pe.matmul(m.PS[:, 6 + g, 0:GT], m.ONES[:, :], acc[:, g * GT:(g + 1) * GT], start=True, stop=True)
            last.then_inc(sum_ready, 1)


def project_heads(nc, m, d, st, kind):
    w, col0, gain = {"q": (d["w_in_b"][0], 0, GB), "k": (d["w_kv"], 0, GKV), "v": (d["w_kv"], D, GKV), "z": (d["w_in_b"][0], D, GB)}[kind]
    norm, turn, silu = kind in "qk", kind in "kv", kind == "z"
    ngain = {"q": QN_, "k": KN_}.get(kind)
    scratch = {"q": d["q_scratch"], "k": d["k_scratch"], "z": d["z_scratch"]}.get(kind)
    keep = {"q": st.QS, "k": st.KS, "z": st.ZS}.get(kind)
    with ExitStack() as ctx:
        def sb(name, shape, dt=F32):
            return ctx.enter_context(nc.sbuf_tensor(f"{kind}_{name}", shape, dt))

        def sem(name):
            return new_sem(nc, m, f"{kind}_{name}")
        raw = [sb(f"raw{s}", [P, D]) for s in range(2)]
        plain = [sb(f"plain{s}", [P, T]) for s in range(2)]
        sq = sb("sq", [P, T])
        r = [sb(f"r{s}", [P, T]) for s in range(2)]
        tile = [sb(f"tile{s}", [P, T]) for s in range(2)]
        swap = sb("swap", [ROT, T])
        cos, sin = sb("cos", [ROT, T]), sb("sin", [ROT, T])
        rows = [sb(f"rows{s}", [P, TT * P]) for s in range(2)]
        srows = [sb(f"srows{s}", [GS, G * P]) for s in range(2)]
        raw_in = [sem(f"raw_in{s}") for s in range(2)]
        tables_in = sem("tables_in")
        scaled, hi_ready, lo_ready = sem("scaled"), sem("hi_ready"), sem("lo_ready")
        block_done, evacuated = sem("block_done"), sem("evacuated")
        sq_ready, summed, ln_step, tile_ready = sem("sq_ready"), sem("summed"), sem("ln_step"), sem("tile_ready")
        turned, rows_ready, granted, dve_step = sem("turned"), sem("rows_ready"), sem("granted"), sem("dve_step")
        scratch_out = [sem(f"scratch_out{s}") for s in range(2)]
        rows_out = [sem(f"rows_out{s}") for s in range(2)]
        block = ctx.enter_context(nc.Block())
        psum = [m.PS[:, 2 * s:2 * s + 2, :] for s in range(2)]
        N = KT

        @block.sync
        def _(sp):
            if norm:
                sp.dma_start(cos[:, :], d["rope_cos"]).then_inc(tables_in, 16)
                sp.dma_start(sin[:, :], d["rope_sin"]).then_inc(tables_in, 16)
            with sp.Fori(0, N // 2) as pair:
                for s in range(2):
                    sp.wait_ge(lo_ready, pair * 2 + (s + 1))
                    sp.sem_inc(granted, 1)
                    sp.dma_start(tiles(raw[s][:, :]), w_block(w, pair * 2 * P + (s * P + col0))).then_inc(raw_in[s], 16)

        @block.gpsimd
        def _(pool):
            with pool.Fori(0, N // 2) as pair:
                for s in range(2):
                    pool.wait_ge(raw_in[s], pair * 16 + 16)
                    pool.tensor_tensor(tiles(raw[s][:, :]), tiles(raw[s][:, :]),
                                       m.PAR[:, gain:gain + KT].unsqueeze(2).to_broadcast([P, KT, P]),
                                       ALU.mult).then_inc(scaled, 1)

        @block.scalar
        def _(act):
            out_p = {"k": d["new_k_prompt"].rearrange("o (t p) h c d -> p (o t) (h c d)", p=P),
                     "v": d["new_v_prompt"].rearrange("o (t p) h e -> p (o t) (h e)", p=P)}.get(kind)
            out_s = {"k": d["new_k_sample"].rearrange("(g b) t h c d -> (b t) g (h c d)", g=G),
                     "v": d["new_v_sample"].rearrange("(g b) t h e -> (b t) g (h e)", g=G)}.get(kind)

            def split_hi(n, s):
                act.wait_ge(scaled, n + 1)
                act.wait_ge(block_done, n + 1)
                act.activation(m.WH[s][:, :], raw[s][:, :], ACT.Copy).then_inc(hi_ready, 1)

            def store_tile(n, s):
                if scratch is not None:
                    act.wait_ge(tile_ready, n + 3)
                    act.dma_start(scratch.rearrange("m p t -> p m t")[:, ds(n, 1), :].rearrange("p m (g t) -> p (m g) t", g=G),
                                  grouped(tile[s][:, :])[:, :, 0:GP]).then_inc(scratch_out[s], 16)

            def store_rows(n, s, slot_uses):
                if turn:
                    act.wait_ge(turned, n + 3)
                    act.wait_ge(rows_out[s], slot_uses * 32 + 32)
                    act.activation(rows[s][:, :], m.PS[:, 6, :], ACT.Copy).then_inc(rows_ready, 1)
                    act.activation(srows[s][:, :], m.PS[0:GS, 7, 0:G * P], ACT.Copy).then_inc(rows_ready, 1)
                    act.wait_ge(rows_ready, n * 2 + 3)
                    act.dma_start(out_p[:, :, ds(n * P, P)], rows[s][:, :].rearrange("p (t c) -> p t c", t=TT)).then_inc(rows_out[s], 16)
                    act.dma_start(out_s[:, :, ds(n * P, P)], srows[s][:, :].rearrange("p (g c) -> p g c", g=G)).then_inc(rows_out[s], 16)

            def norm_scale(n, s):
                if norm:
                    act.wait_ge(summed, n + 1)
                    act.wait_ge(tile_ready, n + 1)
                    rsqrt(act, ln_step, n * 2, m.PS[:, 4:6, 0:GT], HD, m, grouped(r[s][:, :]))

            def square(n, s):
                if norm:
                    act.wait_ge(evacuated, n + 3)
                    act.activation(sq[:, :], plain[s][:, :], ACT.Square).then_inc(sq_ready, 1)
                if silu:
                    act.wait_ge(evacuated, n + 3)
                    act.activation(r[s][:, :], plain[s][:, :], ACT.Exp, scale=-1.0).then_inc(ln_step, 2)

            def body(n, s):
                if isinstance(n, int) and n == N - 1:
                    pass
                else:
                    split_hi(n + 1, 1 - s)
                if not isinstance(n, int) or n >= 2:
                    store_tile(n - 2, s)
                    half = (pair_of(n, s) - 1)
                    store_rows(n - 2, s, half)
                if not isinstance(n, int) or n >= 1:
                    norm_scale(n - 1, 1 - s)
                square(n, s)

            act.sem_inc(rows_ready, 1)
            for s in range(2):
                act.sem_inc(scratch_out[s], 16)
                act.sem_inc(rows_out[s], 32)
            split_hi(0, 0)
            pairs = {}

            def pair_of(n, s):
                return n // 2 if isinstance(n, int) else pairs["at"]
            for n in range(2):
                body(n, n)
            with act.Fori(1, N // 2 - 1) as pair:
                pairs["at"] = pair
                for s in range(2):
                    body(pair * 2 + s, s)
            for n in range(N - 2, N):
                body(n, n % 2)
            norm_scale(N - 1, 1)
            for n in range(N - 2, N):
                store_tile(n, n % 2)
                store_rows(n, n % 2, n // 2)
            for s in range(2):
                act.wait_ge(scratch_out[s], 16 * (N // 2 + 1) if scratch is not None else 16)
                act.wait_ge(rows_out[s], 32 * (N // 2 + 1) if turn else 32)

        @block.vector
        def _(dve):
            per = 5

            def split_lo(n, s):
                dve.wait_ge(hi_ready, n + 1)
                dve.wait_ge(block_done, n + 1)
                dve.tensor_tensor(m.WL[s][:, :], raw[s][:, :], m.WH[s][:, :].bitcast(F32), ALU.subtract).then_inc(lo_ready, 1)

            def finish(n, s, uses):
                chain = Chain(dve, dve_step, n * (3 if silu else per))
                t, t32 = tile[s], tile[s][0:ROT, :]
                dve.wait_ge(ln_step, n * 2 + 2)
                dve.wait_ge(scratch_out[s], uses * 16 + 16)
                if turn:
                    dve.wait_ge(turned, n + 1)
                if silu:
                    chain.link(dve.tensor_scalar(r[s][:, :], r[s][:, :], 1.0, None, ALU.add))
                    chain.link(dve.reciprocal(r[s][:, :], r[s][:, :]))
                    chain.link(dve.tensor_tensor(t[:, :], plain[s][:, :], r[s][:, :], ALU.mult))
                    dve.tensor_copy(keep[:, ds(n * G * GS, G * GS)].rearrange("p (g t) -> p g t", g=G),
                                    grouped(t[:, :])[:, :, GP:GT]).then_inc(tile_ready, 1)
                    return
                chain.link(dve.scalar_tensor_tensor(out=t[:, :], in0=plain[s][:, :], scalar=m.PAR[:, ngain:ngain + 1],
                                                    in1=r[s][:, :], op0=ALU.mult, op1=ALU.mult))
                half = ROT // 2
                dve.sem_inc(granted, 1)
                chain.link(dve.stream_shuffle(swap[:, :], t32, [(i + half) % ROT for i in range(ROT)]))
                chain.link(dve.tensor_tensor(swap[:, :], swap[:, :], sin[:, :], ALU.mult))
                chain.link(dve.tensor_tensor(t32, t32, cos[:, :], ALU.mult))
                chain.link(dve.tensor_tensor(t32, t32, swap[:, :], ALU.add))
                dve.tensor_copy(keep[:, ds(n * G * GS, G * GS)].rearrange("p (g t) -> p g t", g=G),
                                grouped(t[:, :])[:, :, GP:GT]).then_inc(tile_ready, 1)
                assert chain.n == per

            def body(n, s, uses):
                if not (isinstance(n, int) and n == N - 1):
                    split_lo(n + 1, 1 - s)
                dve.wait_ge(block_done, n + 3)
                if norm or silu:
                    dve.tensor_tensor(grouped(plain[s][:, :]), psum[s][:, :, 0:GT], grouped(m.RS[:, :]), ALU.mult).then_inc(evacuated, 1)
                    if not isinstance(n, int) or n >= 1:
                        finish(n - 1, 1 - s, uses if s else uses - 1)
                else:
                    dve.wait_ge(turned, n + 1)
                    dve.tensor_tensor(grouped(tile[s][:, :]), psum[s][:, :, 0:GT], grouped(m.RS[:, :]), ALU.mult).then_inc(evacuated, 1)

            dve.sem_inc(lo_ready, 2)
            dve.sem_inc(evacuated, 2)
            dve.sem_inc(tile_ready, 2)
            if norm:
                dve.wait_ge(tables_in, 32)
            split_lo(0, 0)
            for n in range(2):
                body(n, n, 0)
            with dve.Fori(1, N // 2 - 1) as pair:
                for s in range(2):
                    body(pair * 2 + s, s, pair)
            for n in range(N - 2, N):
                body(n, n % 2, N // 2 - 1)
            if norm or silu:
                finish(N - 1, 1, N // 2 - 1)

        @block.tensor
        def _(pe):
            def turn_tile(n, s):
                if turn:
                    pe.wait_ge(tile_ready if norm else evacuated, n + 3)
                    pe.wait_ge(rows_ready, n * 2 + 1)
                    for t in range(TT):
                        pe.transpose(m.PS[:, 6, t * P:(t + 1) * P],
                                     tile[s][:, (t // 2) * GT + (t % 2) * P:(t // 2) * GT + (t % 2 + 1) * P], m.IDENT[:, :])
                    for g in range(G):
                        last = pe.transpose(m.PS[0:GS, 7, g * P:(g + 1) * P], tile[s][:, g * GT + GP:(g + 1) * GT], m.IDENT[:, :])
                    last.then_inc(turned, 1)

            def sum_squares(n):
                if norm:
                    pe.wait_ge(sq_ready, n + 1)
                    if not isinstance(n, int) or n >= 1:
                        pe.wait_ge(ln_step, n * 2)
                    for g in range(G):
                        last = pe.matmul(m.PS[:, 4 + g, 0:GT], m.ONES[:, :], sq[:, g * GT:(g + 1) * GT], start=True, stop=True)
                    last.then_inc(summed, 1)

            def body(n, s):
                pe.wait_ge(hi_ready, n + 1)
                pe.wait_ge(evacuated, n + 1)
                project_hi(pe, m, s, psum[s], m.XH, m.XL)
                if not isinstance(n, int) or n >= 2:
                    turn_tile(n - 2, s)
                if not isinstance(n, int) or n >= 1:
                    sum_squares(n - 1)
                pe.wait_ge(lo_ready, n + 3)
                project_lo(pe, m, s, psum[s], m.XH).then_inc(block_done, 1)

            pe.sem_inc(block_done, 2)
            pe.sem_inc(turned, 2)
            for n in range(2):
                body(n, n)
            with pe.Fori(1, N // 2) as pair:
                for s in range(2):
                    body(pair * 2 + s, s)
            turn_tile(N - 2, 0)
            sum_squares(N - 1)
            turn_tile(N - 1, 1)


def attention(nc, m, d, st):
    items = [("k", p) for p in range(NPG)] + [("v", p) for p in range(NPG + 1)]
    NR = st.NR
    NV = NPG + 1
    last_in = {t % NR: it for t, it in enumerate(items)}
    HQ = HC * NEW
    WQ = H * NEW
    B = 32
    NB = P // B
    NCH = D // B
    GRP = 2
    with ExitStack() as ctx:
        def sb(name, shape, dt=F32):
            return ctx.enter_context(nc.sbuf_tensor(name, shape, dt))

        def sem(name):
            return new_sem(nc, m, name)
        ring = [sb(f"ring{s}", [P, D]) for s in range(NR)]
        ktg = [sb(f"keys_turned{g}", [P, GRP * D]) for g in range(2)]
        vh_ = [sb(f"value_hi{s}", [P, D], F32R) for s in range(2)]
        vl_ = [sb(f"value_lo{s}", [P, D], F32R) for s in range(2)]
        qblk = sb("q_blocks", [P, NCH * B])
        sct = [sb(f"scores_turned{n}", [P, 2 * GRP * NB * B]) for n in range(2)]
        pr = sb("probs", [P, NPG * HQ])
        wt = sb("weights", [P, NPG * WQ])
        wst = sb("weights_hi_lo", [P, NPG * 2 * WQ], F32R)
        wstn = sb("weights_new_hi_lo", [NEW, 2 * WQ], F32R)
        qcur, kcur = sb("q_cur", [P, HQ]), sb("k_cur", [P, HQ])
        prn = sb("probs_new", [NEW, HQ])
        wtn = sb("weights_new", [NEW, WQ])
        mx, mc, mdiag, mb = sb("max_part", [P, HQ]), sb("max_col", [HQ, 1]), sb("max_diag", [HQ, HQ]), sb("max_row", [P, HQ])
        den, inv = sb("denom", [P, HQ]), sb("inv_denom", [P, HQ])
        mask_new, mask_diag = sb("mask_new", [NEW, NEW]), sb("mask_diag", [P, P])
        pages = sb("page_ids", [1, NSEQ * NPG], I32)
        qh, kh, vh = sb("q_head", [P, 2 * SEQ]), sb("k_head", [P, 2 * SEQ]), sb("v_head", [P, TT * VD])
        zh = sb("z_head", [P, 2 * SEQ])
        pp = sb("prompt_probs", [P, 2 * SEQ])
        pmx, pden, pinv = sb("prompt_max", [P, 2]), sb("prompt_denom", [P, 2]), sb("prompt_inv", [P, 2])
        pwt = sb("prompt_weights_t", [P, TT * SEQ])
        o = sb("o_head", [P, 2 * SEQ])
        ro = sb("o_rms", [P, SEQ])
        orow = sb("o_rows", [WQ, D])
        ost = sb("o_sample", [P, HC * G * GS])

        page_in = [sem(f"page_in{s}") for s in range(NR)]
        ids_in, granted = sem("ids_in"), sem("b_granted")
        const_ready, const_step = sem("const2_ready"), sem("const2_step")
        cur_ready, qblk_ready = sem("cur_ready"), sem("qblk_ready")
        kt_ready, group_scored, sct_ready = sem("kt_ready"), sem("group_scored"), sem("sct_ready")
        moved_act, moved_dve = sem("moved_act"), sem("moved_dve")
        new_scored, max_ready, max_turned, diag_ready, max_spread = (sem("new_scored"), sem("max_ready"), sem("max_turned"),
                                                                     sem("diag_ready"), sem("max_spread"))
        shifted, exp_ready, den_ready, den_sum, wt_ready, whi_ready, weights_ready = (
            sem("shifted"), sem("exp_ready"), sem("den_ready"), sem("den_sum"), sem("wt_ready"), sem("whi_ready"),
            sem("weights_ready"))
        v_hi, v_lo, v_used = sem("v_hi"), sem("v_lo"), sem("v_used")
        olo_ready, orow_ready, o_turned, out_taken = sem("olo_ready"), sem("orow_ready"), sem("o_turned"), sem("out_taken")
        head_in = [sem(f"head_in{n}") for n in range(4)]
        prompt_scored, prompt_maxed, prompt_exp, prompt_w = (sem("prompt_scored"), sem("prompt_maxed"), sem("prompt_exp"),
                                                             sem("prompt_w"))
        prompt_turned, prompt_wt, o_done, o_taken = sem("prompt_turned"), sem("prompt_wt"), sem("o_done"), sem("o_taken")
        osq_ready, osq_sum, o_ln, y_ready, y_out = sem("osq_ready"), sem("osq_sum"), sem("o_ln"), sem("y_ready"), sem("y_out")
        dve_step, dve_tail, y_stored = sem("b_dve_step"), sem("b_dve_tail"), sem("y_stored")
        wait_taken = sem("wait_taken")
        fin_sq, fin_sum, fin_r = sem("fin_sq"), sem("fin_sum"), sem("fin_r")
        block = ctx.enter_context(nc.Block())

        KEYS = [0, 1]
        SMALL = 1
        PWT = 0
        OUT = m.PS[:, 2:6, :]
        PSC = 6

        def arrived(eng, i, t):
            n = len(range(t % NR, len(items), NR))
            eng.wait_ge(page_in[t % NR], i * (16 * n) + 16 * (t // NR + 1))

        def chunks(tile):
            return tile[:, :].rearrange("p (g c j) -> p g c j", g=GRP, c=NCH)

        def move_scores(eng, i, quad, b, signal, last_signal, link):
            for a in range(4):
                src = sct[quad % 2][a * B:(a + 1) * B, :].rearrange("p (g n s r) -> p n g s r", g=2, n=4, s=GRP)
                dst = pr[b * B:(b + 1) * B, quad * 4 * HQ:(quad + 1) * 4 * HQ].rearrange(
                    "p (g s n a q) -> p n g s a q", g=2, s=GRP, n=4, a=4)
                for g in range(2):
                    out, in_ = dst[:, :, g, :, a, :], src[:, :, g, :, b * NEW:(b + 1) * NEW]
                    ins = eng.tensor_copy(out, in_) if link else eng.activation(out, in_, ACT.Copy)
            return ins

        @block.sync
        def _(sp):
            sp.dma_start(pages[:, :], d["page_table"].rearrange("(o b) p -> o (b p)", o=1)).then_inc(ids_in, 16)
            sp.wait_ge(ids_in, 16)
            new_v = d["new_v_sample"].rearrange("b t h e -> b t (h e)")
            n_phys = d["cache_k"].shape[0]
            cache_k = d["cache_k"].rearrange("n p h c d -> n p (h c d)")
            cache_v = d["cache_v"].rearrange("n p h e -> n p (h e)")
            with sp.Fori(0, NSEQ) as i:
                for t, (what, p) in enumerate(items):
                    s = t % NR
                    if p < NPG:
                        page = sp.value_load(pages[0:1, ds(i * NPG + p, 1)], min_val=0, max_val=n_phys - 1)
                        src = (cache_k if what == "k" else cache_v)[ds(page, 1), :, :].rearrange("o p n -> (o p) n")
                        dst = ring[s][:, :]
                    else:
                        src = new_v[ds(i, 1), :, :].rearrange("o t n -> (o t) n")
                        dst = ring[s][0:NEW, :]
                    (was, q), run = (items[t - NR], 1) if t >= NR else (last_in[s], 0)
                    if was == "k":
                        sp.wait_ge(kt_ready, i * NPG + (run * NPG + q + 1))
                    else:
                        sp.wait_ge(v_lo, i * NV + (run * NV + q + 1))
                    sp.sem_inc(granted, 1)
                    sp.dma_start(dst, src).then_inc(page_in[s], 16)

        @block.gpsimd
        def _(pool):
            pool.memset(mask_new[:, :], 0.0).then_inc(const_step, 1)
            pool.memset(mask_diag[:, :], 0.0).then_inc(const_step, 1)
            pool.memset(qblk[:, :], 0.0).then_inc(const_step, 1)
            pool.wait_ge(const_step, 3)
            pool.affine_select(out=mask_new[:, :], in_=mask_new[:, :], compare_op=ALU.is_ge, fill=BIG, base=0,
                               pattern=[[1, NEW]], channel_multiplier=-1).then_inc(const_ready, 1)
            pool.affine_select(out=mask_diag[:, :], in_=mask_diag[:, :], compare_op=ALU.is_ge, fill=BIG, base=0,
                               pattern=[[-1, P]], channel_multiplier=1).then_inc(const_ready, 1)
            pool.sem_inc(y_stored, 1)
            pool.sem_inc(v_lo, NV)
            with pool.Fori(0, NSEQ) as i:
                pool.wait_ge(new_scored, i + 1)
                for dst, src in ((qcur, st.QS), (kcur, st.KS)):
                    pool.tensor_copy(dst[:, :].rearrange("p (m t) -> p m t", t=NEW),
                                     src[:, :].rearrange("p (m t) -> p m t", t=G * GS)[:, :, ds(i * NEW, NEW)]).then_inc(cur_ready, 1)
                for p in range(NV):
                    rows = slice(0, P if p < NPG else NEW)
                    pool.wait_ge(v_hi, i * NV + (p + 1))
                    pool.tensor_tensor(vl_[p % 2][rows, :], ring[(NPG + p) % NR][rows, :], vh_[p % 2][rows, :].bitcast(F32),
                                       ALU.subtract).then_inc(v_lo, 1)
                pool.wait_ge(y_ready, i + 2)
                pool.sem_inc(wait_taken, 1)
                pool.dma_start(d["y_scratch"].rearrange("m p t -> p m t")[:, ds(i * 2, 2), :],
                               o[:, :].rearrange("p (e t) -> p e t", e=2)).then_inc(y_out, 16)
                pool.wait_ge(y_out, i * 16 + 16)
                pool.sem_inc(y_stored, 1)

        @block.scalar
        def _(act):
            act.sem_inc(o_ln, 2)

            def value_hi(i, p):
                rows = slice(0, P if p < NPG else NEW)
                arrived(act, i, NPG + p)
                act.wait_ge(v_used, i * NV + (p + NV - 1 if p >= 2 else NV - p))
                act.activation(vh_[p % 2][rows, :], ring[(NPG + p) % NR][rows, :], ACT.Copy).then_inc(v_hi, 1)

            with act.Fori(0, NSEQ) as i:
                act.wait_ge(o_done, i + 1)
                for n, (dst, src) in enumerate(((qh, d["q_scratch"]), (kh, d["k_scratch"]), (zh, d["z_scratch"]))):
                    if n == 2:
                        act.wait_ge(y_ready, i + 1)
                    act.dma_start(dst[:, :].rearrange("p (c t) -> p c t", c=2),
                                  src.rearrange("m p t -> p m t")[:, ds(i * 2, 2), :]).then_inc(head_in[n], 16)
                act.dma_start(vh[:, :].rearrange("p (t e) -> p t e", t=TT),
                              d["new_v_prompt"].rearrange("o (t p) h e -> p (o t) (h e)", p=P)[:, :, ds(i * VD, VD)]
                              ).then_inc(head_in[3], 16)
                for quad in range(4):
                    act.wait_ge(sct_ready, i * 8 + (2 * quad + 2))
                    if quad == 0:
                        act.wait_ge(exp_ready, i * 2 + 2)
                    for b in (1, 3):
                        ins = move_scores(act, i, quad, b, None, None, False)
                    ins.then_inc(moved_act, 1)
                act.wait_ge(shifted, i * 2 + 2)
                act.activation(pr[:, :], pr[:, :], ACT.Exp, scale=SCALE).then_inc(exp_ready, 1)
                act.activation(prn[:, :], prn[:, :], ACT.Exp, scale=SCALE).then_inc(exp_ready, 1)
                value_hi(i, 0)
                act.wait_ge(wt_ready, i + 1)
                w3, w4 = wt[:, :].rearrange("p (g w) -> p g w", g=NPG), wst[:, :].rearrange("p (g w) -> p g w", g=NPG)
                act.activation(wstn[:, 0:WQ], wtn[:, :], ACT.Copy)
                act.activation(w4[:, :, 0:WQ], w3, ACT.Copy).then_inc(whi_ready, 1)
                value_hi(i, 1)
                for p in range(2, NV):
                    value_hi(i, p)
                    qb = (p - 2) // 3
                    n = (qb + 1) * P
                    if (p - 2) % 3 == 0 and qb < TT:
                        act.wait_ge(prompt_maxed, i * 4 + (qb + 1))
                        for c in range(2):
                            act.activation(pp[:, c * SEQ:c * SEQ + n], m.PS[:, PSC + c, 0:n], ACT.Exp, scale=SCALE,
                                           bias=pmx[:, c:c + 1], accum_out=pden[:, c:c + 1]).then_inc(prompt_exp, 1)
                    if (p - 2) % 3 == 1 and qb < TT:
                        act.wait_ge(prompt_turned, i * 4 + (qb + 1))
                        act.activation(pwt[:, :].rearrange("p (b t) -> p b t", b=TT)[:, 0:qb + 1, qb * P:(qb + 1) * P],
                                       m.PS[:, PWT, 0:n].rearrange("p (b t) -> p b t", t=P), ACT.Copy).then_inc(prompt_wt, 1)
                    if p == 14:
                        act.wait_ge(o_taken, i + 1)
                        act.activation(pp[:, :], o[:, :], ACT.Square).then_inc(osq_ready, 1)
                    if p == 15:
                        act.wait_ge(osq_sum, i + 1)
                        rsqrt(act, o_ln, i * 2 + 2, m.PS[:, SMALL, 0:SEQ], VD, m, ro[:, :])
                act.wait_ge(v_used, i * NV + 2 * NV)
                act.activation(orow[:, :].rearrange("p (c n) -> p c n", c=4), m.PS[WQ:2 * WQ, 2:6, :], ACT.Copy).then_inc(olo_ready, 1)
            act.wait_ge(out_taken, NSEQ + 1)
            act.activation(pr[:, 0:HC * G * GS], ost[:, :], ACT.Square).then_inc(fin_sq, 1)
            act.wait_ge(fin_sum, 1)
            rsqrt(act, fin_r, 0, m.PS[:, 2, 0:H * G * GS], VD, m, ro[:, 0:H * G * GS])

        @block.vector
        def _(dve):
            per = 24
            dve.sem_inc(kt_ready, NPG)
            dve.sem_inc(out_taken, 1)
            dve.sem_inc(exp_ready, 2)
            dve.sem_inc(y_ready, 1)
            dve.wait_ge(const_step, 3)
            dve.wait_ge(const_ready, 2)
            with dve.Fori(0, NSEQ) as i:
                chain = Chain(dve, dve_step, i * per)
                dve.wait_ge(cur_ready, i * 2 + 2)
                for b in range(NB):
                    for c in range(4):
                        ins = dve.tensor_copy(
                            qblk[b * B:(b + 1) * B, :].rearrange("p (m c b q) -> p m c b q", m=HC, c=4, b=8)[:, :, c, b, :],
                            qcur[c * B:(c + 1) * B, :].rearrange("p (m q) -> p m q", m=HC))
                ins.then_inc(qblk_ready, 1)
                for p in range(NPG):
                    g = p // GRP
                    arrived(dve, i, p)
                    dve.wait_ge(group_scored, i * 8 + (g + 1))
                    dve.transpose(ktg[g % 2][:, (p % GRP) * D:(p % GRP + 1) * D], ring[p % NR][:, :]).then_inc(kt_ready, 1)
                    if p % GRP == 1 and g >= 1:
                        turn_scores(dve, i, g - 1, m, KEYS, sct, sct_ready, group_scored, moved_act)
                        if (g - 1) % 2 == 1:
                            quad = (g - 1) // 2
                            if quad == 0:
                                dve.wait_ge(exp_ready, i * 2 + 2)
                            dve.wait_ge(sct_ready, i * 8 + (2 * quad + 2))
                            for b in (0, 2):
                                ins = move_scores(dve, i, quad, b, None, None, True)
                            ins.then_inc(moved_dve, 1)
                turn_scores(dve, i, 7, m, KEYS, sct, sct_ready, group_scored, moved_act)
                dve.wait_ge(sct_ready, i * 8 + 8)
                for b in (0, 2):
                    ins = move_scores(dve, i, 3, b, None, None, True)
                ins.then_inc(moved_dve, 1)
                dve.wait_ge(new_scored, i + 2)
                dve.tensor_tensor(prn[:, :].rearrange("p (m q) -> p m q", q=NEW),
                                  m.PS[0:NEW, 2, 0:HQ].rearrange("p (m q) -> p m q", q=NEW),
                                  mask_new[:, :].unsqueeze(1).to_broadcast([NEW, HC, NEW]), ALU.add).then_inc(max_ready, 1)
                dve.wait_ge(moved_act, i * 4 + 4)
                dve.wait_ge(moved_dve, i * 4 + 4)
                dve.tensor_reduce(mx[:, :], pr[:, :].rearrange("p (g c) -> p c g", c=HQ), AX.X, ALU.max).then_inc(max_ready, 1)
                dve.wait_ge(max_turned, i + 1)
                chain.link(dve.tensor_reduce(mc[:, :], m.PS[0:HQ, SMALL, P:2 * P + NEW], AX.X, ALU.max))
                dve.tensor_scalar(mdiag[:, :], m.IDENT[0:HQ, 0:HQ], mc[:, 0:1], None, ALU.mult).then_inc(diag_ready, 1)
                dve.wait_ge(max_spread, i + 1)
                chain.link(dve.tensor_copy(mb[:, :], m.PS[:, SMALL, 320:320 + HQ]))
                dve.tensor_tensor(pr[:, :].rearrange("p (g c) -> p g c", c=HQ), pr[:, :].rearrange("p (g c) -> p g c", c=HQ),
                                  mb[:, :].unsqueeze(1).to_broadcast([P, NPG, HQ]), ALU.subtract).then_inc(shifted, 1)
                dve.tensor_tensor(prn[:, :], prn[:, :], mb[0:NEW, :], ALU.subtract).then_inc(shifted, 1)
                dve.wait_ge(exp_ready, i * 2 + 4)
                dve.tensor_reduce(den[:, :], pr[:, :].rearrange("p (g c) -> p c g", c=HQ), AX.X, ALU.add).then_inc(den_ready, 1)
                dve.wait_ge(den_sum, i + 1)
                chain.link(dve.reciprocal(inv[:, :], m.PS[:, SMALL, 384:384 + HQ]))
                inv4 = inv[:, :].rearrange("p (h c q) -> p h c q", h=H, c=2)
                chain.link(dve.tensor_scalar(inv4[:, :, 1, :], inv4[:, :, 1, :], m.NLAM[:, 0:1], None, ALU.mult))
                pr4 = pr[:, :].rearrange("p (g h c q) -> p g h c q", g=NPG, h=H, c=2)
                prn4 = prn[:, :].rearrange("p (h c q) -> p h c q", h=H, c=2)
                w4 = wt[:, :].rearrange("p (g h q) -> p g h q", g=NPG, h=H)
                wn4 = wtn[:, :].rearrange("p (h q) -> p h q", h=H)
                dve.tensor_tensor(w4, pr4[:, :, :, 0, :], inv4[:, :, 0, :].unsqueeze(1).to_broadcast([P, NPG, H, NEW]), ALU.mult)
                dve.tensor_tensor(wn4, prn4[:, :, 0, :], inv4[0:NEW, :, 0, :], ALU.mult)
                dve.tensor_tensor(prn4[:, :, 1, :], prn4[:, :, 1, :], inv4[0:NEW, :, 1, :], ALU.mult)
                chain.link(dve.tensor_tensor(pr4[:, :, :, 1, :], pr4[:, :, :, 1, :],
                                             inv4[:, :, 1, :].unsqueeze(1).to_broadcast([P, NPG, H, NEW]), ALU.mult))
                dve.tensor_tensor(wn4, wn4, prn4[:, :, 1, :], ALU.add)
                dve.tensor_tensor(w4, w4, pr4[:, :, :, 1, :], ALU.add).then_inc(wt_ready, 1)
                dve.wait_ge(whi_ready, i + 1)
                ws = wst[:, :].rearrange("p (g w) -> p g w", g=NPG)
                dve.tensor_tensor(wstn[:, WQ:2 * WQ], wtn[:, :], wstn[:, 0:WQ].bitcast(F32), ALU.subtract)
                dve.tensor_tensor(ws[:, :, WQ:2 * WQ], wt[:, :].rearrange("p (g w) -> p g w", g=NPG),
                                  ws[:, :, 0:WQ].bitcast(F32), ALU.subtract).then_inc(weights_ready, 1)
                for qb in range(TT):
                    n = (qb + 1) * P
                    dve.wait_ge(prompt_scored, i * 4 + (qb + 1))
                    for c in range(2):
                        dg = m.PS[:, PSC + c, qb * P:n]
                        ins = dve.tensor_tensor(dg, dg, mask_diag[:, :], ALU.add)
                    chain.link(ins)
                    chain.link(dve.tensor_reduce(pmx[:, :], m.PS[:, PSC:PSC + 2, 0:n], AX.X, ALU.max))
                    dve.tensor_scalar(pmx[:, :], pmx[:, :], -SCALE, None, ALU.mult).then_inc(prompt_maxed, 1)
                    dve.wait_ge(prompt_exp, i * 8 + (2 * qb + 2))
                    chain.link(dve.reciprocal(pinv[:, :], pden[:, :]))
                    chain.link(dve.tensor_scalar(pp[:, SEQ:SEQ + n], pp[:, SEQ:SEQ + n], pinv[:, 1:2], m.NLAM[:, 0:1],
                                                 ALU.mult, ALU.mult))
                    dve.scalar_tensor_tensor(out=pp[:, 0:n], in0=pp[:, 0:n], scalar=pinv[:, 0:1], in1=pp[:, SEQ:SEQ + n],
                                             op0=ALU.mult, op1=ALU.add).then_inc(prompt_w, 1)
                dve.wait_ge(o_done, i + 2)
                dve.wait_ge(y_stored, i + 1)
                dve.tensor_copy(o[:, :].rearrange("p (e t) -> p e t", e=2), m.PS[:, PSC:PSC + 2, :]).then_inc(o_taken, 1)
                dve.wait_ge(head_in[2], i * 16 + 16)
                dve.wait_ge(o_ln, i * 2 + 4)
                for e in range(2):
                    oe = o[:, e * SEQ:(e + 1) * SEQ]
                    chain.link(dve.scalar_tensor_tensor(out=oe, in0=oe, scalar=m.GSUB[:, e:e + 1], in1=ro[:, :],
                                                        op0=ALU.mult, op1=ALU.mult))
                chain.link(dve.tensor_tensor(o[:, :], o[:, :], zh[:, :], ALU.mult))
                dve.sem_inc(y_ready, 1)
                dve.wait_ge(olo_ready, i + 1)
                dve.tensor_tensor(orow[:, :].rearrange("p (c n) -> p c n", c=4), m.PS[0:WQ, 2:6, :],
                                  orow[:, :].rearrange("p (c n) -> p c n", c=4), ALU.add).then_inc(orow_ready, 1)
                dve.wait_ge(o_turned, i + 1)
                for h in range(H):
                    ins = dve.tensor_copy(
                        ost[:, :].rearrange("p (m t) -> p m t", t=G * GS)[:, 2 * h:2 * h + 2, ds(i * NEW, NEW)],
                        m.PS[:, 2, :].rearrange("p (m w) -> p m w", w=WQ)[:, 2 * h:2 * h + 2, h * NEW:(h + 1) * NEW])
                ins.then_inc(out_taken, 1)
                assert chain.n == per, chain.n
            tail = Chain(dve, dve_tail)
            dve.wait_ge(fin_r, 2)
            o4 = ost[:, :].rearrange("p (h e t) -> p h e t", h=H, e=2)
            z4 = st.ZS[:, :].rearrange("p (h e t) -> p h e t", h=H, e=2)
            y4 = st.YS[:, :].rearrange("p (h e t) -> p h e t", h=H, e=2)
            r3 = ro[:, 0:H * G * GS].rearrange("p (h t) -> p h t", h=H)
            for e in range(2):
                tail.link(dve.scalar_tensor_tensor(out=y4[:, :, e, :], in0=o4[:, :, e, :], scalar=m.GSUB[:, e:e + 1],
                                                   in1=r3, op0=ALU.mult, op1=ALU.mult))
                tail.link(dve.tensor_tensor(y4[:, :, e, :], y4[:, :, e, :], z4[:, :, e, :], ALU.mult))

        @block.tensor
        def _(pe):
            def prompt_scores(i, qb):
                if qb == 0:
                    for n in (0, 1, 3):
                        pe.wait_ge(head_in[n], i * 16 + 16)
                else:
                    pe.wait_ge(prompt_exp, i * 8 + 2 * qb)
                for c in range(2):
                    last = pe.matmul(m.PS[:, PSC + c, 0:(qb + 1) * P], qh[:, c * SEQ + qb * P:c * SEQ + (qb + 1) * P],
                                     kh[:, c * SEQ:c * SEQ + (qb + 1) * P], start=True, stop=True)
                last.then_inc(prompt_scored, 1)

            def prompt_turn(i, qb):
                pe.wait_ge(prompt_w, i * 4 + (qb + 1))
                if qb:
                    pe.wait_ge(prompt_wt, i * 4 + qb)
                for kb in range(qb + 1):
                    last = pe.transpose(m.PS[:, PWT, kb * P:(kb + 1) * P], pp[:, kb * P:(kb + 1) * P], m.IDENT[:, :])
                last.then_inc(prompt_turned, 1)

            pe.sem_inc(group_scored, 2)
            pe.sem_inc(new_scored, 1)
            pe.sem_inc(o_done, 1)
            pe.sem_inc(v_used, NV)
            with pe.Fori(0, NSEQ) as i:
                pe.wait_ge(qblk_ready, i + 1)
                for g in range(NPG // GRP):
                    pe.wait_ge(kt_ready, i * NPG + (NPG + GRP * (g + 1)))
                    if g >= 2:
                        pe.wait_ge(sct_ready, i * 8 + (g - 1))
                    for a in range(4):
                        for n in range(4):
                            hc = 4 * n + a
                            for c in range(4):
                                last = pe.matmul(m.PS[a * B:(a + 1) * B, KEYS[g % 2], n * GRP * B:(n + 1) * GRP * B],
                                                 qblk[:, (hc * 4 + c) * B:(hc * 4 + c + 1) * B],
                                                 chunks(ktg[g % 2])[:, :, hc * 4 + c, :],
                                                 start=(c == 0), stop=(c == 3), skip_group_check=True)
                    last.then_inc(group_scored, 1)
                pe.wait_ge(out_taken, i + 1)
                for hc in range(HC):
                    last = pe.matmul(m.PS[0:NEW, 2, hc * NEW:(hc + 1) * NEW], kcur[:, hc * NEW:(hc + 1) * NEW],
                                     qcur[:, hc * NEW:(hc + 1) * NEW], start=True, stop=True)
                last.then_inc(new_scored, 1)
                prompt_scores(i, 0)
                pe.wait_ge(max_ready, i * 2 + 2)
                pe.sem_inc(wait_taken, 1)
                pe.transpose(m.PS[0:HQ, SMALL, P:2 * P], mx[:, :], m.IDENT[:, :])
                pe.transpose(m.PS[0:HQ, SMALL, 2 * P:2 * P + NEW], prn[:, :], m.IDENT[0:NEW, 0:NEW]).then_inc(max_turned, 1)
                pe.wait_ge(diag_ready, i + 1)
                pe.matmul(m.PS[:, SMALL, 320:320 + HQ], m.ONES[0:HQ, :], mdiag[:, :], start=True, stop=True).then_inc(max_spread, 1)
                pe.wait_ge(den_ready, i + 1)
                pe.matmul(m.PS[:, SMALL, 384:384 + HQ], m.ONES[:, :], den[:, :], start=True, stop=False)
                pe.matmul(m.PS[:, SMALL, 384:384 + HQ], m.ONES[0:NEW, :], prn[:, :], start=False, stop=True).then_inc(den_sum, 1)
                pe.wait_ge(weights_ready, i + 1)
                for p in range(NV):
                    pe.wait_ge(v_lo, i * NV + (NV + p + 1))
                    if p < NPG:
                        w, rows = wst[:, p * 2 * WQ:(p + 1) * 2 * WQ], slice(0, P)
                    else:
                        w, rows = wstn[:, :], slice(0, NEW)
                    for c in range(4):
                        for part in (vh_, vl_):
                            last = pe.matmul(OUT[0:2 * WQ, c, :], w, part[p % 2][rows, c * 512:(c + 1) * 512],
                                             start=(p == 0 and part is vh_), stop=(p == NPG and part is vl_),
                                             skip_group_check=True)
                    last.then_inc(v_used, 1)
                    if p in (3, 6, 9):
                        prompt_scores(i, p // 3)
                    if p in (2, 5, 8, 11):
                        prompt_turn(i, p // 3)
                    if p == 12:
                        pe.wait_ge(prompt_wt, i * 4 + 4)
                        for e in range(2):
                            for kb in range(TT):
                                last = pe.matmul(m.PS[:, PSC + e, kb * P:SEQ], vh[:, kb * VD + e * P:kb * VD + (e + 1) * P],
                                                 pwt[:, kb * SEQ + kb * P:(kb + 1) * SEQ], start=(kb == 0), stop=(kb == TT - 1),
                                                 skip_group_check=True)
                        last.then_inc(o_done, 1)
                    if p == 14:
                        pe.wait_ge(osq_ready, i + 1)
                        for e in range(2):
                            last = pe.matmul(m.PS[:, SMALL, :], m.ONES[:, :], pp[:, e * SEQ:(e + 1) * SEQ],
                                             start=(e == 0), stop=(e == 1))
                        last.then_inc(osq_sum, 1)
                pe.wait_ge(orow_ready, i + 1)
                pe.sem_inc(wait_taken, 1)
                for t in range(HC):
                    last = pe.transpose(m.PS[:, 2, t * WQ:(t + 1) * WQ], orow[:, t * P:(t + 1) * P], m.IDENT[0:WQ, 0:WQ])
                last.then_inc(o_turned, 1)
            pe.wait_ge(fin_sq, 1)
            for e in range(2):
                last = pe.matmul(m.PS[:, 2, 0:H * G * GS], m.ONES[:, :],
                                 pr[:, 0:HC * G * GS].rearrange("p (h e t) -> p h e t", h=H, e=2)[:, :, e, :],
                                 start=(e == 0), stop=(e == 1))
            last.then_inc(fin_sum, 1)


def turn_scores(dve, i, g, m, keys, sct, sct_ready, group_scored, moved_act):
    dve.wait_ge(group_scored, i * 8 + (g + 3))
    if g >= 4 and g % 2 == 0:
        dve.wait_ge(moved_act, i * 4 + (g // 2 - 1))
    w = m.PS.shape[2] // 2
    dve.transpose(sct[(g // 2) % 2][:, (g % 2) * w:(g % 2 + 1) * w], m.PS[:, keys[g % 2], 0:w]).then_inc(sct_ready, 1)


def project_out(nc, m, d, st):
    with ExitStack() as ctx:
        def sb(name, shape, dt=F32):
            return ctx.enter_context(nc.sbuf_tensor(name, shape, dt))

        def sem(name):
            return new_sem(nc, m, name)
        yh, yl = sb("ay_hi", [P, KT * T], F32R), sb("ay_lo", [P, KT * T], F32R)
        raw = [sb(f"f_raw{s}", [P, D]) for s in range(2)]
        xr = [sb(f"x_in{s}", [P, T]) for s in range(2)]
        x_in = [sem(f"f_x_in{s}") for s in range(2)]
        ys = [sb(f"y_in{s}", [P, SEQ]) for s in range(2)]
        x2 = [sb(f"x2_{s}", [P, T]) for s in range(2)]
        rows = sb("x2_rows", [P, TT * P])
        srows = sb("x2_srows", [GS, G * P])
        raw_in = [sem(f"f_raw_in{s}") for s in range(2)]
        y_in = [sem(f"y_in_done{s}") for s in range(2)]
        yh_ready, yl_ready, ys_ready = sem("f_yh_ready"), sem("f_yl_ready"), sem("f_ys_ready")
        hi_ready, lo_ready, block_done = sem("f_hi_ready"), sem("f_lo_ready"), sem("f_block_done")
        x2_ready, turned, rows_ready, rows_out, granted = (sem("f_x2_ready"), sem("f_turned"), sem("f_rows_ready"),
                                                           sem("f_rows_out"), sem("f_granted"))
        block = ctx.enter_context(nc.Block())
        psum = [m.PS[:, 2 * s:2 * s + 2, :] for s in range(2)]
        out_p = d["y_prompt"].rearrange("o (t p) c -> p (o t) c", p=P)
        out_s = d["y_sample"].rearrange("(g b) t c -> (b t) g c", g=G)

        @block.sync
        def _(sp):
            for s in range(2):
                sp.dma_start(ys[s][:, :], d["y_scratch"][s]).then_inc(y_in[s], 16)
                sp.wait_ge(lo_ready, s + 1)
                sp.dma_start(tiles(raw[s][:, :]), w_block(d["w_out_b"][0], s * P)).then_inc(raw_in[s], 16)
                sp.dma_start(xr[s][:, :], d["x_scratch"][s]).then_inc(x_in[s], 16)
            for k in range(2, KT):
                sp.wait_ge(yl_ready, k - 1)
                sp.dma_start(ys[k % 2][:, :], d["y_scratch"][k]).then_inc(y_in[k % 2], 16)
            with sp.Fori(1, KT // 2) as pair:
                for s in range(2):
                    sp.wait_ge(lo_ready, pair * 2 + (s + 1))
                    sp.sem_inc(granted, 1)
                    sp.dma_start(tiles(raw[s][:, :]), w_block(d["w_out_b"][0], pair * 2 * P + s * P)).then_inc(raw_in[s], 16)
                    sp.wait_ge(x2_ready, pair * 2 + (s - 1))
                    sp.sem_inc(granted, 1)
                    sp.dma_start(xr[s][:, :], d["x_scratch"].rearrange("m p t -> p m t")[:, ds(pair * 2 + s, 1), :]
                                 .rearrange("p m t -> p (m t)")).then_inc(x_in[s], 16)

        @block.scalar
        def _(act):
            def split_hi(n, s, use):
                act.wait_ge(raw_in[s], use * 16 + 16)
                act.wait_ge(block_done, n + 1)
                act.activation(m.WH[s][:, :], raw[s][:, :], ACT.Copy).then_inc(hi_ready, 1)

            def store(n):
                act.wait_ge(turned, n + 3)
                act.wait_ge(rows_out, n * 32 + 32)
                act.activation(rows[:, :], m.PS[:, 6, :], ACT.Copy).then_inc(rows_ready, 1)
                act.activation(srows[:, :], m.PS[0:GS, 7, 0:G * P], ACT.Copy).then_inc(rows_ready, 1)
                act.wait_ge(rows_ready, n * 2 + 3)
                act.dma_start(out_p[:, :, ds(n * P, P)], rows[:, :].rearrange("p (t c) -> p t c", t=TT)).then_inc(rows_out, 16)
                act.dma_start(out_s[:, :, ds(n * P, P)], srows[:, :].rearrange("p (g c) -> p g c", g=G)).then_inc(rows_out, 16)

            act.sem_inc(rows_ready, 1)
            act.sem_inc(rows_out, 32)
            split_hi(0, 0, 0)
            for g in range(G):
                act.activation(yh[:, :].rearrange("p (k g t) -> p k g t", k=KT, g=G)[:, :, g, GP:GT],
                               st.YS[:, :].rearrange("p (k g t) -> p k g t", k=KT, g=G)[:, :, g, :], ACT.Copy).then_inc(ys_ready, 1)
            for k in range(KT):
                act.wait_ge(y_in[k % 2], 16 * (k // 2 + 1))
                act.activation(grouped(yh[:, k * T:(k + 1) * T])[:, :, 0:GP], ys[k % 2][:, :].rearrange("p (g t) -> p g t", g=G),
                               ACT.Copy).then_inc(yh_ready, 1)
            split_hi(1, 1, 0)
            with act.Fori(1, KT // 2) as pair:
                for s in range(2):
                    split_hi(pair * 2 + s, s, pair)
                    store(pair * 2 + (s - 2))
            store(KT - 2)
            store(KT - 1)
            act.wait_ge(rows_out, 32 * KT + 32)

        @block.vector
        def _(dve):
            def split_lo(n, s):
                dve.wait_ge(hi_ready, n + 1)
                dve.wait_ge(block_done, n + 1)
                dve.tensor_tensor(m.WL[s][:, :], raw[s][:, :], m.WH[s][:, :].bitcast(F32), ALU.subtract).then_inc(lo_ready, 1)

            def body(n, s, use):
                if not (isinstance(n, int) and n == KT - 1):
                    split_lo(n + 1, 1 - s)
                dve.wait_ge(block_done, n + 3)
                dve.wait_ge(turned, n + 1)
                dve.wait_ge(x_in[s], use * 16 + 16)
                dve.tensor_tensor(grouped(x2[s][:, :]), psum[s][:, :, 0:GT], grouped(xr[s][:, :]), ALU.add).then_inc(x2_ready, 1)

            dve.sem_inc(lo_ready, 2)
            split_lo(0, 0)
            dve.wait_ge(ys_ready, G)
            for g in range(G):
                v = [a.rearrange("p (k g t) -> p k g t", k=KT, g=G)[:, :, g, GP:GT] for a in (yl[:, :], yh[:, :])]
                dve.tensor_tensor(v[0], st.YS[:, :].rearrange("p (k g t) -> p k g t", k=KT, g=G)[:, :, g, :],
                                  v[1].bitcast(F32), ALU.subtract).then_inc(ys_ready, 1)
            for k in range(KT):
                dve.wait_ge(yh_ready, k + 1)
                yk = slice(k * T, (k + 1) * T)
                dve.tensor_tensor(grouped(yl[:, yk])[:, :, 0:GP], ys[k % 2][:, :].rearrange("p (g t) -> p g t", g=G),
                                  grouped(yh[:, yk].bitcast(F32))[:, :, 0:GP], ALU.subtract).then_inc(yl_ready, 1)
            for n in range(2):
                body(n, n, 0)
            with dve.Fori(1, KT // 2 - 1) as pair:
                for s in range(2):
                    body(pair * 2 + s, s, pair)
            for n in range(KT - 2, KT):
                body(n, n % 2, n // 2)

        @block.tensor
        def _(pe):
            def turn_tile(n, s):
                pe.wait_ge(x2_ready, n + 1)
                pe.wait_ge(rows_ready, n * 2 + 1)
                for t in range(TT):
                    pe.transpose(m.PS[:, 6, t * P:(t + 1) * P],
                                 x2[s][:, (t // 2) * GT + (t % 2) * P:(t // 2) * GT + (t % 2 + 1) * P], m.IDENT[:, :])
                for g in range(G):
                    last = pe.transpose(m.PS[0:GS, 7, g * P:(g + 1) * P], x2[s][:, g * GT + GP:(g + 1) * GT], m.IDENT[:, :])
                last.then_inc(turned, 1)

            def body(n, s, first=False):
                pe.wait_ge(hi_ready, n + 1)
                if not first:
                    pe.wait_ge(x2_ready, n - 1)
                elif n == 0:
                    pe.wait_ge(yl_ready, KT)
                    pe.wait_ge(ys_ready, 2 * G)
                project_hi(pe, m, s, psum[s], yh, yl)
                if not first:
                    turn_tile(n - 2, s)
                pe.wait_ge(lo_ready, n + 3)
                project_lo(pe, m, s, psum[s], yh).then_inc(block_done, 1)

            pe.sem_inc(block_done, 2)
            pe.sem_inc(turned, 2)
            for n in range(2):
                body(n, n, first=True)
            with pe.Fori(1, KT // 2) as pair:
                for s in range(2):
                    body(pair * 2 + s, s)
            turn_tile(KT - 2, 0)
            turn_tile(KT - 1, 1)


def build(nc, d):
    with ExitStack() as ctx:
        m = memory(nc, ctx)
        first = ctx.enter_context(ExitStack())
        m.keep, m.sems = first, []
        st = Bag()
        st.QS, st.KS, st.ZS = (ctx.enter_context(nc.sbuf_tensor(f"{name}_sample", [P, HC * G * GS], F32)) for name in "qkz")
        with ExitStack() as x:
            m.XH = x.enter_context(nc.sbuf_tensor("x_hi", [P, KT * T], F32R))
            m.XL = x.enter_context(nc.sbuf_tensor("x_lo", [P, KT * T], F32R))
            weight_memory(nc, m, x, "w")
            with ExitStack() as a:
                st.RS2 = a.enter_context(nc.sbuf_tensor("rs_squared", [P, T], F32))
                st.STATE = a.enter_context(nc.sbuf_tensor("state", [P, KT * GS], F32))
                read_inputs(nc, m, d, st)
                st.YH = a.enter_context(nc.sbuf_tensor("y_hi", [P, KT * T], F32R))
                st.YL = a.enter_context(nc.sbuf_tensor("y_lo", [P, KT * T], F32R))
                conv_in(nc, m, d, st)
                conv_out(nc, m, d, st)
            for kind in "qkvz":
                project_heads(nc, m, d, st, kind)
        numbers = [s.num for s in m.sems]
        nc.all_engine_barrier(sems_to_clear=range(min(numbers), max(numbers) + 1))
        first.close()
        m.keep = ctx
        st.YS = ctx.enter_context(nc.sbuf_tensor("y_sample", [P, HC * G * GS], F32))
        st.NR = 7
        attention(nc, m, d, st)
        with ExitStack() as w:
            weight_memory(nc, m, w, "wf")
            project_out(nc, m, d, st)


_INS = ['x_prompt', 'x_sample', 'state_conv', 'cache_k', 'cache_v', 'page_table', 'norm_a', 'w_in_a', 'conv_w',
        'w_out_a', 'norm_kv', 'w_kv', 'k_norm', 'norm_b', 'w_in_b', 'q_norm', 'lam', 'subln_w', 'w_out_b']
_OUTS = [('y_prompt', (1, SEQ, D)), ('y_sample', (NSEQ, NEW, D)), ('new_k_prompt', (1, SEQ, H, 2, HD)),
         ('new_v_prompt', (1, SEQ, H, VD)), ('new_conv_prompt', (1, 1, CONV - 1, D)),
         ('new_k_sample', (NSEQ, NEW, H, 2, HD)), ('new_v_sample', (NSEQ, NEW, H, VD)),
         ('new_conv_sample', (1, NSEQ, CONV - 1, D))]


def _rope_tables():
    import numpy as np
    inv = np.float32(THETA) ** (-np.arange(0, ROT, 2, dtype=np.float32) / np.float32(ROT))
    sample = PAST + np.tile(np.arange(NEW), NSEQ // G)
    pos = np.concatenate([np.concatenate([np.arange(g * GP, (g + 1) * GP), sample]) for g in range(G)])
    ang = pos.astype(np.float32)[None, :] * inv[:, None].astype(np.float32)
    c, s = np.cos(ang), np.sin(ang)
    return np.concatenate([c, c]).astype(np.float32), np.concatenate([-s, s]).astype(np.float32)


def kernel(**inputs):
    import numpy as _np
    import concourse.bacc as _bacc
    from concourse import mybir as _mybir
    from concourse.bass_utils import run_bass_kernel_spmd as _run

    nc = _bacc.Bacc("TRN2", target_bir_lowering=False, num_devices=1)
    arrays, d = {}, {}

    def give(name, a):
        arrays[f"in_{name}_dram"] = a
        d[name] = nc.dram_tensor(f"in_{name}_dram", a.shape, _mybir.dt.from_np(a.dtype), kind="ExternalInput").ap()
    for name in _INS:
        give(name, _np.ascontiguousarray(inputs[name]))
    cos, sin = _rope_tables()
    give("rope_cos", cos)
    give("rope_sin", sin)
    for name, shape in _OUTS:
        d[name] = nc.dram_tensor(f"out_{name}_dram", shape, _mybir.dt.float32, kind="ExternalOutput").ap()
    for name in ("q_scratch", "k_scratch", "z_scratch", "y_scratch", "x_scratch"):
        width = T if name == "x_scratch" else SEQ
        d[name] = nc.dram_tensor(name, (HC, P, width), _mybir.dt.float32, kind="Internal").ap()
    build(nc, d)
    r = _run(nc, [arrays], core_ids=[0])
    return tuple(r.results[0][f"out_{name}_dram"] for name, _ in _OUTS)
```

```python
import math
from contextlib import ExitStack

import concourse.bass as bass
from concourse import mybir

F32 = mybir.dt.float32
F32R = mybir.dt.float32r
I32 = mybir.dt.int32
ALU = mybir.AluOpType
ACT = mybir.ActivationFunctionType
AX = mybir.AxisListType
ds = bass.ds

P = 128
D = 2048
KT = D // P
SEQ = 512
NSEQ, NEW = 8, 4
CONV = 3
H = 8
HC = 2 * H
HD = 128
VD = 256
PAGE = 128
NPG = 16
PAST = NPG * PAGE
G = 2
GP = SEQ // G
GS = NSEQ * NEW // G
GT = GP + GS
T = G * GT
TT = SEQ // P
ROT = HD // 4
THETA = 500000.0
EPS = 1e-6
LAM_INIT = 0.8 - 0.6 * math.exp(-0.3 * 1)
SCALE = HD ** -0.5
BIG = -3.0e38

GA, GKV, GB, CW, KN_, QN_, SUB, LAM = 0, 16, 32, 48, 96, 97, 98, 100
NPAR = 104

SLOTS = 2


class Bag:
    pass


class Chain:

    def __init__(self, eng, sem, base=0):
        self.eng, self.sem, self.base, self.n = eng, sem, base, 0

    def link(self, ins):
        ins.then_inc(self.sem, 1)
        self.n += 1
        self.eng.wait_ge(self.sem, self.base + self.n)


def new_sem(nc, m, name):
    m.sems.append(m.keep.enter_context(nc.semaphore(name)))
    return m.sems[-1]


def grouped(ap):
    return ap.rearrange("p (g t) -> p g t", g=G)


def w_block(w, col):
    return w.rearrange("(k p) n -> p k n", p=P)[:, :, ds(col, P)]


def tiles(ap):
    return ap.rearrange("p (k n) -> p k n", k=KT)


def project_hi(pe, m, s, out, xh, xl, x_ready=None):
    for k in range(KT):
        if x_ready is not None:
            pe.wait_ge(x_ready, k + 1)
        for x in (xh, xl):
            for g in range(G):
                pe.matmul(out[:, g, 0:GT], m.WH[s][:, k * P:(k + 1) * P], x[:, k * T + g * GT:k * T + (g + 1) * GT],
                          start=(k == 0 and x is xh), stop=False, skip_group_check=True)


def project_lo(pe, m, s, out, xh):
    for k in range(KT):
        for g in range(G):
            last = pe.matmul(out[:, g, 0:GT], m.WL[s][:, k * P:(k + 1) * P], xh[:, k * T + g * GT:k * T + (g + 1) * GT],
                             start=False, stop=(k == KT - 1), skip_group_check=True)
    return last


def rsqrt(act, step, at, total, n, m, out, out_squared=None):
    act.activation(out, total, ACT.Ln, bias=m.EPSC[0:total.shape[0], 0:1], scale=1.0 / n).then_inc(step, 1)
    act.wait_ge(step, at + 1)
    if out_squared is not None:
        act.activation(out_squared, out, ACT.Exp, scale=-1.0).then_inc(step, 1)
    return act.activation(out, out, ACT.Exp, scale=-0.5).then_inc(step, 1)


def weight_memory(nc, m, ctx, name):
    m.WH = [ctx.enter_context(nc.sbuf_tensor(f"{name}_hi{s}", [P, D], F32R)) for s in range(SLOTS)]
    m.WL = [ctx.enter_context(nc.sbuf_tensor(f"{name}_lo{s}", [P, D], F32R)) for s in range(SLOTS)]


def raw_memory(nc, m, ctx):
    m.RAW = [ctx.enter_context(nc.sbuf_tensor(f"raw{s}", [P, D], F32)) for s in range(SLOTS)]


def load_next(sp, m, following, lo_ready, raw_in, n):
    w, col0 = following[0:2]
    for s in range(SLOTS):
        sp.wait_ge(lo_ready, n + s + 1)
        sp.dma_start(tiles(m.RAW[s][:, :]), w_block(w, col0 + s * P)).then_inc(raw_in[s], 16)


def memory(nc, ctx):
    def sb(name, shape, dt=F32):
        return ctx.enter_context(nc.sbuf_tensor(name, shape, dt))
    m = Bag()
    m.PAR = sb("params", [P, NPAR])
    m.IDENT = sb("ident", [P, P])
    m.ONES = sb("ones", [P, P])
    m.EPSC = sb("eps", [P, 1])
    m.RS = sb("rs", [P, T])
    m.NLAM = sb("neg_lambda", [P, 1])
    m.GSUB = sb("subln_gain", [P, 2])
    m.PS = ctx.enter_context(nc.psum_tensor("psum", [P, 8, 512], F32))
    return m


def read_inputs(nc, m, d, st, following):
    with ExitStack() as ctx:
        def sb(name, shape, dt=F32):
            return ctx.enter_context(nc.sbuf_tensor(name, shape, dt))

        def sem(name):
            return new_sem(nc, m, name)
        xp = sb("xp_rows", [P, TT, D])
        xs = sb("xs_rows", [GS, G, D])
        srow = sb("state_rows", [GS, D])
        prow = sb("param_rows", [NPAR, P])
        sq = [sb(f"x_sq{s}", [P, T]) for s in range(2)]
        acc = sb("x_sq_sum", [P, T])
        lprod = sb("lam_prod", [P, 2])
        lexp = sb("lam_exp", [P, 2])
        par_in, small_in = sem("par_in"), sem("small_in")
        x_in = [sem(f"x_in{c}") for c in range(4)]
        const_ready, par_t, par_ready = sem("const_ready"), sem("par_transposed"), sem("par_ready")
        xt_ready, xh_ready, xl_ready = sem("xt_ready"), sem("xh_ready"), sem("xl_ready")
        sq_ready, sq_used, sum_ready = sem("sq_ready"), sem("sq_used"), sem("sum_ready")
        state_t, lam_ready, lam_sum, lam_exp = sem("state_transposed"), sem("lam_ready"), sem("lam_sum"), sem("lam_exp")
        raw_in, scaled, hi_ready = [sem(f"i_raw_in{s}") for s in range(SLOTS)], sem("i_scaled"), sem("i_hi_ready")
        act_step, pool_step, dve_step = sem("act_step"), sem("pool_step"), sem("dve_step")
        block = ctx.enter_context(nc.Block())

        @block.sync
        def _(sp):
            rows = [(GA, d["norm_a"].rearrange("l (k p) -> (l k) p", p=P), 16),
                    (GKV, d["norm_kv"].rearrange("(k p) -> k p", p=P), 16),
                    (GB, d["norm_b"].rearrange("l (k p) -> (l k) p", p=P), 16),
                    (CW, d["conv_w"].rearrange("l i (k p) -> (l i k) p", p=P), 48),
                    (KN_, d["k_norm"].rearrange("(k p) -> k p", p=P), 1),
                    (QN_, d["q_norm"], 1),
                    (SUB, d["subln_w"].rearrange("l (k p) -> (l k) p", p=P), 2),
                    (LAM, d["lam"].rearrange("l r p -> (l r) p"), 4)]
            sp.dma_start(xs[:, :, :], d["x_sample"].rearrange("(g b) t c -> (b t) g c", g=G)).then_inc(small_in, 16)
            sp.dma_start(srow[:, :], d["state_conv"].rearrange("l b i c -> (l b i) c")).then_inc(small_in, 16)
            x_rows = d["x_prompt"].rearrange("o (t p) c -> p (o t) c", p=P)
            for c in range(4):
                sp.dma_start(xp[:, :, c * 512:(c + 1) * 512], x_rows[:, :, c * 512:(c + 1) * 512]).then_inc(x_in[c], 16)
            for at, src, n in rows:
                sp.dma_start(prow[at:at + n, :], src).then_inc(par_in, 16)
            for s in range(SLOTS):
                sp.dma_start(tiles(m.RAW[s][:, :]), w_block(following[0], following[1][s])).then_inc(raw_in[s], 16)
            sp.wait_ge(raw_in[1], 16)

        @block.gpsimd
        def _(pool):
            pool.memset(m.ONES[:, :], 1.0).then_inc(pool_step, 1)
            pool.memset(m.EPSC[:, :], EPS).then_inc(pool_step, 1)
            pool.memset(acc[:, :], 0.0).then_inc(pool_step, 1)
            pool.memset(m.IDENT[:, :], 0.0).then_inc(pool_step, 1)
            pool.wait_ge(pool_step, 4)
            pool.affine_select(out=m.IDENT[:, :], in_=m.IDENT[:, :], compare_op=ALU.not_equal, fill=1.0, base=0,
                               pattern=[[-1, P]], channel_multiplier=1).then_inc(const_ready, 1)
            for k in range(KT):
                pool.wait_ge(sq_ready, k + 1)
                pool.wait_ge(sq_used, k) if k else None
                pool.tensor_tensor(acc[:, :], acc[:, :], sq[k % 2][:, :], ALU.add).then_inc(sq_used, 1)
            pool.wait_ge(par_ready, 1)
            pool.wait_ge(raw_in[0], 16)
            pool.tensor_tensor(tiles(m.RAW[0][:, :]), tiles(m.RAW[0][:, :]),
                               m.PAR[:, GA:GA + KT].unsqueeze(2).to_broadcast([P, KT, P]), ALU.mult).then_inc(scaled, 1)

        @block.scalar
        def _(act):
            for k in range(KT):
                b = 2 * (k % 2)
                xt = m.PS[:, b:b + 2, 0:GT]
                act.wait_ge(xt_ready, k + 1)
                act.activation(grouped(m.XH[:, k * T:(k + 1) * T]), xt, ACT.Copy).then_inc(xh_ready, 1)
                if k >= 2:
                    act.wait_ge(sq_used, k - 1)
                act.activation(grouped(sq[k % 2][:, :]), xt, ACT.Square).then_inc(sq_ready, 1)
            act.wait_ge(lam_sum, 1)
            act.activation(lexp[:, :], m.PS[:, 4, 256:258], ACT.Exp).then_inc(lam_exp, 1)
            act.wait_ge(sum_ready, 1)
            rsqrt(act, act_step, 0, m.PS[:, 6:8, 0:GT], D, m, grouped(m.RS[:, :]), grouped(st.RS2[:, :]))
            act.wait_ge(scaled, 1)
            act.activation(m.WH[0][:, :], m.RAW[0][:, :], ACT.Copy).then_inc(hi_ready, 1)

        @block.vector
        def _(dve):
            for k in range(KT):
                b = 2 * (k % 2)
                xk = slice(k * T, (k + 1) * T)
                dve.wait_ge(sq_ready, k + 1)
                dve.tensor_tensor(grouped(m.XL[:, xk]), m.PS[:, b:b + 2, 0:GT], grouped(m.XH[:, xk].bitcast(F32)),
                                  ALU.subtract).then_inc(xl_ready, 1)
            dve.wait_ge(par_t, 1)
            dve.tensor_copy(m.PAR[:, :], m.PS[:, 4, 0:NPAR]).then_inc(par_ready, 1)
            dve.wait_ge(par_ready, 1)
            dve.tensor_tensor(lprod[:, :], m.PAR[:, LAM:LAM + 4:2], m.PAR[:, LAM + 1:LAM + 4:2],
                              ALU.mult).then_inc(lam_ready, 1)
            dve.tensor_scalar(m.GSUB[:, :], m.PAR[:, SUB:SUB + 2], 1.0 - LAM_INIT, None, ALU.mult).then_inc(dve_step, 1)
            dve.wait_ge(state_t, 1)
            dve.tensor_copy(st.STATE[:, :], m.PS[:, 5, 0:KT * GS]).then_inc(dve_step, 1)
            dve.wait_ge(lam_exp, 1)
            dve.scalar_tensor_tensor(out=m.NLAM[:, :], in0=lexp[:, 1:2], scalar=-LAM_INIT, in1=lexp[:, 0:1],
                                     op0=ALU.add, op1=ALU.subtract).then_inc(dve_step, 1)
            dve.wait_ge(hi_ready, 1)
            dve.tensor_tensor(m.WL[0][:, :], m.RAW[0][:, :], m.WH[0][:, :].bitcast(F32), ALU.subtract).then_inc(dve_step, 1)

        @block.tensor
        def _(pe):
            pe.wait_ge(const_ready, 1)
            pe.wait_ge(small_in, 32)
            for k in range(KT):
                b = 2 * (k % 2)
                if k % 4 == 0:
                    pe.wait_ge(x_in[k // 4], 16)
                if k >= 2:
                    pe.wait_ge(xl_ready, k - 1)
                for t in range(TT):
                    pe.transpose(m.PS[:, b + t // 2, (t % 2) * P:(t % 2 + 1) * P], xp[:, t, k * P:(k + 1) * P], m.IDENT[:, :])
                for g in range(G):
                    last = pe.transpose(m.PS[:, b + g, GP:GT], xs[:, g, k * P:(k + 1) * P], m.IDENT[0:GS, 0:GS])
                last.then_inc(xt_ready, 1)
            pe.wait_ge(par_in, 8 * 16)
            pe.transpose(m.PS[:, 4, 0:NPAR], prow[:, :], m.IDENT[0:NPAR, 0:NPAR]).then_inc(par_t, 1)
            for k in range(KT):
                last = pe.transpose(m.PS[:, 5, k * GS:(k + 1) * GS], srow[:, k * P:(k + 1) * P], m.IDENT[0:GS, 0:GS])
            last.then_inc(state_t, 1)
            pe.wait_ge(lam_ready, 1)
            pe.matmul(m.PS[:, 4, 256:258], m.ONES[:, :], lprod[:, :], start=True, stop=True).then_inc(lam_sum, 1)
            pe.wait_ge(sq_used, KT)
            for g in range(G):
                last = pe.matmul(m.PS[:, 6 + g, 0:GT], m.ONES[:, :], acc[:, g * GT:(g + 1) * GT], start=True, stop=True)
            last.then_inc(sum_ready, 1)


CONV_IN_COLS = [D, 2 * D, 3 * D, 0]


def conv_in(nc, m, d, st, following):
    cols = CONV_IN_COLS
    NB = 4 * KT
    with ExitStack() as ctx:
        def sb(name, shape, dt=F32):
            return ctx.enter_context(nc.sbuf_tensor(name, shape, dt))

        def sem(name):
            return new_sem(nc, m, name)
        raw = m.RAW
        cg = sb("c_gate", [P, T])
        zs = sb("z", [P, T])
        ex = sb("z_exp", [P, T])
        up = sb("u_prompt", [P, CONV - 1 + SEQ])
        us = sb("u_sample", [P, NSEQ, CONV - 1 + NEW])
        lastu = sb("u_last", [P, 2 + NSEQ * 2])
        lastr = sb("u_last_rows", [2 + NSEQ * 2, P])
        raw_in = [sem(f"a_raw_in{s}") for s in range(SLOTS)]
        scaled, hi_ready, lo_ready = sem("a_scaled"), sem("a_hi_ready"), sem("a_lo_ready")
        block_done, evacuated = sem("a_block_done"), sem("a_evacuated")
        e_ready, yh_ready, yl_ready = sem("a_e_ready"), sem("a_yh_ready"), sem("a_yl_ready")
        lu_ready, lu_turned, lr_ready, lr_out = sem("a_lu_ready"), sem("a_lu_turned"), sem("a_lr_ready"), sem("a_lr_out")
        dve_step, granted = sem("a_dve_step"), sem("a_slot_granted")
        block = ctx.enter_context(nc.Block())
        psum = [m.PS[:, 2 * s:2 * s + 2, :] for s in range(SLOTS)]

        @block.sync
        def _(sp):
            def load(j, p):
                sp.wait_ge(lo_ready, j * 4 + (p + 1))
                sp.sem_inc(granted, 1)
                sp.dma_start(tiles(raw[p % 2][:, :]), w_block(d["w_in_a"][0], j * P + cols[p])).then_inc(raw_in[p % 2], 16)

            for s in range(SLOTS):
                sp.sem_inc(raw_in[s], 16)
            load(0, 2)
            load(0, 3)
            with sp.Fori(1, KT) as j:
                for p in range(4):
                    load(j, p)
            load_next(sp, m, following, lo_ready, raw_in, NB)
            for s in range(SLOTS):
                sp.wait_ge(raw_in[s], 16 * (NB // 2 + 1))

        @block.gpsimd
        def _(pool):
            def scale(j, p):
                pool.wait_ge(raw_in[p % 2], j * 32 + 16 * (p // 2 + 1))
                pool.tensor_tensor(tiles(raw[p % 2][:, :]), tiles(raw[p % 2][:, :]),
                                   m.PAR[:, GA:GA + KT].unsqueeze(2).to_broadcast([P, KT, P]),
                                   ALU.mult).then_inc(scaled, 1)

            pool.sem_inc(scaled, 1)
            for p in range(1, 4):
                scale(0, p)
            with pool.Fori(1, KT) as j:
                for p in range(4):
                    scale(j, p)

        @block.scalar
        def _(act):
            def split_hi(j, p):
                if isinstance(j, int) and j * 4 + p == NB:
                    act.wait_ge(raw_in[0], 16 * (NB // 2 + 1))
                else:
                    act.wait_ge(scaled, j * 4 + (p + 1))
                act.wait_ge(block_done, j * 4 + (p + 1))
                act.activation(m.WH[p % 2][:, :], raw[p % 2][:, :], ACT.Copy).then_inc(hi_ready, 1)

            def body(j):
                split_hi(j, 1)
                split_hi(j, 2)
                split_hi(j, 3)
                act.wait_ge(evacuated, j * 4 + (3 + SLOTS))
                act.activation(ex[:, :], zs[:, :], ACT.Exp, scale=-1.0).then_inc(e_ready, 1)
                act.wait_ge(lu_turned, j + 2)
                act.activation(lastr[:, :], m.PS[0:18, 6, 0:P], ACT.Copy).then_inc(lr_ready, 1)
                act.wait_ge(lr_ready, j + 2)
                act.dma_start(d["new_conv_prompt"].rearrange("l o i c -> (l o i) c")[:, ds(j * P, P)],
                              lastr[0:2, :]).then_inc(lr_out, 16)
                act.dma_start(d["new_conv_sample"].rearrange("l b i c -> (l b i) c")[:, ds(j * P, P)],
                              lastr[2:18, :]).then_inc(lr_out, 16)
                split_hi(j, 4)
                act.wait_ge(evacuated, j * 4 + (4 + SLOTS))
                act.activation(st.YH[:, ds(j * T, T)], zs[:, :], ACT.Copy).then_inc(yh_ready, 1)
                act.wait_ge(lr_out, j * 32 + 32)
            act.sem_inc(lr_ready, 1)
            act.sem_inc(hi_ready, 1)
            with act.Fori(0, KT - 1) as j:
                body(j)
            body(KT - 1)

        @block.vector
        def _(dve):
            dve.sem_inc(lo_ready, SLOTS + 1)
            dve.sem_inc(evacuated, SLOTS)
            dve.sem_inc(yl_ready, 1)
            dve.memset(up[:, 0:2], 0.0).then_inc(dve_step, 1)
            dve.wait_ge(dve_step, 1)
            per = 18

            def split_lo(j, p):
                dve.wait_ge(hi_ready, j * 4 + (p + 1))
                dve.wait_ge(block_done, j * 4 + (p + 1))
                dve.tensor_tensor(m.WL[p % 2][:, :], raw[p % 2][:, :], m.WH[p % 2][:, :].bitcast(F32),
                                  ALU.subtract).then_inc(lo_ready, 1)

            def body(j):
                chain = Chain(dve, dve_step, j * per + 1)
                split_lo(j, 1)
                dve.wait_ge(block_done, j * 4 + (1 + SLOTS))
                dve.tensor_tensor(grouped(cg[:, :]), psum[0][:, :, 0:GT], grouped(st.RS2[:, :]), ALU.mult).then_inc(evacuated, 1)
                split_lo(j, 2)
                chain.link(dve.tensor_copy(us[:, :, 0:2], st.STATE[:, ds(j * GS, GS)].rearrange("p (b i) -> p b i", i=2)))
                dve.wait_ge(block_done, j * 4 + (2 + SLOTS))
                dve.wait_ge(evacuated, j * 4 + (1 + SLOTS))
                chain.link(dve.tensor_tensor(up[:, 2:2 + SEQ].rearrange("p (g t) -> p g t", g=G), psum[1][:, :, 0:GP],
                                             grouped(cg[:, :])[:, :, 0:GP], ALU.mult))
                for g in range(G):
                    ins = dve.tensor_tensor(us[:, 4 * g:4 * g + 4, 2:6],
                                            psum[1][:, g, GP:GT].rearrange("p (b t) -> p b t", t=NEW),
                                            cg[:, g * GT + GP:(g + 1) * GT].rearrange("p (b t) -> p b t", t=NEW), ALU.mult)
                    if g == 0:
                        chain.link(ins)
                    else:
                        ins.then_inc(evacuated, 1)
                dve.wait_ge(evacuated, j * 4 + (2 + SLOTS))
                split_lo(j, 3)
                dve.wait_ge(lu_turned, j + 1)
                chain.link(dve.tensor_copy(lastu[:, 0:2], up[:, SEQ:SEQ + 2]))
                dve.tensor_copy(lastu[:, 2:18].rearrange("p (b i) -> p b i", i=2), us[:, :, 4:6]).then_inc(lu_ready, 1)
                tap = [m.PAR[:, ds(j + (CW + KT * i), 1)] for i in range(CONV)]
                cvp = grouped(cg[:, :])[:, :, 0:GP]
                chain.link(dve.tensor_scalar(cvp, up[:, 2:2 + SEQ].rearrange("p (g t) -> p g t", g=G), tap[2], None, ALU.mult))
                for i in (1, 0):
                    chain.link(dve.scalar_tensor_tensor(out=cvp, in0=up[:, i:i + SEQ].rearrange("p (g t) -> p g t", g=G),
                                                        scalar=tap[i], in1=cvp, op0=ALU.mult, op1=ALU.add))
                for g in range(G):
                    cvs = cg[:, g * GT + GP:(g + 1) * GT].rearrange("p (b t) -> p b t", t=NEW)
                    ub = us[:, 4 * g:4 * g + 4, :]
                    chain.link(dve.tensor_scalar(cvs, ub[:, :, 2:6], tap[2], None, ALU.mult))
                    for i in (1, 0):
                        chain.link(dve.scalar_tensor_tensor(out=cvs, in0=ub[:, :, i:i + 4], scalar=tap[i], in1=cvs,
                                                            op0=ALU.mult, op1=ALU.add))
                dve.wait_ge(block_done, j * 4 + (3 + SLOTS))
                dve.wait_ge(yl_ready, j + 1)
                dve.tensor_tensor(grouped(zs[:, :]), psum[0][:, :, 0:GT], grouped(m.RS[:, :]), ALU.mult).then_inc(evacuated, 1)
                split_lo(j, 4)
                dve.wait_ge(e_ready, j + 1)
                chain.link(dve.tensor_scalar(ex[:, :], ex[:, :], 1.0, None, ALU.add))
                chain.link(dve.reciprocal(ex[:, :], ex[:, :]))
                chain.link(dve.tensor_tensor(ex[:, :], ex[:, :], zs[:, :], ALU.mult))
                chain.link(dve.tensor_tensor(cg[:, :], cg[:, :], ex[:, :], ALU.mult))
                chain.link(dve.tensor_tensor(cg[:, :], cg[:, :], m.RS[:, :], ALU.mult))
                assert chain.n == per
                dve.wait_ge(block_done, j * 4 + (4 + SLOTS))
                dve.tensor_tensor(grouped(zs[:, :]), psum[1][:, :, 0:GT], grouped(cg[:, :]), ALU.mult).then_inc(evacuated, 1)
                dve.wait_ge(yh_ready, j + 1)
                dve.tensor_tensor(st.YL[:, ds(j * T, T)], zs[:, :], st.YH[:, ds(j * T, T)].bitcast(F32),
                                  ALU.subtract).then_inc(yl_ready, 1)
            with dve.Fori(0, KT - 1) as j:
                body(j)
            body(KT - 1)

        @block.tensor
        def _(pe):
            pe.sem_inc(block_done, SLOTS)
            pe.sem_inc(lu_turned, 1)
            with pe.Fori(0, KT) as j:
                for p in range(4):
                    pe.wait_ge(hi_ready, j * 4 + (p + 1))
                    pe.wait_ge(evacuated, j * 4 + (p + 1))
                    project_hi(pe, m, p % 2, psum[p % 2], m.XH, m.XL)
                    pe.wait_ge(lo_ready, j * 4 + (p + 1 + SLOTS))
                    project_lo(pe, m, p % 2, psum[p % 2], m.XH).then_inc(block_done, 1)
                    if p == 2:
                        pe.wait_ge(lu_ready, j + 1)
                        pe.wait_ge(lr_ready, j + 1)
                        pe.transpose(m.PS[0:18, 6, 0:P], lastu[:, :], m.IDENT[:, :]).then_inc(lu_turned, 1)


def conv_out(nc, m, d, st, following):
    with ExitStack() as ctx:
        def sb(name, shape, dt=F32):
            return ctx.enter_context(nc.sbuf_tensor(name, shape, dt))

        def sem(name):
            return new_sem(nc, m, name)
        raw = m.RAW
        x1 = [sb(f"x1_{s}", [P, T]) for s in range(2)]
        x1_out = [sem(f"o_x1_out{s}") for s in range(2)]
        sq = sb("x1_sq", [P, T])
        acc = sb("x1_sq_sum", [P, T])
        raw_in = [sem(f"o_raw_in{s}") for s in range(SLOTS)]
        hi_ready, lo_ready, block_done, evacuated = sem("o_hi_ready"), sem("o_lo_ready"), sem("o_block_done"), sem("o_evacuated")
        x1_ready, x1_split, xh_ready, sq_ready, sq_used = (sem("o_x1_ready"), sem("o_x1_split"), sem("o_xh_ready"),
                                                           sem("o_sq_ready"), sem("o_sq_used"))
        sum_ready, act_step = sem("o_sum_ready"), sem("o_act_step")
        granted, scaled = sem("o_slot_granted"), sem("o_scaled")
        block = ctx.enter_context(nc.Block())
        psum = [m.PS[:, 2 * s:2 * s + 2, :] for s in range(SLOTS)]

        @block.sync
        def _(sp):
            for s in range(SLOTS):
                sp.sem_inc(raw_in[s], 16)
            with sp.Fori(1, KT // 2) as pair:
                j = pair * 2
                for s in range(2):
                    sp.wait_ge(lo_ready, j + (s + 1))
                    sp.sem_inc(granted, 1)
                    sp.dma_start(tiles(raw[s][:, :]), w_block(d["w_out_a"][0], j * P + s * P)).then_inc(raw_in[s], 16)
            load_next(sp, m, following, lo_ready, raw_in, KT)
            for s in range(SLOTS):
                sp.wait_ge(raw_in[s], 16 * (KT // 2 + 1))

        @block.gpsimd
        def _(pool):
            pool.memset(acc[:, :], 0.0).then_inc(sq_used, 1)
            def add_square(j):
                pool.wait_ge(sq_ready, j + 2)
                pool.wait_ge(sq_used, j + 1)
                pool.tensor_tensor(acc[:, :], acc[:, :], sq[:, :], ALU.add).then_inc(sq_used, 1)

            with pool.Fori(0, KT - 2) as j:
                add_square(j)
            gain = following[2]
            pool.wait_ge(raw_in[0], 16 * (KT // 2 + 1))
            pool.tensor_tensor(tiles(raw[0][:, :]), tiles(raw[0][:, :]),
                               m.PAR[:, gain:gain + KT].unsqueeze(2).to_broadcast([P, KT, P]), ALU.mult).then_inc(scaled, 1)
            for j in range(KT - 2, KT):
                add_square(j)

        @block.scalar
        def _(act):
            def split_hi(j, s):
                if isinstance(j, int) and j + s == KT:
                    act.wait_ge(scaled, 1)
                else:
                    act.wait_ge(raw_in[s % 2], j * 8 + 16 * (s // 2 + 1))
                act.wait_ge(block_done, j + (s + 1))
                act.activation(m.WH[s % 2][:, :], raw[s % 2][:, :], ACT.Copy).then_inc(hi_ready, 1)

            def body(j):
                for s in range(2):
                    split_hi(j, s + 1)
                    act.wait_ge(x1_ready, j + (s + 1))
                    act.activation(m.XH[:, ds((j + s) * T, T)], x1[s][:, :], ACT.Copy).then_inc(xh_ready, 1)
                    act.dma_start(d["x_scratch"].rearrange("m p t -> p m t")[:, ds(j + s, 1), :].rearrange("p m t -> p (m t)"),
                                  x1[s][:, :]).then_inc(x1_out[s], 16)
                    act.wait_ge(sq_used, j + (s + 1))
                    act.activation(sq[:, :], x1[s][:, :], ACT.Square).then_inc(sq_ready, 1)
            act.sem_inc(sq_ready, 1)
            for s in range(2):
                act.sem_inc(x1_out[s], 16)
            act.sem_inc(hi_ready, 1)
            with act.Fori(0, KT // 2 - 1) as pair:
                body(pair * 2)
            body(KT - 2)
            act.wait_ge(sum_ready, 1)
            rsqrt(act, act_step, 0, m.PS[:, 6:8, 0:GT], D, m, grouped(m.RS[:, :]))
            for s in range(2):
                act.wait_ge(x1_out[s], 16 * (KT // 2 + 1))

        @block.vector
        def _(dve):
            dve.sem_inc(lo_ready, SLOTS + 1)
            dve.sem_inc(x1_split, 1)

            def split_lo(j, s):
                dve.wait_ge(hi_ready, j + (s + 1))
                dve.wait_ge(block_done, j + (s + 1))
                dve.tensor_tensor(m.WL[s % 2][:, :], raw[s % 2][:, :], m.WH[s % 2][:, :].bitcast(F32),
                                  ALU.subtract).then_inc(lo_ready, 1)

            def body(j):
                for s in range(2):
                    split_lo(j, s + 1)
                    xj = ds((j + s) * T, T)
                    dve.wait_ge(block_done, j + (s + 1 + SLOTS))
                    dve.wait_ge(x1_split, j + (s + 1))
                    dve.wait_ge(sq_ready, j + (s + 1))
                    dve.wait_ge(x1_out[s], j * 8 + 16)
                    dve.tensor_tensor(grouped(x1[s][:, :]), psum[s][:, :, 0:GT], grouped(m.XH[:, xj].bitcast(F32)),
                                      ALU.add).then_inc(evacuated, 1)
                    dve.wait_ge(evacuated, j + (s + 1))
                    dve.tensor_tensor(x1[s][:, :], x1[s][:, :], m.XL[:, xj].bitcast(F32), ALU.add).then_inc(x1_ready, 1)
                    dve.wait_ge(xh_ready, j + (s + 1))
                    dve.tensor_tensor(m.XL[:, xj], x1[s][:, :], m.XH[:, xj].bitcast(F32), ALU.subtract).then_inc(x1_split, 1)
            with dve.Fori(0, KT // 2 - 1) as pair:
                body(pair * 2)
            body(KT - 2)

        @block.tensor
        def _(pe):
            pe.sem_inc(block_done, SLOTS)
            def one(j, s, wait):
                pe.wait_ge(hi_ready, j + (s + 1))
                if wait:
                    pe.wait_ge(evacuated, j + (s - 1))
                project_hi(pe, m, s, psum[s], st.YH, st.YL)
                pe.wait_ge(lo_ready, j + (s + 1 + SLOTS))
                project_lo(pe, m, s, psum[s], st.YH).then_inc(block_done, 1)
            for s in range(2):
                one(0, s, False)
            with pe.Fori(1, KT // 2) as pair:
                for s in range(2):
                    one(pair * 2, s, True)
            pe.wait_ge(sq_used, KT + 1)
            for g in range(G):
                last = pe.matmul(m.PS[:, 6 + g, 0:GT], m.ONES[:, :], acc[:, g * GT:(g + 1) * GT], start=True, stop=True)
            last.then_inc(sum_ready, 1)


def head_weights(d, kind):
    return {"q": (d["w_in_b"][0], 0, GB), "k": (d["w_kv"], 0, GKV), "v": (d["w_kv"], D, GKV), "z": (d["w_in_b"][0], D, GB)}[kind]


def project_heads(nc, m, d, st, kind, following):
    w, col0, gain = head_weights(d, kind)
    norm, turn, silu = kind in "qk", kind in "kv", kind == "z"
    ngain = {"q": QN_, "k": KN_}.get(kind)
    scratch = {"q": d["q_scratch"], "k": d["k_scratch"], "z": d["z_scratch"]}.get(kind)
    keep = {"q": st.QS, "k": st.KS, "z": st.ZS}.get(kind)
    with ExitStack() as ctx:
        def sb(name, shape, dt=F32):
            return ctx.enter_context(nc.sbuf_tensor(f"{kind}_{name}", shape, dt))

        def sem(name):
            return new_sem(nc, m, f"{kind}_{name}")
        raw = m.RAW
        plain = [sb(f"plain{s}", [P, T]) for s in range(2)]
        sq = sb("sq", [P, T])
        r = [sb(f"r{s}", [P, T]) for s in range(2)]
        tile = [sb(f"tile{s}", [P, T]) for s in range(2)]
        swap = sb("swap", [ROT, T])
        cos, sin = sb("cos", [ROT, T]), sb("sin", [ROT, T])
        rows = [sb(f"rows{s}", [P, TT * P]) for s in range(2)]
        srows = [sb(f"srows{s}", [GS, G * P]) for s in range(2)]
        raw_in = [sem(f"raw_in{s}") for s in range(2)]
        tables_in = sem("tables_in")
        scaled, hi_ready, lo_ready = sem("scaled"), sem("hi_ready"), sem("lo_ready")
        block_done, evacuated = sem("block_done"), sem("evacuated")
        sq_ready, summed, ln_step, tile_ready = sem("sq_ready"), sem("summed"), sem("ln_step"), sem("tile_ready")
        turned, rows_ready, granted, dve_step = sem("turned"), sem("rows_ready"), sem("granted"), sem("dve_step")
        scratch_out = [sem(f"scratch_out{s}") for s in range(2)]
        rows_out = [sem(f"rows_out{s}") for s in range(2)]
        block = ctx.enter_context(nc.Block())
        psum = [m.PS[:, 2 * s:2 * s + 2, :] for s in range(2)]
        N = KT

        @block.sync
        def _(sp):
            if norm:
                sp.dma_start(cos[:, :], d["rope_cos"]).then_inc(tables_in, 16)
                sp.dma_start(sin[:, :], d["rope_sin"]).then_inc(tables_in, 16)
            for s in range(2):
                sp.sem_inc(raw_in[s], 16)
            with sp.Fori(1, N // 2) as pair:
                for s in range(2):
                    sp.wait_ge(lo_ready, pair * 2 + (s + 1))
                    sp.sem_inc(granted, 1)
                    sp.dma_start(tiles(raw[s][:, :]), w_block(w, pair * 2 * P + (s * P + col0))).then_inc(raw_in[s], 16)
            if following:
                load_next(sp, m, following, lo_ready, raw_in, N)
                for s in range(2):
                    sp.wait_ge(raw_in[s], 16 * (N // 2 + 1))

        @block.gpsimd
        def _(pool):
            def scale(pair, s, gain):
                pool.wait_ge(raw_in[s], pair * 16 + 16)
                pool.tensor_tensor(tiles(raw[s][:, :]), tiles(raw[s][:, :]),
                                   m.PAR[:, gain:gain + KT].unsqueeze(2).to_broadcast([P, KT, P]),
                                   ALU.mult).then_inc(scaled, 1)

            pool.sem_inc(scaled, 1)
            scale(0, 1, gain)
            with pool.Fori(1, N // 2) as pair:
                for s in range(2):
                    scale(pair, s, gain)
            if following:
                scale(N // 2, 0, following[2])

        @block.scalar
        def _(act):
            out_p = {"k": d["new_k_prompt"].rearrange("o (t p) h c d -> p (o t) (h c d)", p=P),
                     "v": d["new_v_prompt"].rearrange("o (t p) h e -> p (o t) (h e)", p=P)}.get(kind)
            out_s = {"k": d["new_k_sample"].rearrange("(g b) t h c d -> (b t) g (h c d)", g=G),
                     "v": d["new_v_sample"].rearrange("(g b) t h e -> (b t) g (h e)", g=G)}.get(kind)

            def split_hi(n, s):
                act.wait_ge(scaled, n + 1)
                act.wait_ge(block_done, n + 1)
                act.activation(m.WH[s][:, :], raw[s][:, :], ACT.Copy).then_inc(hi_ready, 1)

            def store_tile(n, s):
                if scratch is not None:
                    act.wait_ge(tile_ready, n + 3)
                    act.dma_start(scratch.rearrange("m p t -> p m t")[:, ds(n, 1), :].rearrange("p m (g t) -> p (m g) t", g=G),
                                  grouped(tile[s][:, :])[:, :, 0:GP]).then_inc(scratch_out[s], 16)

            def store_rows(n, s, slot_uses):
                if turn:
                    act.wait_ge(turned, n + 3)
                    act.wait_ge(rows_out[s], slot_uses * 32 + 32)
                    act.activation(rows[s][:, :], m.PS[:, 6, :], ACT.Copy).then_inc(rows_ready, 1)
                    act.activation(srows[s][:, :], m.PS[0:GS, 7, 0:G * P], ACT.Copy).then_inc(rows_ready, 1)
                    act.wait_ge(rows_ready, n * 2 + 3)
                    act.dma_start(out_p[:, :, ds(n * P, P)], rows[s][:, :].rearrange("p (t c) -> p t c", t=TT)).then_inc(rows_out[s], 16)
                    act.dma_start(out_s[:, :, ds(n * P, P)], srows[s][:, :].rearrange("p (g c) -> p g c", g=G)).then_inc(rows_out[s], 16)

            def norm_scale(n, s):
                if norm:
                    act.wait_ge(summed, n + 1)
                    act.wait_ge(tile_ready, n + 1)
                    rsqrt(act, ln_step, n * 2, m.PS[:, 4:6, 0:GT], HD, m, grouped(r[s][:, :]))

            def square(n, s):
                if norm:
                    act.wait_ge(evacuated, n + 3)
                    act.activation(sq[:, :], plain[s][:, :], ACT.Square).then_inc(sq_ready, 1)
                if silu:
                    act.wait_ge(evacuated, n + 3)
                    act.activation(r[s][:, :], plain[s][:, :], ACT.Exp, scale=-1.0).then_inc(ln_step, 2)

            def body(n, s):
                if following or not (isinstance(n, int) and n == N - 1):
                    split_hi(n + 1, 1 - s)
                if not isinstance(n, int) or n >= 2:
                    store_tile(n - 2, s)
                    half = (pair_of(n, s) - 1)
                    store_rows(n - 2, s, half)
                if not isinstance(n, int) or n >= 1:
                    norm_scale(n - 1, 1 - s)
                square(n, s)

            act.sem_inc(rows_ready, 1)
            for s in range(2):
                act.sem_inc(scratch_out[s], 16)
                act.sem_inc(rows_out[s], 32)
            act.sem_inc(hi_ready, 1)
            pairs = {}

            def pair_of(n, s):
                return n // 2 if isinstance(n, int) else pairs["at"]
            for n in range(2):
                body(n, n)
            with act.Fori(1, N // 2 - 1) as pair:
                pairs["at"] = pair
                for s in range(2):
                    body(pair * 2 + s, s)
            for n in range(N - 2, N):
                body(n, n % 2)
            norm_scale(N - 1, 1)
            for n in range(N - 2, N):
                store_tile(n, n % 2)
                store_rows(n, n % 2, n // 2)
            for s in range(2):
                act.wait_ge(scratch_out[s], 16 * (N // 2 + 1) if scratch is not None else 16)
                act.wait_ge(rows_out[s], 32 * (N // 2 + 1) if turn else 32)

        @block.vector
        def _(dve):
            per = 5

            def split_lo(n, s):
                dve.wait_ge(hi_ready, n + 1)
                dve.wait_ge(block_done, n + 1)
                dve.tensor_tensor(m.WL[s][:, :], raw[s][:, :], m.WH[s][:, :].bitcast(F32), ALU.subtract).then_inc(lo_ready, 1)

            def finish(n, s, uses):
                chain = Chain(dve, dve_step, n * (3 if silu else per))
                t, t32 = tile[s], tile[s][0:ROT, :]
                dve.wait_ge(ln_step, n * 2 + 2)
                dve.wait_ge(scratch_out[s], uses * 16 + 16)
                if turn:
                    dve.wait_ge(turned, n + 1)
                if silu:
                    chain.link(dve.tensor_scalar(r[s][:, :], r[s][:, :], 1.0, None, ALU.add))
                    chain.link(dve.reciprocal(r[s][:, :], r[s][:, :]))
                    chain.link(dve.scalar_tensor_tensor(out=t[:, :], in0=plain[s][:, :], scalar=m.GSUB[:, s:s + 1],
                                                        in1=r[s][:, :], op0=ALU.mult, op1=ALU.mult))
                    dve.tensor_copy(keep[:, ds(n * G * GS, G * GS)].rearrange("p (g t) -> p g t", g=G),
                                    grouped(t[:, :])[:, :, GP:GT]).then_inc(tile_ready, 1)
                    return
                chain.link(dve.scalar_tensor_tensor(out=t[:, :], in0=plain[s][:, :], scalar=m.PAR[:, ngain:ngain + 1],
                                                    in1=r[s][:, :], op0=ALU.mult, op1=ALU.mult))
                half = ROT // 2
                dve.sem_inc(granted, 1)
                chain.link(dve.stream_shuffle(swap[:, :], t32, [(i + half) % ROT for i in range(ROT)]))
                chain.link(dve.tensor_tensor(swap[:, :], swap[:, :], sin[:, :], ALU.mult))
                chain.link(dve.tensor_tensor(t32, t32, cos[:, :], ALU.mult))
                chain.link(dve.tensor_tensor(t32, t32, swap[:, :], ALU.add))
                dve.tensor_copy(keep[:, ds(n * G * GS, G * GS)].rearrange("p (g t) -> p g t", g=G),
                                grouped(t[:, :])[:, :, GP:GT]).then_inc(tile_ready, 1)
                assert chain.n == per

            def body(n, s, uses):
                if following or not (isinstance(n, int) and n == N - 1):
                    split_lo(n + 1, 1 - s)
                dve.wait_ge(block_done, n + 3)
                if norm or silu:
                    dve.tensor_tensor(grouped(plain[s][:, :]), psum[s][:, :, 0:GT], grouped(m.RS[:, :]), ALU.mult).then_inc(evacuated, 1)
                    if not isinstance(n, int) or n >= 1:
                        finish(n - 1, 1 - s, uses if s else uses - 1)
                else:
                    dve.wait_ge(turned, n + 1)
                    dve.tensor_tensor(grouped(tile[s][:, :]), psum[s][:, :, 0:GT], grouped(m.RS[:, :]), ALU.mult).then_inc(evacuated, 1)

            dve.sem_inc(lo_ready, 3)
            dve.sem_inc(evacuated, 2)
            dve.sem_inc(tile_ready, 2)
            if norm:
                dve.wait_ge(tables_in, 32)
            for n in range(2):
                body(n, n, 0)
            with dve.Fori(1, N // 2 - 1) as pair:
                for s in range(2):
                    body(pair * 2 + s, s, pair)
            for n in range(N - 2, N):
                body(n, n % 2, N // 2 - 1)
            if norm or silu:
                finish(N - 1, 1, N // 2 - 1)

        @block.tensor
        def _(pe):
            def turn_tile(n, s):
                if turn:
                    pe.wait_ge(tile_ready if norm else evacuated, n + 3)
                    pe.wait_ge(rows_ready, n * 2 + 1)
                    for t in range(TT):
                        pe.transpose(m.PS[:, 6, t * P:(t + 1) * P],
                                     tile[s][:, (t // 2) * GT + (t % 2) * P:(t // 2) * GT + (t % 2 + 1) * P], m.IDENT[:, :])
                    for g in range(G):
                        last = pe.transpose(m.PS[0:GS, 7, g * P:(g + 1) * P], tile[s][:, g * GT + GP:(g + 1) * GT], m.IDENT[:, :])
                    last.then_inc(turned, 1)

            def sum_squares(n):
                if norm:
                    pe.wait_ge(sq_ready, n + 1)
                    if not isinstance(n, int) or n >= 1:
                        pe.wait_ge(ln_step, n * 2)
                    for g in range(G):
                        last = pe.matmul(m.PS[:, 4 + g, 0:GT], m.ONES[:, :], sq[:, g * GT:(g + 1) * GT], start=True, stop=True)
                    last.then_inc(summed, 1)

            def body(n, s):
                pe.wait_ge(hi_ready, n + 1)
                pe.wait_ge(evacuated, n + 1)
                project_hi(pe, m, s, psum[s], m.XH, m.XL)
                if not isinstance(n, int) or n >= 2:
                    turn_tile(n - 2, s)
                if not isinstance(n, int) or n >= 1:
                    sum_squares(n - 1)
                pe.wait_ge(lo_ready, n + 3)
                project_lo(pe, m, s, psum[s], m.XH).then_inc(block_done, 1)

            pe.sem_inc(block_done, 2)
            pe.sem_inc(turned, 2)
            for n in range(2):
                body(n, n)
            with pe.Fori(1, N // 2) as pair:
                for s in range(2):
                    body(pair * 2 + s, s)
            turn_tile(N - 2, 0)
            sum_squares(N - 1)
            turn_tile(N - 1, 1)


def attention(nc, m, d, st):
    NV = NPG + 1
    keys = [("k", p) for p in range(NPG)]
    values = [("v", p) for p in range(NV)]
    items = keys + values
    NR = st.NR
    last_in = {t % NR: it for t, it in enumerate(items)}
    HQ = HC * NEW
    WQ = H * NEW
    B = 32
    NB = P // B
    NCH = D // B
    GRP = 2
    NG = NPG // GRP
    WHOLE = [1, 5, 9, 13]
    DVE_LO = [3, 7, 11, 15]
    POOL_LO = [p for p in range(NV) if p not in DVE_LO + WHOLE]
    NPARTS = 3
    PART = {p: n % NPARTS for n, p in enumerate(sorted(DVE_LO + POOL_LO))}
    with ExitStack() as ctx:
        def sb(name, shape, dt=F32):
            return ctx.enter_context(nc.sbuf_tensor(name, shape, dt))

        def sem(name):
            return new_sem(nc, m, name)
        ring = [sb(f"ring{s}", [P, D]) for s in range(NR)]
        kth = [sb(f"keys_turned{f}", [P, GRP * D // 2]) for f in range(2)]
        v_hi_of = [sb(f"value_hi{s}", [P, D], F32R) for s in range(NPARTS)]
        v_lo_of = [sb(f"value_lo{s}", [P, D], F32R) for s in range(NPARTS)]
        qblk = sb("q_blocks", [P, NCH * B])
        sct = [sb(f"scores_turned{n}", [P, 2 * GRP * NB * B]) for n in range(2)]
        pr = sb("probs", [P, NPG * HQ])
        wt = sb("weights", [P, NPG * WQ])
        wtf = sb("weights_whole", [P, len(WHOLE) * WQ])
        wst = sb("weights_hi_lo", [P, NPG * 2 * WQ], F32R)
        wstn = sb("weights_new_hi_lo", [NEW, 2 * WQ], F32R)
        qcur, kcur = sb("q_cur", [P, HQ]), sb("k_cur", [P, HQ])
        prn = sb("probs_new", [NEW, HQ])
        wtn = sb("weights_new", [NEW, WQ])
        mx, mc, mdiag, mb = sb("max_part", [P, HQ]), sb("max_col", [HQ, 1]), sb("max_diag", [HQ, HQ]), sb("max_row", [P, HQ])
        den, inv = sb("denom", [P, HQ]), sb("inv_denom", [P, HQ])
        mask_new, mask_diag = sb("mask_new", [NEW, NEW]), sb("mask_diag", [P, P])
        pages = sb("page_ids", [1, NSEQ * NPG], I32)
        qh, kh, vh = sb("q_head", [P, 2 * SEQ]), sb("k_head", [P, 2 * SEQ]), sb("v_head", [P, TT * VD])
        zh = sb("z_head", [P, 2 * SEQ])
        pp = sb("prompt_probs", [P, 2 * SEQ])
        pmx, pden, pinv = sb("prompt_max", [P, 2]), sb("prompt_denom", [P, 2]), sb("prompt_inv", [P, 2])
        pwt = sb("prompt_weights_t", [P, TT * SEQ])
        o = sb("o_head", [P, 2 * SEQ])
        ro = sb("o_rms", [P, SEQ])
        orow = sb("o_rows", [WQ, D])
        ost = sb("o_sample", [P, HC * G * GS])

        rlast = pp[:, 0:H * G * GS]

        page_in = [sem(f"page_in{s}") for s in range(NR)]
        ids_in, granted = sem("ids_in"), sem("b_granted")
        const_ready, const_step = sem("const2_ready"), sem("const2_step")
        cur_ready, qblk_ready = sem("cur_ready"), sem("qblk_ready")
        kt_ready, half_scored, sct_ready, moved = sem("kt_ready"), sem("half_scored"), sem("sct_ready"), sem("moved")
        moved_last = sem("moved_last")
        new_scored, max_ready, max_turned, diag_ready, max_spread = (sem("new_scored"), sem("max_ready"), sem("max_turned"),
                                                                     sem("diag_ready"), sem("max_spread"))
        shifted, exp_ready, den_ready, den_sum, wt_ready, whi_ready, weights_ready = (
            sem("shifted"), sem("exp_ready"), sem("den_ready"), sem("den_sum"), sem("wt_ready"), sem("whi_ready"),
            sem("weights_ready"))
        v_hi, v_lo_pool, v_lo_dve, v_used = sem("v_hi"), sem("v_lo_pool"), sem("v_lo_dve"), sem("v_used")
        olo_ready, orow_ready, o_turned, out_taken = sem("olo_ready"), sem("orow_ready"), sem("o_turned"), sem("out_taken")
        head_in = [sem(f"head_in{n}") for n in range(4)]
        prompt_scored, prompt_maxed, prompt_exp, prompt_w = (sem("prompt_scored"), sem("prompt_maxed"), sem("prompt_exp"),
                                                             sem("prompt_w"))
        prompt_turned, prompt_wt, o_done, o_taken = sem("prompt_turned"), sem("prompt_wt"), sem("o_done"), sem("o_taken")
        osq_ready, osq_sum, o_ln, y_ready, y_out = sem("osq_ready"), sem("osq_sum"), sem("o_ln"), sem("y_ready"), sem("y_out")
        normed, y_stored = sem("normed"), sem("y_stored")
        dve_soft, dve_prompt, dve_tail = sem("b_dve_soft"), sem("b_dve_prompt"), sem("b_dve_tail")
        wait_taken = sem("wait_taken")
        fin_sq, fin_sum, fin_r = sem("fin_sq"), sem("fin_sum"), sem("fin_r")
        block = ctx.enter_context(nc.Block())

        KEYS = [0, 1]
        SMALL = 1
        PWT = 0
        OUT = m.PS[:, 2:6, :]
        PSC = 6
        NEWS = 0

        def in_slot(some, t):
            return len([u for u in some if u % NR == t % NR and u <= t])

        def arrived(eng, r, t):
            first = in_slot(range(NPG), t + NR * len(items))
            eng.wait_ge(page_in[t % NR], r * (16 * len(range(t % NR, len(items), NR))) + 16 * (first + t // NR + 1))

        def key_arrived(eng, i, p):
            if isinstance(i, int) and i == 0:
                eng.wait_ge(page_in[p % NR], 16 * (p // NR + 1))
            else:
                arrived(eng, i - 1, p)

        def value_arrived(eng, r, p):
            t = NPG + p
            if isinstance(r, int) and r == NSEQ - 1:
                before = in_slot(range(NPG), t + NR * len(items)) + (NSEQ - 1) * len(range(t % NR, len(items), NR))
                eng.wait_ge(page_in[t % NR], 16 * (before + in_slot(range(NPG, len(items)), t)))
            else:
                arrived(eng, r, t)

        def split_done(eng, r, p):
            if p in WHOLE:
                eng.wait_ge(v_used, r * NV + (NV + p + 1))
            for by, sem_ in ((POOL_LO, v_lo_pool), (DVE_LO, v_lo_dve)):
                if p in by:
                    eng.wait_ge(sem_, r * len(by) + (len(by) + by.index(p) + 1))

        def page_turned(eng, i, p):
            eng.wait_ge(kt_ready, i * (2 * NPG) + (p // GRP * 2 * GRP + GRP + p % GRP + 1))

        def rows_of(p):
            return slice(0, P if p < NPG else NEW)

        def take_lo(eng, r, p, signal):
            eng.wait_ge(v_hi, r * len(PART) + (sorted(PART).index(p) + 1))
            rows = rows_of(p)
            eng.tensor_tensor(v_lo_of[PART[p]][rows, :], ring[(NPG + p) % NR][rows, :], v_hi_of[PART[p]][rows, :].bitcast(F32),
                              ALU.subtract).then_inc(signal, 1)

        def chunks(tile):
            return tile[:, :].rearrange("p (g c j) -> p g c j", g=GRP, c=NCH // 2)

        def move_scores(i, quad, blocks, put):
            for b in blocks:
                for a in range(4):
                    src = sct[quad % 2][a * B:(a + 1) * B, :].rearrange("p (g n s r) -> p n g s r", g=2, n=4, s=GRP)
                    dst = pr[b * B:(b + 1) * B, quad * 4 * HQ:(quad + 1) * 4 * HQ].rearrange(
                        "p (g s n a q) -> p n g s a q", g=2, s=GRP, n=4, a=4)
                    for g in range(2):
                        ins = put(dst[:, :, g, :, a, :], src[:, :, g, :, b * NEW:(b + 1) * NEW])
            return ins

        @block.sync
        def _(sp):
            new_v = d["new_v_sample"].rearrange("b t h e -> b t (h e)")
            n_phys = d["cache_k"].shape[0]
            cache_k = d["cache_k"].rearrange("n p h c d -> n p (h c d)")
            cache_v = d["cache_v"].rearrange("n p h e -> n p (h e)")

            def load(what, seq, p, s):
                if p < NPG:
                    page = sp.value_load(pages[0:1, ds(seq * NPG + p, 1)], min_val=0, max_val=n_phys - 1)
                    src = (cache_k if what == "k" else cache_v)[ds(page, 1), :, :].rearrange("o p n -> (o p) n")
                    dst = ring[s][:, :]
                else:
                    src = new_v[ds(seq, 1), :, :].rearrange("o t n -> (o t) n")
                    dst = ring[s][0:NEW, :]
                sp.sem_inc(granted, 1)
                sp.dma_start(dst, src).then_inc(page_in[s], 16)

            sp.dma_start(pages[:, :], d["page_table"].rearrange("(o b) p -> o (b p)", o=1)).then_inc(ids_in, 16)
            sp.wait_ge(ids_in, 16)
            for _, p in keys:
                if p >= NR:
                    page_turned(sp, 0, p - NR)
                load("k", 0, p, p % NR)
            with sp.Fori(0, NSEQ - 1) as r:
                for t, (what, p) in enumerate(items):
                    s = t % NR
                    if t == 0:
                        page_turned(sp, r, NPG - 1)
                    if t < NR:
                        split_done(sp, r - 1, last_in[s][1])
                    elif items[t - NR][0] == "k":
                        page_turned(sp, r + 1, items[t - NR][1])
                    else:
                        split_done(sp, r, items[t - NR][1])
                    load(what, r + 1 if what == "k" else r, p, s)
            for t, (_, p) in enumerate(items):
                if t >= NPG:
                    if t - NR >= NPG:
                        split_done(sp, NSEQ - 1, p - NR)
                    else:
                        split_done(sp, NSEQ - 2, last_in[t % NR][1])
                    load("v", NSEQ - 1, p, t % NR)

        @block.gpsimd
        def _(pool):
            def take_cur(i):
                for dst, src in ((qcur, st.QS), (kcur, st.KS)):
                    pool.tensor_copy(dst[:, :].rearrange("p (m t) -> p m t", t=NEW),
                                     src[:, :].rearrange("p (m t) -> p m t", t=G * GS)[:, :, ds(i * NEW, NEW)]).then_inc(cur_ready, 1)

            def lo_parts(r):
                for p in POOL_LO:
                    take_lo(pool, r, p, v_lo_pool)

            def gate(r):
                pool.wait_ge(head_in[2], r * 16 + 16)
                pool.wait_ge(o_ln, r * 2 + 4)
                o3 = o[:, :].rearrange("p (e t) -> p e t", e=2)
                pool.tensor_tensor(o3, o3, ro[:, :].unsqueeze(1).to_broadcast([P, 2, SEQ]), ALU.mult).then_inc(normed, 1)
                pool.wait_ge(normed, r + 1)
                pool.tensor_tensor(o[:, :], o[:, :], zh[:, :], ALU.mult).then_inc(y_ready, 1)
                pool.wait_ge(y_ready, r + 2)
                pool.sem_inc(wait_taken, 1)
                pool.dma_start(d["y_scratch"].rearrange("m p t -> p m t")[:, ds(r * 2, 2), :], o3).then_inc(y_out, 16)
                pool.wait_ge(y_out, r * 16 + 16)
                pool.sem_inc(y_stored, 1)

            pool.sem_inc(v_lo_pool, len(POOL_LO))
            pool.sem_inc(y_ready, 1)
            pool.sem_inc(y_stored, 1)
            pool.memset(mask_new[:, :], 0.0).then_inc(const_step, 1)
            pool.memset(mask_diag[:, :], 0.0).then_inc(const_step, 1)
            pool.memset(qblk[:, :], 0.0).then_inc(const_step, 1)
            take_cur(0)
            pool.wait_ge(const_step, 3)
            pool.affine_select(out=mask_new[:, :], in_=mask_new[:, :], compare_op=ALU.is_ge, fill=BIG, base=0,
                               pattern=[[1, NEW]], channel_multiplier=-1).then_inc(const_ready, 1)
            pool.affine_select(out=mask_diag[:, :], in_=mask_diag[:, :], compare_op=ALU.is_ge, fill=BIG, base=0,
                               pattern=[[-1, P]], channel_multiplier=1).then_inc(const_ready, 1)
            pool.wait_ge(new_scored, 1)
            take_cur(1)
            with pool.Fori(0, NSEQ - 2) as r:
                lo_parts(r)
                pool.wait_ge(new_scored, r + 2)
                take_cur(r + 2)
                gate(r)
            for r in range(NSEQ - 2, NSEQ):
                lo_parts(r)
                gate(r)

        @block.scalar
        def _(act):
            def load_head(r, n):
                if n < 3:
                    dst, src = ((qh, d["q_scratch"]), (kh, d["k_scratch"]), (zh, d["z_scratch"]))[n]
                    act.dma_start(dst[:, :].rearrange("p (c t) -> p c t", c=2),
                                  src.rearrange("m p t -> p m t")[:, ds(r * 2, 2), :]).then_inc(head_in[n], 16)
                else:
                    act.dma_start(vh[:, :].rearrange("p (t e) -> p t e", t=TT),
                                  d["new_v_prompt"].rearrange("o (t p) h e -> p (o t) (h e)", p=P)[:, :, ds(r * VD, VD)]
                                  ).then_inc(head_in[3], 16)

            def start_run(r):
                act.wait_ge(o_done, r + 1)
                for n in (0, 1, 3):
                    load_head(r, n)
                weights_hi(r)

            def load_gate(r):
                act.wait_ge(y_ready, r + 1)
                load_head(r, 2)

            def weights_hi(r):
                act.wait_ge(wt_ready, r + 1)
                act.activation(wstn[:, 0:WQ], wtn[:, :], ACT.Copy)
                act.activation(wst[:, :].rearrange("p (g w) -> p g w", g=NPG)[:, :, 0:WQ],
                               wt[:, :].rearrange("p (g w) -> p g w", g=NPG), ACT.Copy).then_inc(whi_ready, 1)

            def move(i, quad, blocks=range(NB)):
                act.wait_ge(sct_ready, i * NG + (2 * quad + 2))
                move_scores(i, quad, blocks, lambda out, in_: act.activation(out, in_, ACT.Copy)).then_inc(moved, 1)

            def softmax_exp(i):
                act.wait_ge(shifted, i * 2 + 2)
                act.activation(pr[:, :], pr[:, :], ACT.Exp, scale=SCALE).then_inc(exp_ready, 1)
                act.activation(prn[:, :], prn[:, :], ACT.Exp, scale=SCALE).then_inc(exp_ready, 1)

            def value_hi(r, p):
                value_arrived(act, r, p)
                same = [q for q in PART if PART[q] == PART[p]]
                earlier = [q for q in same if q < p]
                if earlier:
                    act.wait_ge(v_used, r * NV + (NV + earlier[-1] + 1))
                else:
                    act.wait_ge(v_used, r * NV + (same[-1] + 1))
                rows = rows_of(p)
                act.activation(v_hi_of[PART[p]][rows, :], ring[(NPG + p) % NR][rows, :], ACT.Copy).then_inc(v_hi, 1)

            def prompt_exps(r, qb):
                n = (qb + 1) * P
                act.wait_ge(prompt_maxed, r * TT + (qb + 1))
                for c in range(2):
                    act.activation(pp[:, c * SEQ:c * SEQ + n], m.PS[:, PSC + c, 0:n], ACT.Exp, scale=SCALE,
                                   bias=pmx[:, c:c + 1], accum_out=pden[:, c:c + 1]).then_inc(prompt_exp, 1)

            def prompt_weights(r, qb):
                act.wait_ge(prompt_turned, r * TT + (qb + 1))
                act.activation(pwt[:, :].rearrange("p (b t) -> p b t", b=TT)[:, 0:qb + 1, qb * P:(qb + 1) * P],
                               m.PS[:, PWT, 0:(qb + 1) * P].rearrange("p (b t) -> p b t", t=P), ACT.Copy).then_inc(prompt_wt, 1)

            def with_values(r, nxt):
                def hi(*these):
                    for p in these:
                        value_hi(r, p)
                hi(0, 2, 3)
                if nxt:
                    move(r + 1, 3, (0, 1))
                prompt_exps(r, 0)
                hi(4, 6, 7)
                prompt_weights(r, 0)
                prompt_exps(r, 1)
                hi(8, 10)
                prompt_weights(r, 1)
                prompt_exps(r, 2)
                hi(11, 12)
                if nxt:
                    softmax_exp(r + 1)
                prompt_weights(r, 2)
                prompt_exps(r, 3)
                hi(14, 15)
                prompt_weights(r, 3)
                hi(16)
                act.wait_ge(o_taken, r + 1)
                act.activation(pp[:, :], o[:, :], ACT.Square).then_inc(osq_ready, 1)
                act.wait_ge(v_used, r * NV + 2 * NV)
                act.activation(orow[:, :].rearrange("p (c n) -> p c n", c=4), m.PS[WQ:2 * WQ, 2:6, :], ACT.Copy).then_inc(olo_ready, 1)
                act.wait_ge(osq_sum, r + 1)
                rsqrt(act, o_ln, r * 2 + 2, m.PS[:, PSC, :], VD, m, ro[:, :])

            act.sem_inc(o_ln, 2)
            for quad in range(3):
                move(0, quad)
            move(0, 3, (0, 1))
            softmax_exp(0)
            with act.Fori(0, NSEQ - 1) as r:
                start_run(r)
                for quad in range(3):
                    move(r + 1, quad)
                    if quad == 0:
                        load_gate(r)
                with_values(r, True)
            start_run(NSEQ - 1)
            load_gate(NSEQ - 1)
            with_values(NSEQ - 1, False)
            act.wait_ge(out_taken, NSEQ + 1)
            act.activation(pr[:, 0:HC * G * GS], ost[:, :], ACT.Square).then_inc(fin_sq, 1)
            act.wait_ge(fin_sum, 1)
            rsqrt(act, fin_r, 0, m.PS[:, 2, 0:H * G * GS], VD, m, rlast)

        @block.vector
        def _(dve):
            def turn_scores(i, g):
                dve.wait_ge(half_scored, i * (2 * NG) + (2 * g + 4))
                if g >= 4 and g % 2 == 0:
                    dve.wait_ge(moved, i * 4 + (g // 2 - 1))
                w = 4 * GRP * B
                dve.transpose(sct[(g // 2) % 2][:, (g % 2) * w:(g % 2 + 1) * w], m.PS[:, KEYS[g % 2], 0:w]).then_inc(sct_ready, 1)

            def weights_lo(r):
                dve.tensor_copy(wtf[:, :].rearrange("p (g w) -> p g w", w=WQ),
                                wt[:, :].rearrange("p (g w) -> p g w", w=WQ)[:, WHOLE[0]:NPG:4, :])
                dve.wait_ge(whi_ready, r + 1)
                ws = wst[:, :].rearrange("p (g w) -> p g w", g=NPG)
                dve.tensor_tensor(wstn[:, WQ:2 * WQ], wtn[:, :], wstn[:, 0:WQ].bitcast(F32), ALU.subtract)
                dve.tensor_tensor(ws[:, :, WQ:2 * WQ], wt[:, :].rearrange("p (g w) -> p g w", g=NPG),
                                  ws[:, :, 0:WQ].bitcast(F32), ALU.subtract).then_inc(weights_ready, 1)

            def lay_queries(i):
                dve.wait_ge(cur_ready, i * 2 + 2)
                for b in range(NB):
                    for c in range(4):
                        ins = dve.tensor_copy(
                            qblk[b * B:(b + 1) * B, :].rearrange("p (m c b q) -> p m c b q", m=HC, c=4, b=8)[:, :, c, b, :],
                            qcur[c * B:(c + 1) * B, :].rearrange("p (m q) -> p m q", m=HC))
                ins.then_inc(qblk_ready, 1)

            def turn_keys(i, g):
                n = D // 2
                for half in range(2):
                    for p in range(g * GRP, (g + 1) * GRP):
                        key_arrived(dve, i, p)
                        dve.wait_ge(half_scored, i * (2 * NG) + (2 * g + half + 1))
                        dve.transpose(kth[half][:, (p % GRP) * n:(p % GRP + 1) * n],
                                      ring[p % NR][:, half * n:(half + 1) * n]).then_inc(kt_ready, 1)

            def with_keys(i):
                for g in range(1, NG):
                    turn_keys(i, g)
                    turn_scores(i, g - 1)
                    if g == 1 and not (isinstance(i, int) and i == 0):
                        weights_lo(i - 1)
                turn_scores(i, NG - 1)

            pr3 = pr[:, :].rearrange("p (g c) -> p g c", c=HQ)

            def soft_new(i, chain):
                dve.wait_ge(new_scored, i + 1)
                dve.tensor_tensor(prn[:, :].rearrange("p (m q) -> p m q", q=NEW),
                                  m.PS[0:NEW, NEWS, 0:HQ].rearrange("p (m q) -> p m q", q=NEW),
                                  mask_new[:, :].unsqueeze(1).to_broadcast([NEW, HC, NEW]), ALU.add).then_inc(max_ready, 1)

            def soft_max(i, chain):
                dve.wait_ge(sct_ready, i * NG + NG)
                move_scores(i, 3, (2, 3), dve.tensor_copy).then_inc(moved_last, 1)
                dve.wait_ge(moved_last, i + 1)
                dve.wait_ge(moved, i * 4 + 4)
                dve.tensor_reduce(mx[:, :], pr3.rearrange("p g c -> p c g"), AX.X, ALU.max).then_inc(max_ready, 1)

            def soft_diag(i, chain):
                dve.wait_ge(max_turned, i + 1)
                chain.link(dve.tensor_reduce(mc[:, :], m.PS[0:HQ, SMALL, P:2 * P + NEW], AX.X, ALU.max))
                dve.tensor_scalar(mdiag[:, :], m.IDENT[0:HQ, 0:HQ], mc[:, 0:1], None, ALU.mult).then_inc(diag_ready, 1)

            def soft_shift(i, chain):
                dve.wait_ge(max_spread, i + 1)
                chain.link(dve.tensor_copy(mb[:, :], m.PS[:, SMALL, 320:320 + HQ]))
                dve.tensor_tensor(pr3, pr3, mb[:, :].unsqueeze(1).to_broadcast([P, NPG, HQ]), ALU.subtract).then_inc(shifted, 1)
                dve.tensor_tensor(prn[:, :], prn[:, :], mb[0:NEW, :], ALU.subtract).then_inc(shifted, 1)

            def soft_den(i, chain):
                dve.wait_ge(exp_ready, i * 2 + 2)
                dve.tensor_reduce(den[:, :], pr3.rearrange("p g c -> p c g"), AX.X, ALU.add).then_inc(den_ready, 1)

            def soft_weights(i, chain):
                dve.wait_ge(den_sum, i + 1)
                chain.link(dve.reciprocal(inv[:, :], m.PS[:, SMALL, 384:384 + HQ]))
                inv4 = inv[:, :].rearrange("p (h c q) -> p h c q", h=H, c=2)
                chain.link(dve.tensor_scalar(inv4[:, :, 1, :], inv4[:, :, 1, :], m.NLAM[:, 0:1], None, ALU.mult))
                pr4 = pr[:, :].rearrange("p (g h c q) -> p g h c q", g=NPG, h=H, c=2)
                prn4 = prn[:, :].rearrange("p (h c q) -> p h c q", h=H, c=2)
                w4 = wt[:, :].rearrange("p (g h q) -> p g h q", g=NPG, h=H)
                wn4 = wtn[:, :].rearrange("p (h q) -> p h q", h=H)
                dve.tensor_tensor(w4, pr4[:, :, :, 0, :], inv4[:, :, 0, :].unsqueeze(1).to_broadcast([P, NPG, H, NEW]), ALU.mult)
                dve.tensor_tensor(wn4, prn4[:, :, 0, :], inv4[0:NEW, :, 0, :], ALU.mult)
                dve.tensor_tensor(prn4[:, :, 1, :], prn4[:, :, 1, :], inv4[0:NEW, :, 1, :], ALU.mult)
                chain.link(dve.tensor_tensor(pr4[:, :, :, 1, :], pr4[:, :, :, 1, :],
                                             inv4[:, :, 1, :].unsqueeze(1).to_broadcast([P, NPG, H, NEW]), ALU.mult))
                dve.tensor_tensor(wn4, wn4, prn4[:, :, 1, :], ALU.add)
                dve.tensor_tensor(w4, w4, pr4[:, :, :, 1, :], ALU.add).then_inc(wt_ready, 1)

            SOFT = [soft_new, soft_max, soft_diag, soft_shift, soft_den, soft_weights]
            SOFT_LINKS = 5

            def prompt_max(r, qb, chain):
                n = (qb + 1) * P
                dve.wait_ge(prompt_scored, r * TT + (qb + 1))
                for c in range(2):
                    dg = m.PS[:, PSC + c, qb * P:n]
                    ins = dve.tensor_tensor(dg, dg, mask_diag[:, :], ALU.add)
                chain.link(ins)
                chain.link(dve.tensor_reduce(pmx[:, :], m.PS[:, PSC:PSC + 2, 0:n], AX.X, ALU.max))
                dve.tensor_scalar(pmx[:, :], pmx[:, :], -SCALE, None, ALU.mult).then_inc(prompt_maxed, 1)

            def prompt_mix(r, qb, chain):
                n = (qb + 1) * P
                dve.wait_ge(prompt_exp, r * (2 * TT) + (2 * qb + 2))
                chain.link(dve.reciprocal(pinv[:, :], pden[:, :]))
                chain.link(dve.tensor_scalar(pp[:, SEQ:SEQ + n], pp[:, SEQ:SEQ + n], pinv[:, 1:2], m.NLAM[:, 0:1],
                                             ALU.mult, ALU.mult))
                dve.scalar_tensor_tensor(out=pp[:, 0:n], in0=pp[:, 0:n], scalar=pinv[:, 0:1], in1=pp[:, SEQ:SEQ + n],
                                         op0=ALU.mult, op1=ALU.add).then_inc(prompt_w, 1)

            PROMPT_LINKS = 4 * TT

            def with_values(r, nxt, after):
                soft, prompt = Chain(dve, dve_soft, r * SOFT_LINKS + SOFT_LINKS), Chain(dve, dve_prompt, r * PROMPT_LINKS)

                def step(n):
                    if nxt:
                        SOFT[n](r + 1, soft)
                step(0)
                prompt_max(r, 0, prompt)
                step(1)
                take_lo(dve, r, 3, v_lo_dve)
                prompt_mix(r, 0, prompt)
                step(2)
                prompt_max(r, 1, prompt)
                take_lo(dve, r, 7, v_lo_dve)
                prompt_mix(r, 1, prompt)
                step(3)
                prompt_max(r, 2, prompt)
                take_lo(dve, r, 11, v_lo_dve)
                prompt_mix(r, 2, prompt)
                prompt_max(r, 3, prompt)
                step(4)
                prompt_mix(r, 3, prompt)
                step(5)
                take_lo(dve, r, 15, v_lo_dve)
                assert not nxt or soft.n == SOFT_LINKS
                dve.wait_ge(o_done, r + 2)
                dve.wait_ge(y_stored, r + 1)
                dve.tensor_copy(o[:, :].rearrange("p (e t) -> p e t", e=2), m.PS[:, PSC:PSC + 2, :]).then_inc(o_taken, 1)
                assert prompt.n == PROMPT_LINKS
                if after:
                    turn_keys(r + 2, 0)
                dve.wait_ge(olo_ready, r + 1)
                dve.tensor_tensor(orow[:, :].rearrange("p (c n) -> p c n", c=4), m.PS[0:WQ, 2:6, :],
                                  orow[:, :].rearrange("p (c n) -> p c n", c=4), ALU.add).then_inc(orow_ready, 1)
                if after:
                    lay_queries(r + 2)
                dve.wait_ge(o_turned, r + 1)
                for h in range(H):
                    ins = dve.tensor_copy(
                        ost[:, :].rearrange("p (m t) -> p m t", t=G * GS)[:, 2 * h:2 * h + 2, ds(r * NEW, NEW)],
                        m.PS[:, 2, :].rearrange("p (m w) -> p m w", w=WQ)[:, 2 * h:2 * h + 2, h * NEW:(h + 1) * NEW])
                ins.then_inc(out_taken, 1)

            dve.sem_inc(v_lo_dve, len(DVE_LO))
            dve.sem_inc(out_taken, 1)
            dve.wait_ge(const_step, 3)
            dve.wait_ge(const_ready, 2)
            lay_queries(0)
            turn_keys(0, 0)
            with_keys(0)
            first_soft = Chain(dve, dve_soft)
            for n in range(len(SOFT)):
                SOFT[n](0, first_soft)
            turn_keys(1, 0)
            lay_queries(1)
            with dve.Fori(0, NSEQ - 2) as r:
                with_keys(r + 1)
                with_values(r, True, True)
            with_keys(NSEQ - 1)
            with_values(NSEQ - 2, True, False)
            weights_lo(NSEQ - 1)
            with_values(NSEQ - 1, False, False)
            tail = Chain(dve, dve_tail)
            dve.wait_ge(fin_r, 2)
            o4 = ost[:, :].rearrange("p (h e t) -> p h e t", h=H, e=2)
            z4 = st.ZS[:, :].rearrange("p (h e t) -> p h e t", h=H, e=2)
            y4 = st.YS[:, :].rearrange("p (h e t) -> p h e t", h=H, e=2)
            r3 = rlast.rearrange("p (h t) -> p h t", h=H)
            for e in range(2):
                tail.link(dve.tensor_tensor(y4[:, :, e, :], o4[:, :, e, :], r3, ALU.mult))
                tail.link(dve.tensor_tensor(y4[:, :, e, :], y4[:, :, e, :], z4[:, :, e, :], ALU.mult))

        @block.tensor
        def _(pe):
            def with_keys(i):
                pe.wait_ge(qblk_ready, i + 1)
                for g in range(NG):
                    if g >= 2:
                        pe.wait_ge(sct_ready, i * NG + (g - 1))
                    for half in range(2):
                        pe.wait_ge(kt_ready, i * (2 * NPG) + 2 * GRP * g + GRP * (half + 1))
                        for a in range(4):
                            for n in (2 * half, 2 * half + 1):
                                hc = 4 * n + a
                                for c in range(4):
                                    last = pe.matmul(m.PS[a * B:(a + 1) * B, KEYS[g % 2], n * GRP * B:(n + 1) * GRP * B],
                                                     qblk[:, (hc * 4 + c) * B:(hc * 4 + c + 1) * B],
                                                     chunks(kth[half])[:, :, (hc * 4 + c) % (NCH // 2), :],
                                                     start=(c == 0), stop=(c == 3), skip_group_check=True)
                        last.then_inc(half_scored, 1)
                pe.wait_ge(sct_ready, i * NG + (NG - 1))
                for hc in range(HC):
                    last = pe.matmul(m.PS[0:NEW, NEWS, hc * NEW:(hc + 1) * NEW], kcur[:, hc * NEW:(hc + 1) * NEW],
                                     qcur[:, hc * NEW:(hc + 1) * NEW], start=True, stop=True)
                last.then_inc(new_scored, 1)

            def turn_max(i):
                pe.wait_ge(max_ready, i * 2 + 2)
                pe.sem_inc(wait_taken, 1)
                pe.transpose(m.PS[0:HQ, SMALL, P:2 * P], mx[:, :], m.IDENT[:, :])
                pe.transpose(m.PS[0:HQ, SMALL, 2 * P:2 * P + NEW], prn[:, :], m.IDENT[0:NEW, 0:NEW]).then_inc(max_turned, 1)

            def spread_max(i):
                pe.wait_ge(diag_ready, i + 1)
                pe.matmul(m.PS[:, SMALL, 320:320 + HQ], m.ONES[0:HQ, :], mdiag[:, :], start=True, stop=True).then_inc(max_spread, 1)

            def sum_probs(i):
                pe.wait_ge(den_ready, i + 1)
                pe.matmul(m.PS[:, SMALL, 384:384 + HQ], m.ONES[:, :], den[:, :], start=True, stop=False)
                pe.matmul(m.PS[:, SMALL, 384:384 + HQ], m.ONES[0:NEW, :], prn[:, :], start=False, stop=True).then_inc(den_sum, 1)

            def prompt_scores(r, qb):
                if qb == 0:
                    pe.wait_ge(o_ln, r * 2 + 1)
                    for n in (0, 1, 3):
                        pe.wait_ge(head_in[n], r * 16 + 16)
                else:
                    pe.wait_ge(prompt_exp, r * (2 * TT) + 2 * qb)
                for c in range(2):
                    last = pe.matmul(m.PS[:, PSC + c, 0:(qb + 1) * P], qh[:, c * SEQ + qb * P:c * SEQ + (qb + 1) * P],
                                     kh[:, c * SEQ:c * SEQ + (qb + 1) * P], start=True, stop=True)
                last.then_inc(prompt_scored, 1)

            def prompt_turn(r, qb, nxt):
                pe.wait_ge(prompt_w, r * TT + (qb + 1))
                if qb == 0 and nxt:
                    pe.wait_ge(max_ready, r * 2 + 3)
                if qb:
                    pe.wait_ge(prompt_wt, r * TT + qb)
                for kb in range(qb + 1):
                    last = pe.transpose(m.PS[:, PWT, kb * P:(kb + 1) * P], pp[:, kb * P:(kb + 1) * P], m.IDENT[:, :])
                last.then_inc(prompt_turned, 1)

            def prompt_out(r):
                pe.wait_ge(prompt_wt, r * TT + TT)
                for e in range(2):
                    for kb in range(TT):
                        last = pe.matmul(m.PS[:, PSC + e, kb * P:SEQ], vh[:, kb * VD + e * P:kb * VD + (e + 1) * P],
                                         pwt[:, kb * SEQ + kb * P:(kb + 1) * SEQ], start=(kb == 0), stop=(kb == TT - 1),
                                         skip_group_check=True)
                last.then_inc(o_done, 1)

            def prompt_squares(r):
                pe.wait_ge(osq_ready, r + 1)
                for e in range(2):
                    last = pe.matmul(m.PS[:, PSC, :], m.ONES[:, :], pp[:, e * SEQ:(e + 1) * SEQ],
                                     start=(e == 0), stop=(e == 1))
                last.then_inc(osq_sum, 1)

            def with_values(r, nxt):
                prompt_scores(r, 0)
                pe.wait_ge(weights_ready, r + 1)
                pe.wait_ge(out_taken, r + 1)
                for p in range(NV):
                    if p in WHOLE:
                        value_arrived(pe, r, p)
                        w = wtf[:, WHOLE.index(p) * WQ:(WHOLE.index(p) + 1) * WQ]
                        for c in range(4):
                            last = pe.matmul(OUT[0:WQ, c, :], w, ring[(NPG + p) % NR][:, c * 512:(c + 1) * 512],
                                             start=False, stop=False, skip_group_check=True)
                    else:
                        split_done(pe, r, p)
                        w = wst[:, p * 2 * WQ:(p + 1) * 2 * WQ] if p < NPG else wstn[:, :]
                        for c in range(4):
                            for part in (v_hi_of, v_lo_of):
                                last = pe.matmul(OUT[0:2 * WQ, c, :], w, part[PART[p]][rows_of(p), c * 512:(c + 1) * 512],
                                                 start=(p == 0 and part is v_hi_of), stop=(p == NPG and part is v_lo_of),
                                                 skip_group_check=True)
                    last.then_inc(v_used, 1)
                    if p == 2 and nxt:
                        turn_max(r + 1)
                    if p in (2, 5, 8):
                        prompt_scores(r, (2, 5, 8).index(p) + 1)
                    if p in (3, 6, 9, 12):
                        prompt_turn(r, (3, 6, 9, 12).index(p), nxt)
                    if p == 4 and nxt:
                        spread_max(r + 1)
                    if p == 10 and nxt:
                        sum_probs(r + 1)
                    if p == 13:
                        prompt_out(r)
                    if p == 16:
                        prompt_squares(r)
                pe.wait_ge(orow_ready, r + 1)
                pe.sem_inc(wait_taken, 1)
                for t in range(HC):
                    last = pe.transpose(m.PS[:, 2, t * WQ:(t + 1) * WQ], orow[:, t * P:(t + 1) * P], m.IDENT[0:WQ, 0:WQ])
                last.then_inc(o_turned, 1)

            pe.sem_inc(half_scored, 2)
            pe.sem_inc(o_done, 1)
            pe.sem_inc(v_used, NV)
            with_keys(0)
            turn_max(0)
            spread_max(0)
            sum_probs(0)
            with pe.Fori(0, NSEQ - 1) as r:
                with_keys(r + 1)
                with_values(r, True)
            with_values(NSEQ - 1, False)
            pe.wait_ge(fin_sq, 1)
            for e in range(2):
                last = pe.matmul(m.PS[:, 2, 0:H * G * GS], m.ONES[:, :],
                                 pr[:, 0:HC * G * GS].rearrange("p (h e t) -> p h e t", h=H, e=2)[:, :, e, :],
                                 start=(e == 0), stop=(e == 1))
            last.then_inc(fin_sum, 1)


def project_out(nc, m, d, st):
    with ExitStack() as ctx:
        def sb(name, shape, dt=F32):
            return ctx.enter_context(nc.sbuf_tensor(name, shape, dt))

        def sem(name):
            return new_sem(nc, m, name)
        yh, yl = sb("ay_hi", [P, KT * T], F32R), sb("ay_lo", [P, KT * T], F32R)
        raw = [sb(f"f_raw{s}", [P, D]) for s in range(2)]
        xr = [sb(f"x_in{s}", [P, T]) for s in range(2)]
        x_in = [sem(f"f_x_in{s}") for s in range(2)]
        YQ = 4
        ys = sb("y_in", [P, KT * SEQ])
        x2 = [sb(f"x2_{s}", [P, T]) for s in range(2)]
        rows = sb("x2_rows", [P, TT * P])
        srows = sb("x2_srows", [GS, G * P])
        raw_in = [sem(f"f_raw_in{s}") for s in range(2)]
        y_in = [sem(f"y_in_done{q}") for q in range(KT // YQ)]
        yh_ready, yl_ready, ys_ready = sem("f_yh_ready"), sem("f_yl_ready"), sem("f_ys_ready")
        hi_ready, lo_ready, block_done = sem("f_hi_ready"), sem("f_lo_ready"), sem("f_block_done")
        x2_ready, turned, rows_ready, rows_out, granted = (sem("f_x2_ready"), sem("f_turned"), sem("f_rows_ready"),
                                                           sem("f_rows_out"), sem("f_granted"))
        block = ctx.enter_context(nc.Block())
        psum = [m.PS[:, 2 * s:2 * s + 2, :] for s in range(2)]
        out_p = d["y_prompt"].rearrange("o (t p) c -> p (o t) c", p=P)
        out_s = d["y_sample"].rearrange("(g b) t c -> (b t) g c", g=G)

        @block.sync
        def _(sp):
            def load_weights(s):
                sp.dma_start(tiles(raw[s][:, :]), w_block(d["w_out_b"][0], s * P)).then_inc(raw_in[s], 16)

            load_weights(0)
            for q in range(KT // YQ):
                sp.dma_start(ys[:, q * YQ * SEQ:(q + 1) * YQ * SEQ].rearrange("p (k t) -> p k t", k=YQ),
                             d["y_scratch"][q * YQ:(q + 1) * YQ].rearrange("k p t -> p k t")).then_inc(y_in[q], 16)
            load_weights(1)
            for s in range(2):
                sp.dma_start(xr[s][:, :], d["x_scratch"][s]).then_inc(x_in[s], 16)
            with sp.Fori(1, KT // 2) as pair:
                for s in range(2):
                    sp.wait_ge(lo_ready, pair * 2 + (s + 1))
                    sp.sem_inc(granted, 1)
                    sp.dma_start(tiles(raw[s][:, :]), w_block(d["w_out_b"][0], pair * 2 * P + s * P)).then_inc(raw_in[s], 16)
                    sp.wait_ge(x2_ready, pair * 2 + (s - 1))
                    sp.sem_inc(granted, 1)
                    sp.dma_start(xr[s][:, :], d["x_scratch"].rearrange("m p t -> p m t")[:, ds(pair * 2 + s, 1), :]
                                 .rearrange("p m t -> p (m t)")).then_inc(x_in[s], 16)

        @block.scalar
        def _(act):
            def split_hi(n, s, use):
                act.wait_ge(raw_in[s], use * 16 + 16)
                act.wait_ge(block_done, n + 1)
                act.activation(m.WH[s][:, :], raw[s][:, :], ACT.Copy).then_inc(hi_ready, 1)

            def store(n):
                act.wait_ge(turned, n + 3)
                act.wait_ge(rows_out, n * 32 + 32)
                act.activation(rows[:, :], m.PS[:, 6, :], ACT.Copy).then_inc(rows_ready, 1)
                act.activation(srows[:, :], m.PS[0:GS, 7, 0:G * P], ACT.Copy).then_inc(rows_ready, 1)
                act.wait_ge(rows_ready, n * 2 + 3)
                act.dma_start(out_p[:, :, ds(n * P, P)], rows[:, :].rearrange("p (t c) -> p t c", t=TT)).then_inc(rows_out, 16)
                act.dma_start(out_s[:, :, ds(n * P, P)], srows[:, :].rearrange("p (g c) -> p g c", g=G)).then_inc(rows_out, 16)

            act.sem_inc(rows_ready, 1)
            act.sem_inc(rows_out, 32)
            split_hi(0, 0, 0)
            for g in range(G):
                act.activation(yh[:, :].rearrange("p (k g t) -> p k g t", k=KT, g=G)[:, :, g, GP:GT],
                               st.YS[:, :].rearrange("p (k g t) -> p k g t", k=KT, g=G)[:, :, g, :], ACT.Copy).then_inc(ys_ready, 1)
            for k in range(KT):
                act.wait_ge(y_in[k // YQ], 16)
                act.activation(grouped(yh[:, k * T:(k + 1) * T])[:, :, 0:GP], ys[:, k * SEQ:(k + 1) * SEQ].rearrange("p (g t) -> p g t", g=G),
                               ACT.Copy).then_inc(yh_ready, 1)
            split_hi(1, 1, 0)
            with act.Fori(1, KT // 2) as pair:
                for s in range(2):
                    split_hi(pair * 2 + s, s, pair)
                    store(pair * 2 + (s - 2))
            store(KT - 2)
            store(KT - 1)
            act.wait_ge(rows_out, 32 * KT + 32)

        @block.vector
        def _(dve):
            def split_lo(n, s):
                dve.wait_ge(hi_ready, n + 1)
                dve.wait_ge(block_done, n + 1)
                dve.tensor_tensor(m.WL[s][:, :], raw[s][:, :], m.WH[s][:, :].bitcast(F32), ALU.subtract).then_inc(lo_ready, 1)

            def body(n, s, use):
                if not (isinstance(n, int) and n == KT - 1):
                    split_lo(n + 1, 1 - s)
                dve.wait_ge(block_done, n + 3)
                dve.wait_ge(turned, n + 1)
                dve.wait_ge(x_in[s], use * 16 + 16)
                dve.tensor_tensor(grouped(x2[s][:, :]), psum[s][:, :, 0:GT], grouped(xr[s][:, :]), ALU.add).then_inc(x2_ready, 1)

            dve.sem_inc(lo_ready, 2)
            split_lo(0, 0)
            dve.wait_ge(ys_ready, G)
            for g in range(G):
                v = [a.rearrange("p (k g t) -> p k g t", k=KT, g=G)[:, :, g, GP:GT] for a in (yl[:, :], yh[:, :])]
                dve.tensor_tensor(v[0], st.YS[:, :].rearrange("p (k g t) -> p k g t", k=KT, g=G)[:, :, g, :],
                                  v[1].bitcast(F32), ALU.subtract).then_inc(ys_ready, 1)
            for k in range(KT):
                dve.wait_ge(yh_ready, k + 1)
                yk = slice(k * T, (k + 1) * T)
                dve.tensor_tensor(grouped(yl[:, yk])[:, :, 0:GP], ys[:, k * SEQ:(k + 1) * SEQ].rearrange("p (g t) -> p g t", g=G),
                                  grouped(yh[:, yk].bitcast(F32))[:, :, 0:GP], ALU.subtract).then_inc(yl_ready, 1)
            for n in range(2):
                body(n, n, 0)
            with dve.Fori(1, KT // 2 - 1) as pair:
                for s in range(2):
                    body(pair * 2 + s, s, pair)
            for n in range(KT - 2, KT):
                body(n, n % 2, n // 2)

        @block.tensor
        def _(pe):
            def turn_tile(n, s):
                pe.wait_ge(x2_ready, n + 1)
                pe.wait_ge(rows_ready, n * 2 + 1)
                for t in range(TT):
                    pe.transpose(m.PS[:, 6, t * P:(t + 1) * P],
                                 x2[s][:, (t // 2) * GT + (t % 2) * P:(t // 2) * GT + (t % 2 + 1) * P], m.IDENT[:, :])
                for g in range(G):
                    last = pe.transpose(m.PS[0:GS, 7, g * P:(g + 1) * P], x2[s][:, g * GT + GP:(g + 1) * GT], m.IDENT[:, :])
                last.then_inc(turned, 1)

            def body(n, s, first=False):
                pe.wait_ge(hi_ready, n + 1)
                if not first:
                    pe.wait_ge(x2_ready, n - 1)
                elif n == 0:
                    pe.wait_ge(ys_ready, 2 * G)
                project_hi(pe, m, s, psum[s], yh, yl, yl_ready if first and n == 0 else None)
                if not first:
                    turn_tile(n - 2, s)
                pe.wait_ge(lo_ready, n + 3)
                project_lo(pe, m, s, psum[s], yh).then_inc(block_done, 1)

            pe.sem_inc(block_done, 2)
            pe.sem_inc(turned, 2)
            for n in range(2):
                body(n, n, first=True)
            with pe.Fori(1, KT // 2) as pair:
                for s in range(2):
                    body(pair * 2 + s, s)
            turn_tile(KT - 2, 0)
            turn_tile(KT - 1, 1)


def build(nc, d):
    with ExitStack() as ctx:
        m = memory(nc, ctx)
        first = ctx.enter_context(ExitStack())
        m.keep, m.sems = first, []
        st = Bag()
        st.QS, st.KS, st.ZS = (ctx.enter_context(nc.sbuf_tensor(f"{name}_sample", [P, HC * G * GS], F32)) for name in "qkz")
        with ExitStack() as x:
            m.XH = x.enter_context(nc.sbuf_tensor("x_hi", [P, KT * T], F32R))
            m.XL = x.enter_context(nc.sbuf_tensor("x_lo", [P, KT * T], F32R))
            weight_memory(nc, m, x, "w")
            raw_memory(nc, m, x)
            with ExitStack() as a:
                st.RS2 = a.enter_context(nc.sbuf_tensor("rs_squared", [P, T], F32))
                st.STATE = a.enter_context(nc.sbuf_tensor("state", [P, KT * GS], F32))
                read_inputs(nc, m, d, st, (d["w_in_a"][0], CONV_IN_COLS[0:2]))
                st.YH = a.enter_context(nc.sbuf_tensor("y_hi", [P, KT * T], F32R))
                st.YL = a.enter_context(nc.sbuf_tensor("y_lo", [P, KT * T], F32R))
                conv_in(nc, m, d, st, (d["w_out_a"][0], 0))
                conv_out(nc, m, d, st, head_weights(d, "q"))
            for kind, then in (("q", "k"), ("k", "v"), ("v", "z"), ("z", None)):
                project_heads(nc, m, d, st, kind, head_weights(d, then) if then else None)
        numbers = [s.num for s in m.sems]
        nc.all_engine_barrier(sems_to_clear=range(min(numbers), max(numbers) + 1))
        first.close()
        m.keep = ctx
        st.YS = ctx.enter_context(nc.sbuf_tensor("y_sample", [P, HC * G * GS], F32))
        st.NR = 7
        attention(nc, m, d, st)
        with ExitStack() as w:
            weight_memory(nc, m, w, "wf")
            project_out(nc, m, d, st)


_INS = ['x_prompt', 'x_sample', 'state_conv', 'cache_k', 'cache_v', 'page_table', 'norm_a', 'w_in_a', 'conv_w',
        'w_out_a', 'norm_kv', 'w_kv', 'k_norm', 'norm_b', 'w_in_b', 'q_norm', 'lam', 'subln_w', 'w_out_b']
_OUTS = [('y_prompt', (1, SEQ, D)), ('y_sample', (NSEQ, NEW, D)), ('new_k_prompt', (1, SEQ, H, 2, HD)),
         ('new_v_prompt', (1, SEQ, H, VD)), ('new_conv_prompt', (1, 1, CONV - 1, D)),
         ('new_k_sample', (NSEQ, NEW, H, 2, HD)), ('new_v_sample', (NSEQ, NEW, H, VD)),
         ('new_conv_sample', (1, NSEQ, CONV - 1, D))]


def _rope_tables():
    import numpy as np
    inv = np.float32(THETA) ** (-np.arange(0, ROT, 2, dtype=np.float32) / np.float32(ROT))
    sample = PAST + np.tile(np.arange(NEW), NSEQ // G)
    pos = np.concatenate([np.concatenate([np.arange(g * GP, (g + 1) * GP), sample]) for g in range(G)])
    ang = pos.astype(np.float32)[None, :] * inv[:, None].astype(np.float32)
    c, s = np.cos(ang), np.sin(ang)
    return np.concatenate([c, c]).astype(np.float32), np.concatenate([-s, s]).astype(np.float32)


def kernel(**inputs):
    import numpy as _np
    import concourse.bacc as _bacc
    from concourse import mybir as _mybir
    from concourse.bass_utils import run_bass_kernel_spmd as _run

    nc = _bacc.Bacc("TRN2", target_bir_lowering=False, num_devices=1)
    arrays, d = {}, {}

    def give(name, a):
        arrays[f"in_{name}_dram"] = a
        d[name] = nc.dram_tensor(f"in_{name}_dram", a.shape, _mybir.dt.from_np(a.dtype), kind="ExternalInput").ap()
    for name in _INS:
        give(name, _np.ascontiguousarray(inputs[name]))
    cos, sin = _rope_tables()
    give("rope_cos", cos)
    give("rope_sin", sin)
    for name, shape in _OUTS:
        d[name] = nc.dram_tensor(f"out_{name}_dram", shape, _mybir.dt.float32, kind="ExternalOutput").ap()
    for name in ("q_scratch", "k_scratch", "z_scratch", "y_scratch", "x_scratch"):
        width = T if name == "x_scratch" else SEQ
        d[name] = nc.dram_tensor(name, (HC, P, width), _mybir.dt.float32, kind="Internal").ap()
    build(nc, d)
    r = _run(nc, [arrays], core_ids=[0])
    return tuple(r.results[0][f"out_{name}_dram"] for name, _ in _OUTS)
```
